# Optimizing a Trainium2 kernel written in Bass

```python
import math
import jax
import jax.numpy as jnp
from jax import lax
import numpy as np

D_MODEL = 1024
BATCH = 1
SEQ = 256
DEPTH = 1

PLE_DIM = 256
EPS = 1e-6
GDN_HEADS = 8
GDN_DK = 128
GDN_DV = 128
GDN_CONV = 4
GDN_CHUNK = 64
GDN_QK = GDN_HEADS * GDN_DK
GDN_V = GDN_HEADS * GDN_DV
FOX_HEADS = 16
FOX_HD = 64
FOX_W = FOX_HEADS * FOX_HD
FOX_QBLOCK = 128
N_EXPERTS = 64
TOP_K = 8
D_EXPERT = 256
D_SHARED = 256
ROUTED_SCALE = 2.5
MOE_TOKEN_BLOCK = 128
IN_SPLITS = (2 * GDN_QK + GDN_V, GDN_V, GDN_HEADS, GDN_HEADS, 3 * FOX_W, FOX_HEADS, 2 * D_MODEL)
D_IN = 2 * GDN_QK + 2 * GDN_V + 2 * GDN_HEADS + 3 * FOX_W + FOX_HEADS + 2 * D_MODEL

kernel_name = 'hybrid_gdn_fox_moe_block'

def rms_norm(x, gain):
    xf = x.astype(jnp.float32)
    y = xf * lax.rsqrt(jnp.mean(xf * xf, axis=-1, keepdims=True) + EPS)
    return (y * gain.astype(jnp.float32)).astype(x.dtype)

def l2_norm(x):
    xf = x.astype(jnp.float32)
    return xf * lax.rsqrt(jnp.sum(xf * xf, axis=-1, keepdims=True) + EPS)

def split_cols(t, sizes):
    out, off = [], 0
    for n in sizes:
        out.append(t[..., off:off + n])
        off += n
    return out

def causal_depthwise_conv(x, w):
    c = x.shape[-1]
    return lax.conv_general_dilated(
        x, w[:, None, :].astype(x.dtype), window_strides=(1,), padding=[(GDN_CONV - 1, 0)],
        dimension_numbers=('NWC', 'WIO', 'NWC'), feature_group_count=c)

def gated_delta_rule(q, k, v, log_alpha, beta):
    f32 = jnp.float32
    B, S, H, DK = q.shape
    DV = v.shape[-1]
    C = GDN_CHUNK
    N = S // C

    def chunks(t):
        t = t.astype(f32).reshape((B, N, C, H) + t.shape[3:])
        return jnp.moveaxis(t, 3, 1)

    q = chunks(q) * (DK ** -0.5)
    k = chunks(k)
    v = chunks(v)
    beta = chunks(beta)
    g = jnp.cumsum(chunks(log_alpha), axis=-1)
    causal = jnp.tril(jnp.ones((C, C), bool))
    strict = jnp.tril(jnp.ones((C, C), bool), -1)
    decay = jnp.exp(jnp.where(causal, g[..., :, None] - g[..., None, :], -jnp.inf))
    kk = jnp.einsum('bhnid,bhnjd->bhnij', k, k)
    lower = jnp.where(strict, beta[..., :, None] * kk * decay, 0.0)
    a_mat = lower + jnp.eye(C, dtype=f32)
    rhs = jnp.concatenate([v * beta[..., None], k * (beta * jnp.exp(g))[..., None]], axis=-1)
    sol = lax.linalg.triangular_solve(a_mat, rhs, left_side=True, lower=True, unit_diagonal=True)
    u, w = sol[..., :DV], sol[..., DV:]
    qk = jnp.where(causal, jnp.einsum('bhnid,bhnjd->bhnij', q, k) * decay, 0.0)
    g_last = g[..., -1]
    k_tail = k * jnp.exp(g_last[..., None] - g)[..., None]
    q_g = q * jnp.exp(g)[..., None]
    xs = tuple(jnp.moveaxis(t, 2, 0) for t in (q_g, qk, u, w, k_tail, g_last))

    def step(state, inp):
        q_c, qk_c, u_c, w_c, kt_c, gl_c = inp
        v_new = u_c - jnp.einsum('bhck,bhkv->bhcv', w_c, state)
        o_c = jnp.einsum('bhck,bhkv->bhcv', q_c, state) + jnp.einsum('bhij,bhjv->bhiv', qk_c, v_new)
        state = state * jnp.exp(gl_c)[..., None, None] + jnp.einsum('bhck,bhcv->bhkv', kt_c, v_new)
        return state, o_c

    s0 = jnp.zeros((B, H, DK, DV), f32)
    _, o = lax.scan(step, s0, xs)
    o = jnp.moveaxis(o, 0, 2)
    return jnp.moveaxis(o, 1, 3).reshape(B, S, H, DV)

def forgetting_attention(q, k, v, log_f):
    f32 = jnp.float32
    B, S, H, D = q.shape
    c = jnp.moveaxis(jnp.cumsum(log_f.astype(f32), axis=1), 1, 2)
    scale = D ** -0.5
    outs = []
    for blk in range(S // FOX_QBLOCK):
        q0, q1 = blk * FOX_QBLOCK, (blk + 1) * FOX_QBLOCK
        s = jnp.einsum('bqhd,bkhd->bhqk', q[:, q0:q1], k[:, :q1], preferred_element_type=f32) * scale
        s = s + c[:, :, q0:q1, None] - c[:, :, None, :q1]
        mask = (q0 + jnp.arange(FOX_QBLOCK))[:, None] >= jnp.arange(q1)[None, :]
        probs = jax.nn.softmax(jnp.where(mask, s, -jnp.inf), axis=-1)
        outs.append(jnp.einsum('bhqk,bkhd->bqhd', probs.astype(v.dtype), v[:, :q1]))
    return jnp.concatenate(outs, axis=1)

def routed_moe(hn, w_router, router_bias, we_gate, we_up, we_down, ws_gate, ws_up, ws_down):
    f32 = jnp.float32
    B, S, D = hn.shape
    t = hn.reshape(B * S, D)
    scores = jax.nn.sigmoid(jnp.dot(t, w_router, preferred_element_type=f32))
    _, idx = lax.top_k(scores + router_bias.astype(f32), TOP_K)
    sel = jnp.take_along_axis(scores, idx, axis=-1)
    wts = sel / jnp.sum(sel, axis=-1, keepdims=True) * ROUTED_SCALE
    gates = jnp.einsum('tk,tke->te', wts, jax.nn.one_hot(idx, N_EXPERTS, dtype=f32))
    nb = t.shape[0] // MOE_TOKEN_BLOCK

    def block(args):
        tb, gb = args
        a = jnp.einsum('td,edf->tef', tb, we_gate)
        b = jnp.einsum('td,edf->tef', tb, we_up)
        hid = jax.nn.silu(a) * b * gb[..., None].astype(tb.dtype)
        return jnp.einsum('tef,efd->td', hid, we_down)

    routed = lax.map(block, (t.reshape(nb, MOE_TOKEN_BLOCK, D), gates.reshape(nb, MOE_TOKEN_BLOCK, N_EXPERTS)))
    routed = routed.reshape(B, S, D)
    shared = jnp.einsum('bsf,fd->bsd', jax.nn.silu(jnp.einsum('bsd,df->bsf', hn, ws_gate)) * jnp.einsum('bsd,df->bsf', hn, ws_up), ws_down)
    return routed + shared

def setup_inputs(seed: int = 0) -> dict:
    key = jax.random.key(seed)
    ks = jax.random.split(key, 32)
    f32 = jnp.float32
    L = DEPTH

    def nrm(k, shape, fan_in):
        return jax.random.normal(k, shape, f32) * (fan_in ** -0.5)

    def gain(k, shape):
        return 1.0 + 0.05 * jax.random.normal(k, shape, f32)

    dt = jnp.exp(jax.random.uniform(ks[5], (L, GDN_HEADS), f32, math.log(1e-3), math.log(0.1)))
    return {
        'x': jax.random.normal(ks[0], (BATCH, SEQ, D_MODEL), f32),
        'p': jax.random.normal(ks[1], (DEPTH, BATCH, SEQ, PLE_DIM), f32),
        'norm_mix': gain(ks[2], (L, D_MODEL)),
        'w_in': nrm(ks[3], (L, D_MODEL, D_IN), D_MODEL),
        'conv_w': nrm(ks[4], (L, GDN_CONV, 2 * GDN_QK + GDN_V), GDN_CONV),
        'a_log': jnp.log(jax.random.uniform(ks[6], (L, GDN_HEADS), f32, 1.0, 16.0)),
        'dt_bias': dt + jnp.log(-jnp.expm1(-dt)),
        'gdn_norm': gain(ks[7], (L, GDN_DV)),
        'fox_f_bias': 3.0 + 0.5 * jax.random.normal(ks[8], (L, FOX_HEADS), f32),
        'q_norm': gain(ks[9], (L, FOX_HD)),
        'k_norm': gain(ks[10], (L, FOX_HD)),
        'w_branch_gdn': nrm(ks[11], (L, GDN_V, D_MODEL), GDN_V),
        'w_branch_fox': nrm(ks[12], (L, FOX_W, D_MODEL), FOX_W),
        'w_out': nrm(ks[13], (L, D_MODEL, D_MODEL), D_MODEL),
        'norm_ffn': gain(ks[14], (L, D_MODEL)),
        'w_router': nrm(ks[15], (L, D_MODEL, N_EXPERTS), D_MODEL),
        'router_bias': 0.01 * jax.random.normal(ks[16], (L, N_EXPERTS), f32),
        'we_gate': nrm(ks[17], (L, N_EXPERTS, D_MODEL, D_EXPERT), D_MODEL),
        'we_up': nrm(ks[18], (L, N_EXPERTS, D_MODEL, D_EXPERT), D_MODEL),
        'we_down': nrm(ks[19], (L, N_EXPERTS, D_EXPERT, D_MODEL), D_EXPERT),
        'ws_gate': nrm(ks[20], (L, D_MODEL, D_SHARED), D_MODEL),
        'ws_up': nrm(ks[21], (L, D_MODEL, D_SHARED), D_MODEL),
        'ws_down': nrm(ks[22], (L, D_SHARED, D_MODEL), D_SHARED),
        'w_ple': nrm(ks[23], (L, PLE_DIM, D_MODEL), PLE_DIM),
        'ple_norm': gain(ks[24], (L, D_MODEL)),
        'ple_gate_norm': gain(ks[25], (L, D_MODEL)),
        'w_ple_gate': nrm(ks[26], (L, D_MODEL, D_MODEL), D_MODEL),
    }

def reference(x, p, norm_mix, w_in, conv_w, a_log, dt_bias, gdn_norm, fox_f_bias, q_norm, k_norm,
              w_branch_gdn, w_branch_fox, w_out, norm_ffn, w_router, router_bias,
              we_gate, we_up, we_down, ws_gate, ws_up, ws_down,
              w_ple, ple_norm, ple_gate_norm, w_ple_gate):
    f32 = jnp.float32
    B, S, _ = x.shape
    h = x
    for i in range(DEPTH):
        xn = rms_norm(h, norm_mix[i])
        proj = jnp.einsum('bsd,de->bse', xn, w_in[i])
        gdn_qkv, gdn_z, gdn_a, gdn_b, fox_qkv, fox_f, merge = split_cols(proj, IN_SPLITS)

        qkv = jax.nn.silu(causal_depthwise_conv(gdn_qkv, conv_w[i]))
        q_a = l2_norm(qkv[..., :GDN_QK].reshape(B, S, GDN_HEADS, GDN_DK))
        k_a = l2_norm(qkv[..., GDN_QK:2 * GDN_QK].reshape(B, S, GDN_HEADS, GDN_DK))
        v_a = qkv[..., 2 * GDN_QK:].reshape(B, S, GDN_HEADS, GDN_DV)
        log_alpha = -jnp.exp(a_log[i].astype(f32)) * jax.nn.softplus(gdn_a.astype(f32) + dt_bias[i].astype(f32))
        beta = jax.nn.sigmoid(gdn_b.astype(f32))
        o_a = gated_delta_rule(q_a, k_a, v_a, log_alpha, beta)
        o_a = rms_norm(o_a, gdn_norm[i]) * jax.nn.silu(gdn_z.reshape(B, S, GDN_HEADS, GDN_DV).astype(f32))
        y_a = jnp.einsum('bse,ed->bsd', o_a.reshape(B, S, GDN_V).astype(h.dtype), w_branch_gdn[i])

        q_f = rms_norm(fox_qkv[..., :FOX_W].reshape(B, S, FOX_HEADS, FOX_HD), q_norm[i])
        k_f = rms_norm(fox_qkv[..., FOX_W:2 * FOX_W].reshape(B, S, FOX_HEADS, FOX_HD), k_norm[i])
        v_f = fox_qkv[..., 2 * FOX_W:].reshape(B, S, FOX_HEADS, FOX_HD)
        log_f = jax.nn.log_sigmoid(fox_f.astype(f32) + fox_f_bias[i].astype(f32))
        o_f = forgetting_attention(q_f, k_f, v_f, log_f)
        y_f = jnp.einsum('bse,ed->bsd', o_f.reshape(B, S, FOX_W).astype(h.dtype), w_branch_fox[i])

        gate_a = jax.nn.sigmoid(merge[..., :D_MODEL])
        gate_f = jax.nn.sigmoid(merge[..., D_MODEL:])
        h = h + jnp.einsum('bsd,de->bse', gate_a * y_a + gate_f * y_f, w_out[i])

        h = h + routed_moe(rms_norm(h, norm_ffn[i]), w_router[i], router_bias[i], we_gate[i], we_up[i],
                           we_down[i], ws_gate[i], ws_up[i], ws_down[i])

        e = rms_norm(jnp.einsum('bsp,pd->bsd', p[i], w_ple[i]), ple_norm[i])
        g = jax.nn.sigmoid(jnp.einsum('bsd,de->bse', rms_norm(h, ple_gate_norm[i]), w_ple_gate[i]))
        h = h + g * e
    return h


_drawn_inputs = setup_inputs


def setup_inputs(seed=0):
    import zlib

    import numpy as np

    out = dict(_drawn_inputs(seed))
    spreads = {}
    factors = {'ple_norm': 3.012, 'ple_gate_norm': 7.603}
    for name, (base, spread) in spreads.items():
        noise = np.random.default_rng([zlib.crc32(name.encode()), seed]).standard_normal(out[name].shape)
        drawn = base * np.exp(spread * noise) if base else spread * noise
        out[name] = jnp.asarray(drawn.astype(out[name].dtype))
    for name, factor in factors.items():
        out[name] = (out[name] * factor).astype(out[name].dtype)
    return out
```

```python
from contextlib import ExitStack

import concourse.bass as bass
from concourse import mybir

P = 128
F32 = mybir.dt.float32
BF16 = mybir.dt.bfloat16
ALU = mybir.AluOpType
ACT = mybir.ActivationFunctionType
AX = mybir.AxisListType

S, D = 256, 1024
NT = S // P
KC = D // P
GH, DK = 8, 128
FH, FD = 16, 64
NE, TOPK, DE = 64, 8, 256
ROUTED_SCALE = 2.5
EPS = 1e-6
LEVELS = 7
MASKED = -1e30

C_QKV, C_Z, C_AB, C_FOX, C_F, C_MERGE = 0, 3072, 4096, 4112, 7184, 7200
WT = 512
A_SLOTS = 3
E_WORDS = 3 * KC * DE
E_SLOTS = 4

R_CONV, R_NMIX, R_NFFN, R_NPG, R_GDN, R_QN, R_KN, R_ALL = 0, 96, 104, 112, 120, 121, 122, 123


def bc(ap, axis, n):
    v = ap.unsqueeze(axis)
    shape = list(v.shape)
    shape[axis] = n
    return v.to_broadcast(shape)


def bank_fills():
    f = ["cols"]
    f += [f"xT.{n}.{j}" for n in range(NT) for j in range(2)]
    f += [f"qkv.{c}" for c in range(12)]
    f += ["small"]
    f += [f"z.{j}.{n}" for j in range(2) for n in range(NT)]
    f += ["cum", "gbT"]
    f += [f"tq.{n}.{j}" for j in range(6) for n in range(NT)]
    f += [f"fox.{j}.{n}" for j in range(6) for n in range(NT)]
    f += [f"tk.{n}.{j}" for n in range(NT) for j in range(4)]
    f += [f"gb.{j}" for j in range(4)] + [f"bb.{j}" for j in range(4)]
    for j in range(4):
        f += [f"kk.{j}", f"qk.{j}"]
    for lv in range(LEVELS):
        f += [f"P.{lv}.{j}" for j in range(4)]
        if lv > 0:
            for j in range(4):
                f += ([f"X.{lv}.{j}"] if lv < LEVELS - 1 else []) + [f"V.{lv}.{j}"]
    for j in range(2):
        f += [f"tg.{j}", f"wT.{j}", f"u0.{j}"]
    for j in range(2):
        f += [f"o0.{j}", f"s1.{j}"]
    for j in range(2):
        f += [f"u1.{j}"]
    for j in range(2):
        f += [f"o1.{j}"]
    f += [f"merge.{j}.{n}" for j in range(4) for n in range(NT)]
    f += [f"oT.{n}.{j}" for n in range(NT) for j in range(2)]
    f += [f"fT.{n}.{j}" for n in range(NT) for j in range(4)]
    f += ["cT"] + [f"cb.{j}" for j in range(8)]
    f += [f"ya.{j}.{n}" for j in range(2) for n in range(NT)]
    for g in range(9):
        if g < 8:
            f += [f"s.{2 * g}", f"s.{2 * g + 1}"]
        if g > 0:
            f += [f"pT.{2 * g - 2}", f"pT.{2 * g - 1}", f"pv.{g - 1}"]
    f += [f"yf.{j}.{n}" for j in range(2) for n in range(NT)]
    f += [f"mT.{n}.{j}" for n in range(NT) for j in range(2)]
    f += [f"wo.{j}.{n}" for j in range(2) for n in range(NT)]
    f += [f"hT.{n}.{j}" for n in range(NT) for j in range(2)]
    f += ["router"]
    f += [f"pT2.{n}" for n in range(NT)]
    f += [f"e.{n}.{j}" for n in range(NT) for j in range(2)]
    return f


def program(nc, x, p, norm_mix, w_in, conv_w, a_log, dt_bias, gdn_norm, fox_f_bias, q_norm, k_norm,
            w_branch_gdn, w_branch_fox, w_out, norm_ffn, w_router, router_bias, we_gate, we_up, we_down,
            ws_gate, ws_up, ws_down, w_ple, ple_norm, ple_gate_norm, w_ple_gate, out):
    ctx = ExitStack()
    with ctx:
        def sb(name, shape, dt=F32):
            return ctx.enter_context(nc.sbuf_tensor(name, shape, dt))

        def sem(name):
            return ctx.enter_context(nc.semaphore(name))

        bank = [ctx.enter_context(nc.psum_tensor(f"bank{i}", [P, 512], F32)) for i in range(8)]

        h = sb("h", [P, NT, D])
        actT = sb("actT", [P, KC, S])
        ident = sb("ident", [P, P])
        ones = sb("ones", [P, P])
        tri = sb("tri", [P, P])
        stri = sb("stri", [P, P])
        negm = sb("negm", [P, P])
        lmask = sb("lmask", [P, LEVELS, P], BF16)
        nhalf = sb("nhalf", [P, 32])
        cols = sb("cols", [P, P])
        bias3 = sb("bias3", [P, 32])
        nega = sb("nega", [P, GH])
        rbias = sb("rbias", [P, NE])
        gates = sb("gates", [P, NT, NE])
        wsm = sb("wsm", [P, KC, 32])
        wrt = sb("wrt", [P, KC, NE])

        stat_used = [0]
        stat = sb("stat", [P, 1000])

        def stats(n):
            lo = stat_used[0]
            stat_used[0] += n
            assert stat_used[0] <= 1000
            return stat[:, lo:lo + n]

        A_WORDS = 45056
        arena = sb("arena", [P, A_WORDS])

        def at(lo, n):
            assert lo + n <= A_WORDS
            return arena[:, lo:lo + n]

        wring = [at(i * KC * WT, KC * WT).rearrange("p (c n) -> p c n", c=KC) for i in range(A_SLOTS)]
        R1 = A_SLOTS * KC * WT
        R2, RZ, RF = R1 + 6144, R1 + 12288, R1 + 14336
        TDT = RF + 6144
        TLT, TMT, TX, TV, TPB = (TDT + 2048 * i for i in range(1, 6))

        def prob(lo, n=16):
            return at(lo, n * P).rearrange("p (b t) -> p b t", b=n)

        qkvT = prob(R1, 48).rearrange("p (c n) t -> p c (n t)", n=NT)
        qk = at(R2, 4096).rearrange("p (n c) -> p n c", n=NT)
        vbeta = prob(R2 + 4096)
        zs = at(RZ, 2048).rearrange("p (n c) -> p n c", n=NT)
        fox = at(RF, 6144).rearrange("p (n c) -> p n c", n=NT)
        dT, lT, mT, xi, vi, pb = (prob(t) for t in (TDT, TLT, TMT, TX, TV, TPB))
        rows = at(TMT, P)
        xn = at(TPB, 2048).rearrange("p (n c) -> p n c", n=NT)
        sq = at(TMT, 2048)
        gd, bd = prob(TX), prob(TV)
        blocks = prob(TV, 8)
        kbe = prob(TLT, 8)
        s1 = prob(TLT + 1024, 8)
        qgT, wTn = prob(TX, 8), prob(TX + 1024, 8)
        u0, u1 = prob(TPB, 8), prob(TPB + 1024, 8)
        oa = at(TMT, 2048).rearrange("p (n c) -> p n c", n=NT)
        oT = at(R2 + 4096, 2048).rearrange("p (c t) -> p c t", c=KC)
        merge = at(R2, 4096).rearrange("p (n c) -> p n c", n=NT)
        foxT = at(R1, 4096).rearrange("p (c t) -> p c t", c=16)
        scores = [at(R1 + 4096 + 384 * i, 384) for i in range(2)]
        probsT = [at(R1 + 4096 + 768 + 384 * i, 384) for i in range(2)]
        cbm = at(TDT, 6144).rearrange("p (f k) -> p f k", f=FH)
        cd = at(TX, 4096).rearrange("p (f k) -> p f k", f=FH)
        ofT = at(RZ, 2048).rearrange("p (c t) -> p c t", c=KC)
        mix = at(TX, 2048).rearrange("p (n c) -> p n c", n=NT)
        mixf = at(TV, 2048).rearrange("p (n c) -> p n c", n=NT)
        mixT = at(TPB, 2048).rearrange("p (c t) -> p c t", c=KC)

        ering = [at(i * E_WORDS, E_WORDS) for i in range(E_SLOTS)]
        eg = [v[:, 0:2048].rearrange("p (c f) -> p c f", c=KC) for v in ering]
        eu = [v[:, 2048:4096].rearrange("p (c f) -> p c f", c=KC) for v in ering]
        ed = [v[:, 4096:6144].rearrange("p (c d) -> p c d", c=2) for v in ering]
        B0 = E_SLOTS * E_WORDS
        hn = at(B0, 2048).rearrange("p (n c) -> p n c", n=NT)
        e_t = at(B0 + 2048, 2048).rearrange("p (n c) -> p n c", n=NT)
        p_t = at(B0 + 4096, 512).rearrange("p (n c) -> p n c", n=NT)
        pT = at(B0 + 4608, 512).rearrange("p (c t) -> p c t", c=2)
        wple = at(B0 + 5120, 2048).rearrange("p (c d) -> p c d", c=2)
        plen = at(B0 + 7168, 1024)
        hid = [at(B0 + 8192 + 256 * i, 256) for i in range(2)]
        sil = [at(B0 + 8704 + 256 * i, 256) for i in range(2)]
        hidT = [at(B0 + 9216 + 256 * i, 256).rearrange("p (c t) -> p c t", c=2) for i in range(2)]
        wpg = [at(i * KC * WT, KC * WT).rearrange("p (c n) -> p c n", c=KC) for i in range(2)]
        gt = at(B0 + 9728, 2048).rearrange("p (n c) -> p n c", n=NT)

        x_loaded, rows_loaded, bias_loaded, small_loaded = (sem(s) for s in ("x_loaded", "rows_loaded", "bias_loaded", "small_loaded"))
        w_loaded = [sem(f"w_loaded{i}") for i in range(A_SLOTS)]
        consts = sem("consts")
        masks_made = sem("masks_made")
        filled = [sem(f"filled{i}") for i in range(8)]
        drained = [sem(f"drained{i}") for i in range(8)]
        dve_step, act_step, pool_step = sem("dve_step"), sem("act_step"), sem("pool_step")
        sumsq = sem("sumsq")
        rinv_made = sem("rinv_made")
        xn_ready = sem("xn_ready")
        conv_done = sem("conv_done")
        soft = sem("soft")
        beta_ready = sem("beta_ready")
        logs_ready = sem("logs_ready")
        gstat = sem("gstat")
        geg = sem("geg")
        gd_made, bd_made, cd_made = sem("gd_made"), sem("bd_made"), sem("cd_made")
        qkss, qkrinv, qk_normed = sem("qkss"), sem("qkrinv"), sem("qk_normed")
        d_ready, dexp_ready = sem("d_ready"), sem("dexp_ready")
        d_masked = sem("d_masked")
        m_ready = sem("m_ready")
        scaled = sem("scaled")
        oss, orinv, o_normed = sem("oss"), sem("orinv"), sem("o_normed")
        fss, frinv, f_normed = sem("fss"), sem("frinv"), sem("f_normed")
        smax, sexp, sdiv = sem("smax"), sem("sexp"), sem("sdiv")
        mixed = sem("mixed")
        h_ready = sem("h_ready")
        sig_ready = sem("sig_ready")
        gates_ready = sem("gates_ready")
        p_loaded = sem("p_loaded")
        ess, erinv, e_ready = sem("ess"), sem("erinv"), sem("e_ready")
        e_loaded = [sem(f"e_loaded{i}") for i in range(E_SLOTS)]
        gu_filled, gu_silu, hid_ready = sem("gu_filled"), sem("gu_silu"), sem("hid_ready")
        hidT_filled, hidT_ready, down_done = sem("hidT_filled"), sem("hidT_ready"), sem("down_done")
        wpg_loaded = sem("wpg_loaded")
        sg_ready, out_ready, out_stored = sem("sg_ready"), sem("out_ready"), sem("out_stored")
        pg_filled = sem("pg_filled")

        fills = bank_fills()
        place = {name: (i % 8, i // 8) for i, name in enumerate(fills)}

        def ps(name):
            return bank[place[name][0]]

        def wait_filled(eng, name):
            b, turn = place[name]
            eng.wait_ge(filled[b], turn + 1)

        def wait_drained(eng, name):
            b, turn = place[name]
            eng.wait_ge(drained[b], turn + 1)

        w_in2, = (w_in[0],)
        wtiles = [(w_in2, C_QKV + WT * t, f"qkv.{2 * t + 1}") for t in range(6)]
        wtiles += [(w_in2, C_Z + WT * j, f"z.{j}.1") for j in range(2)]
        wtiles += [(w_in2, C_FOX + WT * j, f"fox.{j}.1") for j in range(6)]
        wtiles += [(w_in2, C_MERGE + WT * j, f"merge.{j}.1") for j in range(4)]
        wtiles += [(w_branch_gdn[0], WT * j, f"ya.{j}.1") for j in range(2)]
        wtiles += [(w_branch_fox[0], WT * j, f"yf.{j}.1") for j in range(2)]
        wtiles += [(w_out[0], WT * j, f"wo.{j}.1") for j in range(2)]
        W_QKV, W_Z, W_FOX, W_MERGE, W_YA, W_YF, W_WO = 0, 6, 8, 14, 18, 20, 22

        block = ctx.enter_context(nc.Block())

        ss_x = [stats(NT) for _ in range(3)]
        rinv_x = [stats(NT) for _ in range(3)]
        u_s = stats(64).rearrange("p (n c) -> p n c", n=NT)
        l_s = stats(64).rearrange("p (n c) -> p n c", n=NT)
        t_s = stats(64).rearrange("p (n c) -> p n c", n=NT)
        beta = stats(16).rearrange("p (n c) -> p n c", n=NT)
        la = stats(48).rearrange("p (n c) -> p n c", n=NT)
        cs = stats(96)
        gb = stats(32)
        gtail = stats(16)
        eg_s = stats(16)
        et_s = stats(16)
        be_s = stats(16)
        cf = stats(32).rearrange("p (n c) -> p n c", n=NT)
        gbT = stats(256)
        qk_ss = stats(32).rearrange("p (n c) -> p n c", n=NT)
        qk_ri = stats(32).rearrange("p (n c) -> p n c", n=NT)
        cT = gbT
        mx = stats(64)
        o_ss, o_ri = stats(16), stats(16)
        f_ss = sb("f_ss", [P, NT, 32])
        f_ri = sb("f_ri", [P, NT, 32])
        den = sb("den", [P, 32])
        dri = sb("dri", [P, 32])
        sg = sb("sg", [P, NT, NE])
        sel = sb("sel", [P, NT, NE])
        top = sb("top", [P, NT, 8])
        gsum = sb("gsum", [P, NT, 2])
        e_ss, e_ri = sb("e_ss", [P, NT]), sb("e_ri", [P, NT])

        @block.sync
        def _(sp):
            sp.dma_start(h[:, :, :], x[0].rearrange("(n p) d -> p n d", p=P)).then_inc(x_loaded, 16)
            rv = rows
            sp.dma_start(rv[R_CONV:R_NMIX, :], conv_w[0].rearrange("i (c q) -> (i c) q", q=P)).then_inc(rows_loaded, 16)
            for r, v in ((R_NMIX, norm_mix), (R_NPG, ple_gate_norm)):
                sp.dma_start(rv[r:r + 8, :], v.rearrange("a (c q) -> (a c) q", q=P)).then_inc(rows_loaded, 16)
            with nc.allow_non_contiguous_dma(reason="4 KB in all"):
                sp.dma_start(rv[R_NFFN:R_NFFN + 8, :], norm_ffn.rearrange("a (q c) -> (a c) q", q=P)).then_inc(rows_loaded, 16)
            sp.dma_start(rv[R_GDN:R_GDN + 1, :], gdn_norm).then_inc(rows_loaded, 16)
            for r, v in ((R_QN, q_norm), (R_KN, k_norm)):
                for half in range(2):
                    sp.dma_start(rv[r:r + 1, FD * half:FD * half + FD], v).then_inc(rows_loaded, 16)

            def load(t):
                src, c0, _ = wtiles[t]
                if t >= A_SLOTS:
                    wait_filled(sp, wtiles[t - A_SLOTS][2])
                sp.dma_start(wring[t % A_SLOTS], src.rearrange("(c q) n -> q c n", q=P)[:, :, c0:c0 + WT]).then_inc(w_loaded[t % A_SLOTS], 16)

            for t in range(3):
                load(t)
            sp.dma_start(bias3[:, 0:8], dt_bias.to_broadcast([P, 8])).then_inc(bias_loaded, 16)
            sp.dma_start(bias3[:, 16:32], fox_f_bias.to_broadcast([P, 16])).then_inc(bias_loaded, 16)
            sp.dma_start(nega[:, :], a_log.to_broadcast([P, 8])).then_inc(bias_loaded, 16)
            sp.dma_start(rbias[:, :], router_bias.to_broadcast([P, NE])).then_inc(bias_loaded, 16)
            wv = w_in2.rearrange("(c q) n -> q c n", q=P)
            sp.dma_start(wsm[:, :, 0:16], wv[:, :, C_AB:C_AB + 16]).then_inc(small_loaded, 16)
            sp.dma_start(wsm[:, :, 16:32], wv[:, :, C_F:C_F + 16]).then_inc(small_loaded, 16)
            sp.dma_start(wrt[:, :, :], w_router[0].rearrange("(q c) n -> q c n", q=P)).then_inc(small_loaded, 16)
            for t in range(3, len(wtiles)):
                load(t)

            sp.wait_ge(h_ready, 4)
            sp.dma_start(p_t, p[0, 0].rearrange("(n q) c -> q n c", q=P)).then_inc(p_loaded, 16)
            sp.dma_start(wple, w_ple[0].rearrange("(c q) d -> q c d", q=P)).then_inc(p_loaded, 16)
            sp.dma_start(plen, ple_norm.to_broadcast([P, D])).then_inc(p_loaded, 16)

            def load_expert(s, g_w, u_w, d_w):
                sp.dma_start(eg[s], g_w.rearrange("(q c) f -> q c f", c=KC)).then_inc(e_loaded[s], 16)
                sp.dma_start(eu[s], u_w.rearrange("(q c) f -> q c f", c=KC)).then_inc(e_loaded[s], 16)
                sp.dma_start(ed[s], d_w.rearrange("(q c) d -> q c d", c=2)).then_inc(e_loaded[s], 16)

            load_expert(3, ws_gate[0], ws_up[0], ws_down[0])
            for s in range(3):
                load_expert(s, we_gate[0, s], we_up[0, s], we_down[0, s])
            with sp.Fori(0, NE // 4 - 1) as i:
                for j in range(4):
                    sp.wait_ge(down_done, i * 4 + (j + 1))
                    e = i * 4 + (j + 3)
                    load_expert((j + 3) % 4, *(w[0, bass.ds(e, 1)].rearrange("a r c -> (a r) c") for w in (we_gate, we_up, we_down)))
            sp.wait_ge(down_done, NE - 4 + 1)
            load_expert(3, *(w[0, NE - 1] for w in (we_gate, we_up, we_down)))
            sp.wait_ge(down_done, NE + 1)
            for j in range(2):
                sp.dma_start(wpg[j], w_ple_gate[0].rearrange("(c q) n -> q c n", q=P)[:, :, WT * j:WT * j + WT]).then_inc(wpg_loaded, 16)
            for n in range(NT):
                sp.wait_ge(out_ready, n + 1)
                sp.dma_start(out[0, n * P:(n + 1) * P, :], gt[:, n, :]).then_inc(out_stored, 16)
            sp.wait_ge(out_stored, 32)

        @block.gpsimd
        def _(pool):
            g = nc.gpsimd
            steps = [0]

            def seq(ins):
                steps[0] += 1
                ins.then_inc(pool_step, 1)
                pool.wait_ge(pool_step, steps[0])

            def select(t, src, op, fill, base, pattern, mult):
                return g.affine_select(out=t, in_=src, compare_op=op, fill=fill, base=base, pattern=pattern, channel_multiplier=mult)

            g.memset(ident[:, :], 0.0).then_inc(pool_step, 1)
            g.memset(ones[:, :], 1.0).then_inc(pool_step, 1)
            g.memset(nhalf[:, :], -0.5).then_inc(pool_step, 1)
            g.memset(bias3[:, 8:16], 0.0).then_inc(pool_step, 1)
            g.memset(negm[:, :], 0.0).then_inc(pool_step, 1)
            steps[0] = 5
            pool.wait_ge(pool_step, 5)
            select(ident[:, :], ident[:, :], ALU.not_equal, 1.0, 0, [[-1, P]], 1).then_inc(consts, 1)
            def roots(k):
                for n in range(NT):
                    pool.wait_ge(sumsq, NT * k + n + 1)
                    seq(g.tensor_scalar(rinv_x[k][:, n:n + 1], ss_x[k][:, n:n + 1], 1.0 / D, EPS, ALU.mult, ALU.add))
                    g.tensor_tensor(rinv_x[k][:, n:n + 1], rinv_x[k][:, n:n + 1], nhalf[:, 0:1], ALU.pow).then_inc(rinv_made, 1)
            roots(0)
            select(tri[:, :], ones[:, :], ALU.is_ge, 0.0, 0, [[1, P]], -1).then_inc(consts, 1)
            select(stri[:, :], ones[:, :], ALU.is_gt, 0.0, 0, [[1, P]], -1).then_inc(consts, 1)
            select(negm[:, :], negm[:, :], ALU.is_ge, MASKED, 0, [[-1, P]], 1).then_inc(consts, 1)
            for lv in range(LEVELS + 1):
                b = 1 << lv
                nb = P // b
                v = blocks[:, lv, :].rearrange("p (k w) -> p k w", w=b)
                seq(select(v, ones[:, :].rearrange("p (k w) -> p k w", w=b), ALU.is_ge, 0.0, 0, [[-b, nb], [0, b]], 1)) if lv < LEVELS else seq(g.tensor_copy(blocks[:, lv, :], ones[:, :]))
                if lv < LEVELS:
                    seq(select(v, v, ALU.is_ge, 0.0, b - 1, [[b, nb], [0, b]], -1))
            for lv in range(LEVELS):
                g.tensor_tensor(lmask[:, lv, :], blocks[:, lv + 1, :], blocks[:, lv, :], ALU.subtract).then_inc(masks_made, 1)
            wait_drained(pool, "gbT")
            pool.wait_ge(masks_made, LEVELS)
            for j in range(4):
                for n in range(NT):
                    i = NT * j + n
                    pool.wait_ge(qkss, i + 1)
                    v = qk_ri[:, n, 4 * j:4 * j + 4]
                    seq(g.tensor_scalar(v, qk_ss[:, n, 4 * j:4 * j + 4], 1.0, EPS, ALU.mult, ALU.add))
                    ins = g.tensor_tensor(v, v, nhalf[:, 0:4], ALU.pow)
                    if j < 2:
                        seq(ins)
                        ins = g.tensor_scalar(v, v, DK ** -0.5, 0.0, ALU.mult, ALU.add)
                    ins.then_inc(qkrinv, 1)
            for t, lo, s in ((gd, 0, gd_made), (bd, P, bd_made)):
                src = bc(gbT[0:16, lo:lo + P], 1, 16)
                select(t[0:16], src, ALU.is_equal, 0.0, 0, [[-1, 16], [0, P]], 1).then_inc(s, 1)
            for n in range(NT):
                pool.wait_ge(fss, n + 1)
                seq(g.tensor_scalar(f_ri[:, n, :], f_ss[:, n, :], 1.0 / FD, EPS, ALU.mult, ALU.add))
                g.tensor_tensor(f_ri[:, n, :], f_ri[:, n, :], nhalf[:, :], ALU.pow).then_inc(frinv, 1)
            pool.wait_ge(oss, 1)
            seq(g.tensor_scalar(o_ri, o_ss, 1.0 / DK, EPS, ALU.mult, ALU.add))
            g.tensor_tensor(o_ri, o_ri, nhalf[:, 0:16], ALU.pow).then_inc(orinv, 1)
            wait_drained(pool, "cT")
            for j in range(2):
                wait_filled(pool, f"o1.{j}")
            select(cd[0:16], bc(cT[0:16, :], 1, 16), ALU.is_equal, 0.0, 0, [[-1, 16], [0, S]], 1).then_inc(cd_made, 1)
            roots(1)
            for n in range(NT):
                pool.wait_ge(ess, n + 1)
                seq(g.tensor_scalar(e_ri[:, n:n + 1], e_ss[:, n:n + 1], 1.0 / D, EPS, ALU.mult, ALU.add))
                g.tensor_tensor(e_ri[:, n:n + 1], e_ri[:, n:n + 1], nhalf[:, 0:1], ALU.pow).then_inc(erinv, 1)
            roots(2)

        @block.scalar
        def _(act):
            a = nc.scalar
            steps = [0]

            def seq(ins):
                steps[0] += 1
                ins.then_inc(act_step, 1)
                act.wait_ge(act_step, steps[0])

            def squares(k, src, junk):
                for n in range(NT):
                    a.activation(junk[:, n, :], src[:, n, :], ACT.Square, accum_out=ss_x[k][:, n:n + 1]).then_inc(sumsq, 1)

            def drain(name, dst, func=ACT.Copy, cols_used=512, **kw):
                wait_filled(act, name)
                a.activation(dst, ps(name)[:, 0:cols_used] if len(dst.shape) == 2 else
                             ps(name)[:, 0:cols_used].rearrange("p (a b) -> p a b", a=dst.shape[1]), func, **kw).then_inc(drained[place[name][0]], 1)

            act.wait_ge(x_loaded, 16)
            squares(0, h, xn)
            for c in range(12):
                wait_drained(act, f"qkv.{c}")
                v = qkvT[:, 2 * c:2 * c + 2, :]
                a.activation(v, v, ACT.Silu).then_inc(conv_done, 1)
            for j in range(2):
                for n in range(NT):
                    drain(f"z.{j}.{n}", zs[:, n, WT * j:WT * j + WT], ACT.Silu)
            act.wait_ge(logs_ready, 1)
            seq(a.activation(t_s, t_s, ACT.Exp, scale=-1.0))
            a.activation(l_s, t_s, ACT.Ln, bias=1.0).then_inc(soft, 1)
            a.activation(beta, u_s[:, :, 8:16], ACT.Exp, scale=-1.0).then_inc(soft, 1)
            a.activation(nega[:, :], nega[:, :], ACT.Exp).then_inc(soft, 1)
            for j in range(4):
                for n in range(NT):
                    drain(f"tq.{n}.{j}", qk[:, n, WT * j:WT * j + WT])
            act.wait_ge(gstat, 1)
            a.activation(eg_s, gb[:, 0:16], ACT.Exp).then_inc(geg, 1)
            a.activation(et_s, gtail, ACT.Exp).then_inc(geg, 1)
            for j in range(6):
                for n in range(NT):
                    drain(f"fox.{j}.{n}", fox[:, n, WT * j:WT * j + WT])
            for n in range(NT):
                for j in range(4):
                    drain(f"tk.{n}.{j}", qkvT[:, 4 * j:4 * j + 4, n * P:n * P + P])
            for j in range(4):
                act.wait_ge(d_ready, j + 1)
                a.activation(dT[:, 4 * j:4 * j + 4, :], dT[:, 4 * j:4 * j + 4, :], ACT.Exp).then_inc(dexp_ready, 1)
            for lv in range(1, LEVELS):
                for j in range(4):
                    drain(f"P.{lv}.{j}", pb[:, 4 * j:4 * j + 4, :])
            for j in range(2):
                hs = slice(4 * j, 4 * j + 4)
                drain(f"tg.{j}", qgT[:, hs, :])
                drain(f"wT.{j}", wTn[:, hs, :], scale=-1.0)
                drain(f"u0.{j}", u0[:, hs, :])
            for j in range(2):
                drain(f"o0.{j}", oa[:, 0, WT * j:WT * j + WT])
                drain(f"s1.{j}", s1[:, 4 * j:4 * j + 4, :])
            for j in range(2):
                drain(f"u1.{j}", u1[:, 4 * j:4 * j + 4, :])
            for j in range(2):
                drain(f"o1.{j}", oa[:, 1, WT * j:WT * j + WT])
            for j in range(4):
                for n in range(NT):
                    drain(f"merge.{j}.{n}", merge[:, n, WT * j:WT * j + WT], ACT.Sigmoid)
            for n in range(NT):
                for j in range(2):
                    drain(f"oT.{n}.{j}", oT[:, 4 * j:4 * j + 4, n * P:n * P + P], scale=cols[:, R_GDN:R_GDN + 1])
            for n in range(NT):
                for j in range(4):
                    r = R_QN if j < 2 else R_KN
                    drain(f"fT.{n}.{j}", foxT[:, 4 * j:4 * j + 4, n * P:n * P + P], scale=cols[:, r:r + 1])
            for g in range(9):
                if g < 8:
                    for f in (2 * g, 2 * g + 1):
                        act.wait_ge(smax, 2 * f + 2)
                        for n in range(NT):
                            v = scores[f % 2][:, P:3 * P] if n else scores[f % 2][:, 0:P]
                            a.activation(v, v, ACT.Exp, bias=mx[:, 2 * f + n:2 * f + n + 1], accum_out=den[:, 2 * f + n:2 * f + n + 1]).then_inc(sexp, 1)
                if g > 0:
                    for f in (2 * g - 2, 2 * g - 1):
                        drain(f"pT.{f}", probsT[f % 2], cols_used=384)
                    drain(f"pv.{g - 1}", ofT[:, g - 1, :], cols_used=S)
            for n in range(NT):
                for j in range(2):
                    drain(f"mT.{n}.{j}", mixT[:, 4 * j:4 * j + 4, n * P:n * P + P])
            act.wait_ge(h_ready, 4)
            squares(1, h, hn)
            drain("router", sg[:, :, :], ACT.Sigmoid, cols_used=P)
            for n in range(NT):
                drain(f"pT2.{n}", pT[:, :, n * P:n * P + P], cols_used=S)
            for n in range(NT):
                for j in range(2):
                    drain(f"e.{n}.{j}", e_t[:, n, WT * j:WT * j + WT])
            for n in range(NT):
                act.wait_ge(xn_ready, 2 * NT)
                for j in range(2):
                    wait_drained(act, f"e.{n}.{j}")
                    wait_filled(act, f"hT.{NT - 1}.1")
                a.activation(hn[:, n, :], e_t[:, n, :], ACT.Square, accum_out=e_ss[:, n:n + 1]).then_inc(ess, 1)

            def expert(i):
                for n in range(NT):
                    act.wait_ge(gu_filled, i + n + 1)
                    a.activation(sil[n], bank[4 + n][:, 0:DE], ACT.Silu).then_inc(gu_silu, 1)
                for n in range(NT):
                    act.wait_ge(hidT_filled, i + n + 1)
                    a.activation(hidT[n], bank[6 + n][:, 0:DE].rearrange("p (c t) -> p c t", c=2), ACT.Copy).then_inc(hidT_ready, 1)

            expert(0)
            with act.Fori(1, NE + 1) as e:
                expert(e * 2)
            act.wait_ge(h_ready, 8)
            squares(2, h, hn)
            for j in range(2):
                for n in range(NT):
                    act.wait_ge(pg_filled, NT * j + n + 1)
                    a.activation(gt[:, n, WT * j:WT * j + WT], bank[4 + NT * j + n][:, :], ACT.Sigmoid).then_inc(sg_ready, 1)

        @block.tensor
        def _(pe):
            t = nc.tensor

            def open_bank(name):
                b, turn = place[name]
                if turn > 0:
                    pe.wait_ge(drained[b], turn)
                return bank[b]

            def close(ins, name):
                ins.then_inc(filled[place[name][0]], 1)

            def transposes(name, srcs, rows_in=P):
                o = open_bank(name)
                for i, v in enumerate(srcs):
                    w = v.shape[1]
                    ins = t.transpose(o[0:w, i * P:i * P + rows_in], v, ident[0:rows_in, 0:rows_in])
                close(ins, name)

            def project(name, w, n, lhs=actT):
                o = open_bank(name)
                for c in range(KC):
                    ins = t.matmul(o[:, :], lhs[:, c, n * P:n * P + P], w[:, c, :], start=(c == 0), stop=(c == KC - 1))
                close(ins, name)

            def weights(k):
                pe.wait_ge(w_loaded[k % A_SLOTS], 16 * (k // A_SLOTS + 1))
                return wring[k % A_SLOTS]

            pe.wait_ge(consts, 1)
            pe.wait_ge(rows_loaded, 16 * 9)
            transposes("cols", [rows[0:R_ALL, :]], R_ALL)
            for n in range(NT):
                pe.wait_ge(xn_ready, n + 1)
                for j in range(2):
                    transposes(f"xT.{n}.{j}", [xn[:, n, P * c:P * c + P] for c in range(4 * j, 4 * j + 4)])
            for n in range(NT):
                for j in range(2):
                    wait_drained(pe, f"xT.{n}.{j}")
            for c2 in range(12):
                w = weights(W_QKV + c2 // 2)
                o = open_bank(f"qkv.{c2}")
                for i in range(2):
                    col = (2 * c2 + i) % 4 * P
                    for c in range(KC):
                        ins = t.matmul(o[:, i * S:i * S + S], w[:, c, col:col + P], actT[:, c, :], start=(c == 0), stop=(c == KC - 1))
                close(ins, f"qkv.{c2}")
            pe.wait_ge(small_loaded, 48)
            o = open_bank("small")
            for n in range(NT):
                for c in range(KC):
                    ins = t.matmul(o[:, 32 * n:32 * n + 32], actT[:, c, n * P:n * P + P], wsm[:, c, :], start=(c == 0), stop=(c == KC - 1))
            close(ins, "small")
            for j in range(2):
                w = weights(W_Z + j)
                for n in range(NT):
                    project(f"z.{j}.{n}", w, n)
            pe.wait_ge(logs_ready, 2)
            pe.wait_ge(consts, 4)
            o = open_bank("cum")
            for k, m in enumerate((tri, ones)):
                for n in range(NT):
                    lo = 48 * k + 24 * n
                    ins = t.matmul(o[:, lo:lo + 24], m[:, :], la[:, n, :], start=True, stop=True)
            close(ins, "cum")
            pe.wait_ge(gstat, 1)
            transposes("gbT", [gb[:, 0:16], gb[:, 16:32]])
            for j in range(6):
                pe.wait_ge(conv_done, 2 * j + 2)
                for n in range(NT):
                    transposes(f"tq.{n}.{j}", [qkvT[:, c, n * P:n * P + P] for c in range(4 * j, 4 * j + 4)])
            for j in range(6):
                w = weights(W_FOX + j)
                for n in range(NT):
                    project(f"fox.{j}.{n}", w, n)
            pe.wait_ge(qk_normed, 8)
            for n in range(NT):
                for j in range(4):
                    transposes(f"tk.{n}.{j}", [qk[:, n, P * c:P * c + P] for c in range(4 * j, 4 * j + 4)])
            for nm, src, s in (("gb", gd, gd_made), ("bb", bd, bd_made)):
                pe.wait_ge(s, 1)
                for j in range(4):
                    o = open_bank(f"{nm}.{j}")
                    close(t.matmul(o[:, :], ones[0:16, :], src[0:16, 4 * j:4 * j + 4, :], start=True, stop=True), f"{nm}.{j}")

            def problems(name, lhs, rhs, hs=range(4)):
                o = open_bank(name)
                for i, b in enumerate(hs):
                    ins = t.matmul(o[:, i * P:i * P + P], lhs(b), rhs(b), start=True, stop=True)
                close(ins, name)

            def qTb(b):
                return qkvT[:, b % GH, b // GH * P:b // GH * P + P]

            def kTb(b):
                return qkvT[:, GH + b % GH, b // GH * P:b // GH * P + P]

            for n in range(NT):
                for j in range(4):
                    wait_drained(pe, f"tk.{n}.{j}")
            for j in range(4):
                bs = range(4 * j, 4 * j + 4)
                problems(f"kk.{j}", kTb, kTb, bs)
                problems(f"qk.{j}", kTb, qTb, bs)
            for lv in range(LEVELS):
                for j in range(4):
                    bs = range(4 * j, 4 * j + 4)
                    pe.wait_ge(m_ready, 4 * lv + j + 1)
                    if lv > 1:
                        wait_drained(pe, f"X.{lv - 1}.{j}")
                    if lv == 1:
                        wait_drained(pe, f"P.0.{j}")
                    problems(f"P.{lv}.{j}", lambda b: mT[:, b, :], (lambda b: xi[:, b, :]) if lv else (lambda b: ident[:, :]), bs)
                if lv == 0:
                    continue
                for j in range(4):
                    bs = range(4 * j, 4 * j + 4)
                    wait_drained(pe, f"P.{lv}.{j}")
                    if lv > 1:
                        wait_drained(pe, f"V.{lv - 1}.{j}")
                    if lv < LEVELS - 1:
                        problems(f"X.{lv}.{j}", lambda b: vi[:, b, :], lambda b: pb[:, b, :], bs)
                    problems(f"V.{lv}.{j}", lambda b: pb[:, b, :], lambda b: vi[:, b, :], bs)
            for j in range(4):
                wait_drained(pe, f"V.{LEVELS - 1}.{j}")
            pe.wait_ge(scaled, 3)
            for j in range(2):
                hs = range(4 * j, 4 * j + 4)
                transposes(f"tg.{j}", [qk[:, 1, P * c:P * c + P] for c in hs])
                problems(f"wT.{j}", lambda b: kbe[:, b, :], lambda b: vi[:, GH + b, :], hs)
                problems(f"u0.{j}", lambda b: vi[:, b, :], lambda b: vbeta[:, b, :], hs)
            for j in range(2):
                hs = range(4 * j, 4 * j + 4)
                wait_drained(pe, f"u0.{j}")
                problems(f"o0.{j}", lambda b: dT[:, b, :], lambda b: u0[:, b, :], hs)
                problems(f"s1.{j}", lambda b: qk[:, 0, D + P * b:D + P * b + P], lambda b: u0[:, b, :], hs)

            def two(name, terms, hs):
                o = open_bank(name)
                for i, b in enumerate(hs):
                    for k, (lhs, rhs) in enumerate(terms):
                        ins = t.matmul(o[:, i * P:i * P + P], lhs(b), rhs(b), start=(k == 0), stop=(k == 1))
                close(ins, name)

            for j in range(2):
                wait_drained(pe, f"wT.{j}")
                wait_drained(pe, f"s1.{j}")
                two(f"u1.{j}", [(lambda b: vi[:, GH + b, :], lambda b: vbeta[:, GH + b, :]),
                                (lambda b: wTn[:, b, :], lambda b: s1[:, b, :])], range(4 * j, 4 * j + 4))
            for j in range(2):
                wait_drained(pe, f"tg.{j}")
                wait_drained(pe, f"u1.{j}")
                two(f"o1.{j}", [(lambda b: qgT[:, b, :], lambda b: s1[:, b, :]),
                                (lambda b: dT[:, GH + b, :], lambda b: u1[:, b, :])], range(4 * j, 4 * j + 4))
            for j in range(4):
                w = weights(W_MERGE + j)
                for n in range(NT):
                    project(f"merge.{j}.{n}", w, n)
            for n in range(NT):
                pe.wait_ge(o_normed, n + 1)
                for j in range(2):
                    transposes(f"oT.{n}.{j}", [oa[:, n, P * c:P * c + P] for c in range(4 * j, 4 * j + 4)])
            for n in range(NT):
                pe.wait_ge(f_normed, n + 1)
                for j in range(4):
                    transposes(f"fT.{n}.{j}", [fox[:, n, P * c:P * c + P] for c in range(4 * j, 4 * j + 4)])
            o = open_bank("cT")
            for n in range(NT):
                ins = t.transpose(o[0:16, n * P:n * P + P], cf[:, n, :], ident[:, :])
            close(ins, "cT")
            pe.wait_ge(cd_made, 1)
            for j in range(8):
                o = open_bank(f"cb.{j}")
                close(t.matmul(o[:, :], ones[0:16, :], cd[0:16, 2 * j:2 * j + 2, :], start=True, stop=True), f"cb.{j}")
            for n in range(NT):
                for j in range(2):
                    wait_drained(pe, f"oT.{n}.{j}")
            for j in range(2):
                w = weights(W_YA + j)
                for n in range(NT):
                    project(f"ya.{j}.{n}", w, n, oT)
            for n in range(NT):
                for j in range(4):
                    wait_drained(pe, f"fT.{n}.{j}")
            for g in range(9):
                if g < 8:
                    for i in range(2):
                        lo = FD * i
                        o = open_bank(f"s.{2 * g + i}")
                        t.matmul(o[:, 0:P], foxT[lo:lo + FD, g, 0:P], foxT[lo:lo + FD, 8 + g, 0:P], start=True, stop=True)
                        close(t.matmul(o[:, P:P + S], foxT[lo:lo + FD, g, P:S], foxT[lo:lo + FD, 8 + g, :], start=True, stop=True), f"s.{2 * g + i}")
                if g > 0:
                    for i in range(2):
                        f = 2 * g - 2 + i
                        pe.wait_ge(sdiv, f + 1)
                        transposes(f"pT.{f}", [scores[f % 2][:, k * P:k * P + P] for k in range(3)])
                    name = f"pv.{g - 1}"
                    o = open_bank(name)
                    for i in range(2):
                        f = 2 * g - 2 + i
                        lo = FD * i
                        wait_drained(pe, f"pT.{f}")
                        v = [fox[:, n, 2 * D + FD * f:2 * D + FD * f + FD] for n in range(NT)]
                        t.matmul(o[lo:lo + FD, 0:P], v[0], probsT[i][:, 0:P], start=True, stop=True)
                        t.matmul(o[lo:lo + FD, P:S], v[0], probsT[i][:, P:2 * P], start=True, stop=False)
                        ins = t.matmul(o[lo:lo + FD, P:S], v[1], probsT[i][:, 2 * P:3 * P], start=False, stop=True)
                    close(ins, name)
            for g in range(8):
                wait_drained(pe, f"pv.{g}")
            for j in range(2):
                w = weights(W_YF + j)
                for n in range(NT):
                    project(f"yf.{j}.{n}", w, n, ofT)
            for n in range(NT):
                pe.wait_ge(mixed, 2 * NT)
                for j in range(2):
                    transposes(f"mT.{n}.{j}", [mix[:, n, P * c:P * c + P] for c in range(4 * j, 4 * j + 4)])
            for n in range(NT):
                for j in range(2):
                    wait_drained(pe, f"mT.{n}.{j}")
            for j in range(2):
                w = weights(W_WO + j)
                for n in range(NT):
                    project(f"wo.{j}.{n}", w, n, mixT)
            for n in range(NT):
                pe.wait_ge(xn_ready, NT + n + 1)
                for j in range(2):
                    transposes(f"hT.{n}.{j}", [hn[:, n, P * c:P * c + P] for c in range(4 * j, 4 * j + 4)])
            for n in range(NT):
                for j in range(2):
                    wait_drained(pe, f"hT.{n}.{j}")
            o = open_bank("router")
            for n in range(NT):
                for c in range(KC):
                    ins = t.matmul(o[:, NE * n:NE * n + NE], actT[:, c, n * P:n * P + P], wrt[:, c, :], start=(c == 0), stop=(c == KC - 1))
            close(ins, "router")
            pe.wait_ge(p_loaded, 48)
            for n in range(NT):
                transposes(f"pT2.{n}", [p_t[:, n, 0:P], p_t[:, n, P:S]])
            for n in range(NT):
                wait_drained(pe, f"pT2.{n}")
            for n in range(NT):
                for j in range(2):
                    o = open_bank(f"e.{n}.{j}")
                    for c in range(2):
                        ins = t.matmul(o[:, :], pT[:, c, n * P:n * P + P], wple[:, c, WT * j:WT * j + WT], start=(c == 0), stop=(c == 1))
                    close(ins, f"e.{n}.{j}")
            for b in range(8):
                n_fills = len([1 for q in fills if place[q][0] == b])
                pe.wait_ge(drained[b], n_fills)

            def expert(s, loads, i, first=False, last=False):
                pe.wait_ge(e_loaded[s], loads)
                for n in range(NT):
                    for wk, part in ((eg, 0), (eu, DE)):
                        for c in range(KC):
                            ins = t.matmul(bank[4 + n][:, part:part + DE], actT[:, c, n * P:n * P + P], wk[s][:, c, :],
                                           start=(c == 0), stop=(c == KC - 1))
                    ins.then_inc(gu_filled, 1)
                for n in range(NT):
                    pe.wait_ge(hid_ready, i + n + 1)
                    for c in range(2):
                        ins = t.transpose(bank[6 + n][:, c * P:c * P + P], hid[n][:, c * P:c * P + P], ident[:, :])
                    ins.then_inc(hidT_filled, 1)
                for n in range(NT):
                    pe.wait_ge(hidT_ready, i + n + 1)
                    for j in range(2):
                        for c in range(2):
                            ins = t.matmul(bank[2 * n + j][:, :], hidT[n][:, c, :], ed[s][:, c, WT * j:WT * j + WT],
                                           start=first and c == 0, stop=last and c == 1, skip_group_check=True)
                ins.then_inc(down_done, 1)

            expert(3, 48, 0, first=True)
            with pe.Fori(0, NE // 4 - 1) as i:
                for j in range(4):
                    expert(j, (i + (2 if j == 3 else 1)) * 48, i * 8 + (2 * j + 2))
            for j in range(4):
                expert(j, 48 * (NE // 4 + (j == 3)), 2 * NE - 8 + 2 * j + 2, last=(j == 3))
            for n in range(NT):
                pe.wait_ge(xn_ready, 2 * NT + n + 1)
                for j in range(2):
                    for c in range(4):
                        ins = t.transpose(bank[2 * n + j][:, c * P:c * P + P], hn[:, n, (4 * j + c) * P:(4 * j + c + 1) * P], ident[:, :])
                    ins.then_inc(hidT_filled, 1)
            pe.wait_ge(wpg_loaded, 32)
            pe.wait_ge(e_ready, NT + 2 * NT)
            for j in range(2):
                for n in range(NT):
                    for c in range(KC):
                        ins = t.matmul(bank[4 + NT * j + n][:, :], actT[:, c, n * P:n * P + P], wpg[j][:, c, :], start=(c == 0), stop=(c == KC - 1))
                    ins.then_inc(pg_filled, 1)

        @block.vector
        def _(dve):
            v = nc.vector
            steps = [0]

            def step(ins):
                steps[0] += 1
                ins.then_inc(dve_step, 1)
                return steps[0]

            def seq(ins):
                dve.wait_ge(dve_step, step(ins))

            def close(ins, name):
                ins.then_inc(drained[place[name][0]], 1)

            def blocks4(name, n=4):
                return ps(name)[:, 0:n * P].rearrange("p (a b) -> p a b", a=n)

            def norm(k, dst):
                for n in range(NT):
                    dve.wait_ge(rinv_made, NT * k + n + 1)
                    v.tensor_scalar(dst[:, n, :], h[:, n, :], rinv_x[k][:, n:n + 1], None, ALU.mult).then_inc(xn_ready, 1)

            wait_filled(dve, "cols")
            seq(v.tensor_copy(cols[:, 0:R_ALL], ps("cols")[:, 0:R_ALL]))
            close(v.tensor_scalar(cols[:, R_QN:R_QN + 1], cols[:, R_QN:R_QN + 1], FD ** -0.5, None, ALU.mult), "cols")
            norm(0, xn)
            wait_drained(dve, "cols")
            for n in range(NT):
                for j in range(2):
                    nm = f"xT.{n}.{j}"
                    wait_filled(dve, nm)
                    close(v.tensor_tensor(actT[:, 4 * j:4 * j + 4, n * P:n * P + P], blocks4(nm), bc(cols[:, R_NMIX + 4 * j:R_NMIX + 4 * j + 4], 2, P), ALU.mult), nm)
            for c2 in range(12):
                nm = f"qkv.{c2}"
                wait_filled(dve, nm)
                for s in range(4):
                    for i in range(2):
                        ct = 2 * c2 + i
                        wcol = cols[:, R_CONV + 24 * (3 - s) + ct:R_CONV + 24 * (3 - s) + ct + 1]
                        src = ps(nm)[:, i * S:i * S + S - s]
                        dst = qkvT[:, ct, s:S]
                        if s == 0:
                            k = step(v.tensor_scalar(dst, src, wcol, None, ALU.mult))
                        else:
                            dve.wait_ge(dve_step, k - 1 + i if s == 1 else k - 1)
                            ins = v.scalar_tensor_tensor(out=dst, in0=src, scalar=wcol, in1=dst, op0=ALU.mult, op1=ALU.add)
                            if s == 3 and i == 1:
                                close(ins, nm)
                            else:
                                k = step(ins)
            dve.wait_ge(bias_loaded, 64)
            dve.wait_ge(consts, 1)
            wait_filled(dve, "small")
            close(v.tensor_tensor(u_s, ps("small")[:, 0:64].rearrange("p (n c) -> p n c", n=NT), bc(bias3[:, :], 1, NT), ALU.add), "small")
            wait_drained(dve, "small")
            seq(v.tensor_scalar(t_s, u_s, -1.0, None, ALU.mult))
            v.tensor_tensor(t_s, t_s, u_s, ALU.max).then_inc(logs_ready, 1)
            dve.wait_ge(soft, 3)
            seq(v.tensor_scalar(t_s[:, :, 0:8], u_s[:, :, 0:8], 0.0, None, ALU.max))
            seq(v.tensor_tensor(t_s[:, :, 0:8], t_s[:, :, 0:8], l_s[:, :, 0:8], ALU.add))
            seq(v.tensor_scalar(nega[:, :], nega[:, :], -1.0, None, ALU.mult))
            seq(v.tensor_tensor(la[:, :, 0:8], t_s[:, :, 0:8], bc(nega[:, :], 1, NT), ALU.mult))
            seq(v.tensor_scalar(t_s[:, :, 16:32], u_s[:, :, 16:32], 0.0, None, ALU.min))
            v.tensor_tensor(la[:, :, 8:24], t_s[:, :, 16:32], l_s[:, :, 16:32], ALU.subtract).then_inc(logs_ready, 1)
            seq(v.tensor_scalar(beta, beta, 1.0, None, ALU.add))
            seq(v.reciprocal(beta, beta))
            wait_filled(dve, "cum")
            close(v.tensor_copy(cs, ps("cum")[:, 0:96]), "cum")
            wait_drained(dve, "cum")
            run = cs[:, 0:48].rearrange("p (n c) -> p n c", n=NT)
            tot = cs[:, 48:96].rearrange("p (n c) -> p n c", n=NT)
            seq(v.tensor_tensor(gtail.rearrange("p (n c) -> p n c", n=NT), tot[:, :, 0:8], run[:, :, 0:8], ALU.subtract))
            seq(v.tensor_scalar(cf[:, 0, :], run[:, 0, 8:24], -1.0, None, ALU.mult))
            seq(v.tensor_tensor(cf[:, 1, :], run[:, 1, 8:24], tot[:, 0, 8:24], ALU.add))
            seq(v.tensor_scalar(cf[:, 1, :], cf[:, 1, :], -1.0, None, ALU.mult))
            seq(v.tensor_copy(gb[:, 16:32].rearrange("p (n c) -> p n c", n=NT), beta))
            v.tensor_copy(gb[:, 0:16].rearrange("p (n c) -> p n c", n=NT), run[:, :, 0:8]).then_inc(gstat, 1)
            wait_filled(dve, "gbT")
            close(v.tensor_copy(gbT[0:16, :], ps("gbT")[0:16, 0:256]), "gbT")
            for j in range(4):
                for n in range(NT):
                    nm = f"tq.{n}.{j}"
                    wait_drained(dve, nm)
                    src = qk[:, n, WT * j:WT * j + WT]
                    seq(v.tensor_tensor(sq[:, 0:WT], src, src, ALU.mult))
                    v.tensor_reduce(qk_ss[:, n, 4 * j:4 * j + 4], sq[:, 0:WT].rearrange("p (a b) -> p a b", a=4), AX.X, ALU.add).then_inc(qkss, 1)
                    dve.wait_ge(qkss, NT * j + n + 1)
            for j in range(2):
                for n in range(NT):
                    nm = f"tq.{n}.{4 + j}"
                    wait_filled(dve, nm)
                    close(v.tensor_tensor(vbeta[:, GH * n + 4 * j:GH * n + 4 * j + 4, :], blocks4(nm), bc(beta[:, n, 4 * j:4 * j + 4], 2, P), ALU.mult), nm)
            for j in range(4):
                for n in range(NT):
                    dve.wait_ge(qkrinv, NT * j + n + 1)
                    src = qk[:, n, WT * j:WT * j + WT].rearrange("p (a b) -> p a b", a=4)
                    v.tensor_tensor(src, src, bc(qk_ri[:, n, 4 * j:4 * j + 4], 2, P), ALU.mult).then_inc(qk_normed, 1)
            dve.wait_ge(qk_normed, 8)
            dve.wait_ge(consts, 4)
            for j in range(4):
                nm = f"gb.{j}"
                wait_filled(dve, nm)
                d4 = dT[:, 4 * j:4 * j + 4, :]
                close(v.tensor_tensor(d4, blocks4(nm), bc(gb[:, 4 * j:4 * j + 4], 2, P), ALU.subtract), nm)
                wait_drained(dve, nm)
                v.tensor_scalar(d4, d4, 0.0, None, ALU.min).then_inc(d_ready, 1)
            for j in range(4):
                dve.wait_ge(dexp_ready, j + 1)
                d4 = dT[:, 4 * j:4 * j + 4, :]
                v.tensor_tensor(d4, d4, bc(tri[:, :], 1, 4), ALU.mult).then_inc(d_masked, 1)
            for j in range(4):
                dve.wait_ge(d_masked, j + 1)
                nm = f"bb.{j}"
                l4, d4 = lT[:, 4 * j:4 * j + 4, :], dT[:, 4 * j:4 * j + 4, :]
                seq(v.tensor_tensor(l4, d4, bc(stri[:, :], 1, 4), ALU.mult))
                wait_filled(dve, nm)
                close(v.tensor_tensor(l4, l4, blocks4(nm), ALU.mult), nm)
            for j in range(4):
                l4, d4 = lT[:, 4 * j:4 * j + 4, :], dT[:, 4 * j:4 * j + 4, :]
                wait_drained(dve, f"bb.{j}")
                wait_filled(dve, f"kk.{j}")
                close(v.tensor_tensor(l4, l4, blocks4(f"kk.{j}"), ALU.mult), f"kk.{j}")
                wait_filled(dve, f"qk.{j}")
                close(v.tensor_tensor(d4, d4, blocks4(f"qk.{j}"), ALU.mult), f"qk.{j}")

            dve.wait_ge(masks_made, LEVELS)

            def coupling(lv):
                for j in range(4):
                    if lv == 0:
                        wait_drained(dve, f"kk.{j}")
                    else:
                        wait_filled(dve, f"P.{lv - 1}.{j}")
                    v.tensor_tensor(mT[:, 4 * j:4 * j + 4, :], lT[:, 4 * j:4 * j + 4, :], bc(lmask[:, lv, :], 1, 4), ALU.mult).then_inc(m_ready, 1)

            coupling(0)
            for j in range(4):
                dve.wait_ge(m_ready, j + 1)
                wait_filled(dve, f"gb.{j}")
                wait_filled(dve, f"bb.3")
                seq(v.tensor_tensor(vi[:, 4 * j:4 * j + 4, :], bc(ident[:, :], 1, 4), mT[:, 4 * j:4 * j + 4, :], ALU.subtract))
                nm = f"P.0.{j}"
                wait_filled(dve, nm)
                close(v.tensor_tensor(xi[:, 4 * j:4 * j + 4, :], bc(ident[:, :], 1, 4), blocks4(nm), ALU.subtract), nm)
            for lv in range(1, LEVELS):
                coupling(lv)
                for j in range(4):
                    for t, nm in ((xi, f"X.{lv}.{j}"), (vi, f"V.{lv}.{j}")):
                        if t is xi and lv == LEVELS - 1:
                            continue
                        wait_filled(dve, nm)
                        if t is xi and lv > 1:
                            wait_drained(dve, f"X.{lv - 1}.{j}")
                        elif t is xi:
                            wait_drained(dve, f"P.0.{j}")
                        elif lv > 1:
                            wait_drained(dve, f"V.{lv - 1}.{j}")
                        t4 = t[:, 4 * j:4 * j + 4, :]
                        close(v.tensor_tensor(t4, t4, blocks4(nm), ALU.subtract), nm)
            dve.wait_ge(geg, 2)
            seq(v.tensor_tensor(be_s, eg_s, gb[:, 16:32], ALU.mult))
            q1 = qk[:, 1, 0:D].rearrange("p (h d) -> p h d", h=GH)
            k0 = qk[:, 0, D:2 * D].rearrange("p (h d) -> p h d", h=GH)
            k1 = qk[:, 1, D:2 * D].rearrange("p (h d) -> p h d", h=GH)
            for n in range(NT):
                for j in range(4):
                    wait_drained(dve, f"tk.{n}.{j}")
            v.tensor_tensor(q1, q1, bc(eg_s[:, 8:16], 2, P), ALU.mult).then_inc(scaled, 1)
            wait_filled(dve, f"P.{LEVELS - 1}.3")
            v.tensor_tensor(kbe, k1, bc(be_s[:, 8:16], 2, P), ALU.mult).then_inc(scaled, 1)
            v.tensor_tensor(k0, k0, bc(et_s[:, 0:8], 2, P), ALU.mult).then_inc(scaled, 1)
            for n in range(NT):
                for part in range(2):
                    for j in range(2):
                        wait_drained(dve, f"fox.{2 * part + j}.{n}")
                    wait_filled(dve, "o1.1")
                    src = fox[:, n, D * part:D * part + D]
                    seq(v.tensor_tensor(at(TPB, 1024), src, src, ALU.mult))
                    ins = v.tensor_reduce(f_ss[:, n, 16 * part:16 * part + 16], at(TPB, 1024).rearrange("p (a b) -> p a b", a=16), AX.X, ALU.add)
                    if part:
                        ins.then_inc(fss, 1)
                        dve.wait_ge(fss, n + 1)
                    else:
                        seq(ins)
            for nm in ("o0.0", "o0.1", "o1.0", "o1.1"):
                wait_drained(dve, nm)
            o16 = oa.rearrange("p n (h v) -> p (n h) v", h=GH)
            for n in range(NT):
                seq(v.tensor_tensor(at(TPB, 1024), oa[:, n, :], oa[:, n, :], ALU.mult))
                ins = v.tensor_reduce(o_ss[:, 8 * n:8 * n + 8], at(TPB, 1024).rearrange("p (a b) -> p a b", a=8), AX.X, ALU.add)
                if n:
                    ins.then_inc(oss, 1)
                else:
                    seq(ins)
            for n in range(NT):
                dve.wait_ge(frinv, n + 1)
                src = fox[:, n, 0:2 * D].rearrange("p (a b) -> p a b", a=32)
                v.tensor_tensor(src, src, bc(f_ri[:, n, :], 2, FD), ALU.mult).then_inc(f_normed, 1)
            dve.wait_ge(orinv, 1)
            for j in range(2):
                for n in range(NT):
                    wait_drained(dve, f"z.{j}.{n}")
            for n in range(NT):
                o8 = o16[:, 8 * n:8 * n + 8, :]
                seq(v.tensor_tensor(o8, o8, bc(o_ri[:, 8 * n:8 * n + 8], 2, P), ALU.mult))
                v.tensor_tensor(oa[:, n, :], oa[:, n, :], zs[:, n, :], ALU.mult).then_inc(o_normed, 1)
            wait_filled(dve, "cT")
            dve.wait_ge(bd_made, 1)
            close(v.tensor_copy(cT[0:16, :], ps("cT")[0:16, 0:256]), "cT")
            for n in range(NT):
                for j in range(2):
                    wait_filled(dve, f"oT.{n}.{j}")
            for j in range(8):
                nm = f"cb.{j}"
                wait_filled(dve, nm)
                src = ps(nm)[:, :].rearrange("p (f k) -> p f k", f=2)
                dst = cbm[:, 2 * j:2 * j + 2, :]
                v.tensor_tensor(dst[:, :, 0:P], src[:, :, 0:P], bc(negm[:, :], 1, 2), ALU.add).then_inc(dve_step, 1)
                v.tensor_copy(dst[:, :, P:2 * P], src[:, :, 0:P]).then_inc(dve_step, 1)
                steps[0] += 2
                close(v.tensor_tensor(dst[:, :, 2 * P:3 * P], src[:, :, P:S], bc(negm[:, :], 1, 2), ALU.add), nm)
            wait_filled(dve, "cb.7")
            for j in range(2):
                for n in range(NT):
                    nm = f"ya.{j}.{n}"
                    wait_filled(dve, nm)
                    for jm in range(4):
                        wait_drained(dve, f"merge.{jm}.{n}")
                    close(v.tensor_tensor(mix[:, n, WT * j:WT * j + WT], ps(nm)[:, :], merge[:, n, WT * j:WT * j + WT], ALU.mult), nm)
            for g in range(8):
                wait_drained(dve, f"cb.{g}")
            for g in range(9):
                if g < 8:
                    for f in (2 * g, 2 * g + 1):
                        nm = f"s.{f}"
                        wait_filled(dve, nm)
                        if g > 0:
                            wait_filled(dve, f"pT.{f - 2}")
                        sc = scores[f % 2]
                        close(v.tensor_tensor(sc, ps(nm)[:, 0:384], cbm[:, f, :], ALU.add), nm)
                        wait_drained(dve, nm)
                        v.tensor_reduce(mx[:, 2 * f:2 * f + 1], sc[:, 0:P], AX.X, ALU.max, negate=True).then_inc(smax, 1)
                        v.tensor_reduce(mx[:, 2 * f + 1:2 * f + 2], sc[:, P:3 * P], AX.X, ALU.max, negate=True).then_inc(smax, 1)
                    for f in (2 * g, 2 * g + 1):
                        dve.wait_ge(sexp, 2 * f + 2)
                        sc = scores[f % 2]
                        seq(v.reciprocal(dri[:, 2 * f:2 * f + 2], den[:, 2 * f:2 * f + 2]))
                        seq(v.tensor_scalar(sc[:, 0:P], sc[:, 0:P], dri[:, 2 * f:2 * f + 1], None, ALU.mult))
                        v.tensor_scalar(sc[:, P:3 * P], sc[:, P:3 * P], dri[:, 2 * f + 1:2 * f + 2], None, ALU.mult).then_inc(sdiv, 1)
            for j in range(2):
                for n in range(NT):
                    nm = f"yf.{j}.{n}"
                    wait_filled(dve, nm)
                    close(v.tensor_tensor(mixf[:, n, WT * j:WT * j + WT], ps(nm)[:, :], merge[:, n, D + WT * j:D + WT * j + WT], ALU.mult), nm)
                    wait_drained(dve, nm)
                    wait_drained(dve, f"ya.{j}.{n}")
                    m = mix[:, n, WT * j:WT * j + WT]
                    v.tensor_tensor(m, m, mixf[:, n, WT * j:WT * j + WT], ALU.add).then_inc(mixed, 1)
            for j in range(2):
                for n in range(NT):
                    nm = f"wo.{j}.{n}"
                    wait_filled(dve, nm)
                    hv = h[:, n, WT * j:WT * j + WT]
                    close(v.tensor_tensor(hv, hv, ps(nm)[:, :], ALU.add), nm)
                    wait_drained(dve, nm)
                    v.memset(stat[:, 990 + 2 * j + n:991 + 2 * j + n], 0.0).then_inc(h_ready, 1)

            def norm_perm(k):
                for n in range(NT):
                    dve.wait_ge(rinv_made, NT * k + n + 1)
                    v.tensor_scalar(hn[:, n, :].rearrange("p (c q) -> p c q", c=KC), h[:, n, :].rearrange("p (q c) -> p c q", c=KC),
                                    rinv_x[k][:, n:n + 1], None, ALU.mult).then_inc(xn_ready, 1)

            norm_perm(1)
            for n in range(NT):
                for j in range(2):
                    nm = f"hT.{n}.{j}"
                    wait_filled(dve, nm)
                    close(v.tensor_tensor(actT[:, 4 * j:4 * j + 4, n * P:n * P + P], blocks4(nm), bc(cols[:, R_NFFN + 4 * j:R_NFFN + 4 * j + 4], 2, P), ALU.mult), nm)
            wait_drained(dve, "router")
            for n in range(NT):
                seq(v.tensor_tensor(sel[:, n, :], sg[:, n, :], rbias[:, :], ALU.add))
                seq(v.max(top[:, n, :], sel[:, n, :]))
                seq(v.match_replace(out=gates[:, n, :], in_to_replace=top[:, n, :], in_values=sel[:, n, :], imm_value=-1e30))
                seq(v.tensor_tensor(gates[:, n, :], gates[:, n, :], sel[:, n, :], ALU.not_equal))
                seq(v.tensor_tensor(gates[:, n, :], gates[:, n, :], sg[:, n, :], ALU.mult))
                seq(v.tensor_reduce(gsum[:, n, 0:1], gates[:, n, :], AX.X, ALU.add))
                seq(v.reciprocal(gsum[:, n, 1:2], gsum[:, n, 0:1]))
                v.tensor_scalar(gates[:, n, :], gates[:, n, :], gsum[:, n, 1:2], ROUTED_SCALE, ALU.mult, ALU.mult).then_inc(gates_ready, 1)
            for n in range(NT):
                dve.wait_ge(erinv, n + 1)
                seq(v.tensor_scalar(e_t[:, n, :], e_t[:, n, :], e_ri[:, n:n + 1], None, ALU.mult))
                v.tensor_tensor(e_t[:, n, :], e_t[:, n, :], plen, ALU.mult).then_inc(e_ready, 1)
            dve.wait_ge(gates_ready, NT)

            def expert(i, gate):
                for n in range(NT):
                    dve.wait_ge(gu_silu, i + n + 1)
                    up = bank[4 + n][:, DE:2 * DE].rearrange("p (q c) -> p c q", c=2)
                    s2 = sil[n].rearrange("p (q c) -> p c q", c=2)
                    dst = hid[n].rearrange("p (c q) -> p c q", c=2)
                    if gate is None:
                        v.tensor_tensor(dst, s2, up, ALU.mult).then_inc(hid_ready, 1)
                    else:
                        v.scalar_tensor_tensor(out=dst, in0=s2, scalar=gate(n), in1=up, op0=ALU.mult, op1=ALU.mult).then_inc(hid_ready, 1)

            expert(0, None)
            with dve.Fori(0, NE) as e:
                expert(e * 2 + 2, lambda n: gates[:, n, bass.ds(e, 1)])
            dve.wait_ge(down_done, NE + 1)
            for n in range(NT):
                for j in range(2):
                    hv = h[:, n, WT * j:WT * j + WT]
                    v.tensor_tensor(hv, hv, bank[2 * n + j][:, :], ALU.add).then_inc(h_ready, 1)
            dve.wait_ge(h_ready, 8)
            norm(2, hn)
            for n in range(NT):
                for j in range(2):
                    dve.wait_ge(hidT_filled, 2 * (NE + 1) + 2 * n + j + 1)
                    src = bank[2 * n + j][:, :].rearrange("p (a b) -> p a b", a=4)
                    v.tensor_tensor(actT[:, 4 * j:4 * j + 4, n * P:n * P + P], src, bc(cols[:, R_NPG + 4 * j:R_NPG + 4 * j + 4], 2, P), ALU.mult).then_inc(e_ready, 1)
            for n in range(NT):
                dve.wait_ge(sg_ready, NT + n + 1)
                seq(v.tensor_tensor(gt[:, n, :], gt[:, n, :], e_t[:, n, :], ALU.mult))
                v.tensor_tensor(gt[:, n, :], gt[:, n, :], h[:, n, :], ALU.add).then_inc(out_ready, 1)


_INS = ['x', 'p', 'norm_mix', 'w_in', 'conv_w', 'a_log', 'dt_bias', 'gdn_norm', 'fox_f_bias', 'q_norm', 'k_norm',
        'w_branch_gdn', 'w_branch_fox', 'w_out', 'norm_ffn', 'w_router', 'router_bias', 'we_gate', 'we_up', 'we_down',
        'ws_gate', 'ws_up', 'ws_down', 'w_ple', 'ple_norm', 'ple_gate_norm', 'w_ple_gate']


def kernel(**inputs):
    import numpy as np
    import concourse.bacc as bacc
    from concourse.bass_utils import run_bass_kernel_spmd

    nc = bacc.Bacc("TRN2", target_bir_lowering=False, num_devices=1)
    arrays, args = {}, []
    for name in _INS:
        a = np.ascontiguousarray(inputs[name])
        arrays[f"in_{name}"] = a
        args.append(nc.dram_tensor(f"in_{name}", a.shape, mybir.dt.from_np(a.dtype), kind="ExternalInput").ap())
    res = nc.dram_tensor("out_0", (1, S, D), F32, kind="ExternalOutput").ap()
    program(nc, *args, res)
    r = run_bass_kernel_spmd(nc, [arrays], core_ids=[0])
    return r.results[0]["out_0"]
```

```python
from contextlib import ExitStack

import concourse.bass as bass
from concourse import mybir

P = 128
F32 = mybir.dt.float32
BF16 = mybir.dt.bfloat16
ALU = mybir.AluOpType
ACT = mybir.ActivationFunctionType
AX = mybir.AxisListType

S, D = 256, 1024
NT = S // P
KC = D // P
GH, DK = 8, 128
FH, FD = 16, 64
NE, TOPK, DE = 64, 8, 256
ROUTED_SCALE = 2.5
EPS = 1e-6
LEVELS = 7
MASKED = -1e30

C_QKV, C_Z, C_AB, C_FOX, C_F, C_MERGE = 0, 3072, 4096, 4112, 7184, 7200
WT = 512
A_SLOTS = 3
CAP = 64
PAIRS = NE // 2
EW = KC * DE
PAIR_WORDS = 6 * EW
LOOKAHEAD = 4

R_CONV, R_NMIX, R_NFFN, R_NPG, R_GDN, R_QN, R_KN, R_ALL = 0, 96, 104, 112, 120, 121, 122, 123


def bc(ap, axis, n):
    v = ap.unsqueeze(axis)
    shape = list(v.shape)
    shape[axis] = n
    return v.to_broadcast(shape)


def bank_fills():
    f = ["cols"]
    f += [f"xT.{n}.{j}" for n in range(NT) for j in range(2)]
    f += [f"qkv.{c}" for c in range(12)]
    f += ["small"]
    f += [f"z.{j}.{n}" for j in range(2) for n in range(NT)]
    f += ["cum", "gbT"]
    f += [f"tq.{n}.{j}" for j in range(6) for n in range(NT)]
    f += [f"fox.{j}.{n}" for j in range(6) for n in range(NT)]
    f += [f"tk.{n}.{j}" for n in range(NT) for j in range(4)]
    f += [f"gb.{j}" for j in range(4)] + [f"bb.{j}" for j in range(4)]
    for j in range(4):
        f += [f"kk.{j}", f"qk.{j}"]
    for lv in range(LEVELS):
        f += [f"P.{lv}.{j}" for j in range(4)]
        if lv > 0:
            for j in range(4):
                f += ([f"X.{lv}.{j}"] if lv < LEVELS - 1 else []) + [f"V.{lv}.{j}"]
    for j in range(2):
        f += [f"tg.{j}", f"wT.{j}", f"u0.{j}"]
    for j in range(2):
        f += [f"o0.{j}", f"s1.{j}"]
    for j in range(2):
        f += [f"u1.{j}"]
    for j in range(2):
        f += [f"o1.{j}"]
    f += [f"merge.{j}.{n}" for j in range(4) for n in range(NT)]
    f += [f"oT.{n}.{j}" for n in range(NT) for j in range(2)]
    f += [f"fT.{n}.{j}" for n in range(NT) for j in range(4)]
    f += ["cT"] + [f"cb.{j}" for j in range(8)]
    f += [f"ya.{j}.{n}" for j in range(2) for n in range(NT)]
    for g in range(9):
        if g < 8:
            f += [f"s.{2 * g}", f"s.{2 * g + 1}"]
        if g > 0:
            f += [f"pT.{2 * g - 2}", f"pT.{2 * g - 1}", f"pv.{g - 1}"]
    f += [f"yf.{j}.{n}" for j in range(2) for n in range(NT)]
    f += [f"mT.{n}.{j}" for n in range(NT) for j in range(2)]
    f += [f"wo.{j}.{n}" for j in range(2) for n in range(NT)]
    f += [f"hT.{n}.{j}" for n in range(NT) for j in range(2)]
    f += ["router", "rank"]
    f += [f"pT2.{n}" for n in range(NT)]
    f += [f"e.{n}.{j}" for n in range(NT) for j in range(2)]
    return f


def program(nc, x, p, norm_mix, w_in, conv_w, a_log, dt_bias, gdn_norm, fox_f_bias, q_norm, k_norm,
            w_branch_gdn, w_branch_fox, w_out, norm_ffn, w_router, router_bias, we_gate, we_up, we_down,
            ws_gate, ws_up, ws_down, w_ple, ple_norm, ple_gate_norm, w_ple_gate, out):
    ctx = ExitStack()
    with ctx:
        def sb(name, shape, dt=F32):
            return ctx.enter_context(nc.sbuf_tensor(name, shape, dt))

        def sem(name):
            return ctx.enter_context(nc.semaphore(name))

        bank = [ctx.enter_context(nc.psum_tensor(f"bank{i}", [P, 512], F32)) for i in range(8)]

        h = sb("h", [P, NT, D])
        actT = sb("actT", [P, KC, S])
        ident = sb("ident", [P, P])
        ones = sb("ones", [P, P])
        tri = sb("tri", [P, P])
        stri = sb("stri", [P, P])
        negm = sb("negm", [P, P])
        lmask = sb("lmask", [P, LEVELS, P], BF16)
        nhalf = sb("nhalf", [P, 32])
        cols = sb("cols", [P, P])
        bias3 = sb("bias3", [P, 32])
        nega = sb("nega", [P, GH])
        rbias = sb("rbias", [P, NE])
        NX = NE + LOOKAHEAD
        posx = sb("posx", [P, NT, NX])
        gparts = sb("gparts", [P, NT, NX, 3], BF16)
        iota = sb("iota", [P, CAP])
        onehot = sb("onehot", [P, NT, 2 * CAP], BF16)
        identb = sb("identb", [P, P], BF16)
        passes = sb("passes", [P, 2], mybir.dt.int32)
        gslot = sb("gslot", [P, 1])
        wsm = sb("wsm", [P, KC, 32])
        wrt = sb("wrt", [P, KC, NE])

        stat_used = [0]
        stat = sb("stat", [P, 1000])

        def stats(n):
            lo = stat_used[0]
            stat_used[0] += n
            assert stat_used[0] <= 1000
            return stat[:, lo:lo + n]

        A_WORDS = 45056
        arena = sb("arena", [P, A_WORDS])

        def at(lo, n):
            assert lo + n <= A_WORDS
            return arena[:, lo:lo + n]

        wring = [at(i * KC * WT, KC * WT).rearrange("p (c n) -> p c n", c=KC) for i in range(A_SLOTS)]
        R1 = A_SLOTS * KC * WT
        R2, RZ, RF = R1 + 6144, R1 + 12288, R1 + 14336
        TDT = RF + 6144
        TLT, TMT, TX, TV, TPB = (TDT + 2048 * i for i in range(1, 6))

        def prob(lo, n=16):
            return at(lo, n * P).rearrange("p (b t) -> p b t", b=n)

        qkvT = prob(R1, 48).rearrange("p (c n) t -> p c (n t)", n=NT)
        qk = at(R2, 4096).rearrange("p (n c) -> p n c", n=NT)
        vbeta = prob(R2 + 4096)
        zs = at(RZ, 2048).rearrange("p (n c) -> p n c", n=NT)
        fox = at(RF, 6144).rearrange("p (n c) -> p n c", n=NT)
        dT, lT, mT, xi, vi, pb = (prob(t) for t in (TDT, TLT, TMT, TX, TV, TPB))
        rows = at(TMT, P)
        xn = at(TPB, 2048).rearrange("p (n c) -> p n c", n=NT)
        sq = at(TMT, 2048)
        gd, bd = prob(TX), prob(TV)
        blocks = prob(TV, 8)
        kbe = prob(TLT, 8)
        s1 = prob(TLT + 1024, 8)
        qgT, wTn = prob(TX, 8), prob(TX + 1024, 8)
        u0, u1 = prob(TPB, 8), prob(TPB + 1024, 8)
        oa = at(TMT, 2048).rearrange("p (n c) -> p n c", n=NT)
        oT = at(R2 + 4096, 2048).rearrange("p (c t) -> p c t", c=KC)
        merge = at(R2, 4096).rearrange("p (n c) -> p n c", n=NT)
        foxT = at(R1, 4096).rearrange("p (c t) -> p c t", c=16)
        scores = [at(R1 + 4096 + 384 * i, 384) for i in range(2)]
        probsT = [at(R1 + 4096 + 768 + 384 * i, 384) for i in range(2)]
        cbm = at(TDT, 6144).rearrange("p (f k) -> p f k", f=FH)
        cd = at(TX, 4096).rearrange("p (f k) -> p f k", f=FH)
        ofT = at(RZ, 2048).rearrange("p (c t) -> p c t", c=KC)
        mix = at(TX, 2048).rearrange("p (n c) -> p n c", n=NT)
        mixf = at(TV, 2048).rearrange("p (n c) -> p n c", n=NT)
        mixT = at(TPB, 2048).rearrange("p (c t) -> p c t", c=KC)

        pair_at = [PAIR_WORDS, 0]
        ering = [at(lo, PAIR_WORDS) for lo in pair_at]
        gu_in = [r[:, 0:4 * EW].rearrange("p (m e w) -> p m e w", m=2, e=2) for r in ering]
        d_in = [r[:, 4 * EW:6 * EW].rearrange("p (e w) -> p e w", e=2) for r in ering]
        B0 = 2 * PAIR_WORDS
        hparts = at(B0, 3072).bitcast(BF16).rearrange("p (k n c) -> p k n c", k=3, n=NT)
        e_t = at(B0 + 3072, 2048).rearrange("p (n c) -> p n c", n=NT)
        ngain = at(B0 + 3072, D)
        xg = at(B0 + 5120, D).rearrange("p (c s) -> p c s", c=KC)
        y = at(B0 + 6144, D)
        wple = at(B0 + 5120, 2048).rearrange("p (c d) -> p c d", c=2)
        spread = [at(B0 + 7168 + 256 * i, 256).rearrange("p (n t) -> p n t", n=NT) for i in range(2)]
        p_t = at(B0 + 7168, 512).rearrange("p (n c) -> p n c", n=NT)
        hid, sil = at(B0 + 7680, 256), at(B0 + 7936, 256)
        hidT = at(B0 + 8192, 256).rearrange("p (c t) -> p c t", c=2)
        hn = at(B0 + 8448, 2048).rearrange("p (n c) -> p n c", n=NT)
        gt = hn
        WPG = B0 + 10496
        wpg = [at(WPG + i * KC * WT, KC * WT).rearrange("p (c n) -> p c n", c=KC) for i in range(2)]
        sgw = at(WPG, EW).rearrange("p (c f) -> p c f", c=KC)
        suw = at(WPG + EW, EW).rearrange("p (c f) -> p c f", c=KC)
        sdw = at(WPG + 2 * EW, EW).rearrange("p (c d) -> p c d", c=2)
        shid = [at(WPG + 3 * EW + 256 * i, 256) for i in range(2)]
        ssil = [at(WPG + 3 * EW + 512 + 256 * i, 256) for i in range(2)]
        shidT = [at(WPG + 3 * EW + 1024 + 256 * i, 256).rearrange("p (c t) -> p c t", c=2) for i in range(2)]
        pT = at(WPG + 8192, 512).rearrange("p (c t) -> p c t", c=2)
        plen = at(WPG + 8704, 1024)

        x_loaded, rows_loaded, bias_loaded, small_loaded = (sem(s) for s in ("x_loaded", "rows_loaded", "bias_loaded", "small_loaded"))
        w_loaded = [sem(f"w_loaded{i}") for i in range(A_SLOTS)]
        consts = sem("consts")
        masks_made = sem("masks_made")
        filled = [sem(f"filled{i}") for i in range(8)]
        drained = [sem(f"drained{i}") for i in range(8)]
        dve_step, act_step, pool_step = sem("dve_step"), sem("act_step"), sem("pool_step")
        sumsq = sem("sumsq")
        rinv_made = sem("rinv_made")
        xn_ready = sem("xn_ready")
        conv_done = sem("conv_done")
        soft = sem("soft")
        beta_ready = sem("beta_ready")
        logs_ready = sem("logs_ready")
        gstat = sem("gstat")
        geg = sem("geg")
        gd_made, bd_made, cd_made = sem("gd_made"), sem("bd_made"), sem("cd_made")
        qkss, qkrinv, qk_normed = sem("qkss"), sem("qkrinv"), sem("qk_normed")
        d_ready, dexp_ready = sem("d_ready"), sem("dexp_ready")
        d_masked = sem("d_masked")
        m_ready = sem("m_ready")
        scaled = sem("scaled")
        oss, orinv, o_normed = sem("oss"), sem("orinv"), sem("o_normed")
        fss, frinv, f_normed = sem("fss"), sem("frinv"), sem("f_normed")
        smax, sexp, sdiv = sem("smax"), sem("sexp"), sem("sdiv")
        mixed = sem("mixed")
        h_ready = sem("h_ready")
        sig_ready = sem("sig_ready")
        gates_ready = sem("gates_ready")
        p_loaded = sem("p_loaded")
        ess, erinv, e_ready = sem("ess"), sem("erinv"), sem("e_ready")
        shared_loaded, ngain_loaded = sem("shared_loaded"), sem("ngain_loaded")
        gu_loaded = [sem(f"gu_loaded{i}") for i in range(2)]
        d_loaded = [sem(f"d_loaded{i}") for i in range(2)]
        gu_filled, gu_silu, hid_ready = sem("gu_filled"), sem("gu_silu"), sem("hid_ready")
        hidT_filled, hidT_ready, shared_done = sem("hidT_filled"), sem("hidT_ready"), sem("shared_done")
        parts_ready = sem("parts_ready")
        passes_ready = sem("passes_ready")
        onehot_ready = sem("onehot_ready")
        xa_filled, xb_filled = sem("xa_filled"), sem("xb_filled")
        xa_ready, xb_ready = sem("xa_ready"), sem("xb_ready")
        place_filled, place_ready = sem("place_filled"), sem("place_ready")
        pgu_filled, psilu, phid_ready = sem("pgu_filled"), sem("psilu"), sem("phid_ready")
        phidT_filled, phidT_ready = sem("phidT_filled"), sem("phidT_ready")
        y_filled = [sem("y0_filled"), sem("y1_filled")]
        y_ready = [sem("y0_ready"), sem("y1_ready")]
        spread_made, place_half, onehot_half, iota_moved = (sem(q) for q in ("spread_made", "place_half", "onehot_half", "iota_moved"))
        added = sem("added")
        wpg_loaded = sem("wpg_loaded")
        sg_ready, out_ready, out_stored = sem("sg_ready"), sem("out_ready"), sem("out_stored")
        pg_filled = sem("pg_filled")

        fills = bank_fills()
        place = {name: (i % 8, i // 8) for i, name in enumerate(fills)}

        def ps(name):
            return bank[place[name][0]]

        def wait_filled(eng, name):
            b, turn = place[name]
            eng.wait_ge(filled[b], turn + 1)

        def wait_drained(eng, name):
            b, turn = place[name]
            eng.wait_ge(drained[b], turn + 1)

        w_in2, = (w_in[0],)
        wtiles = [(w_in2, C_QKV + WT * t, f"qkv.{2 * t + 1}") for t in range(6)]
        wtiles += [(w_in2, C_Z + WT * j, f"z.{j}.1") for j in range(2)]
        wtiles += [(w_in2, C_FOX + WT * j, f"fox.{j}.1") for j in range(6)]
        wtiles += [(w_in2, C_MERGE + WT * j, f"merge.{j}.1") for j in range(4)]
        wtiles += [(w_branch_gdn[0], WT * j, f"ya.{j}.1") for j in range(2)]
        wtiles += [(w_branch_fox[0], WT * j, f"yf.{j}.1") for j in range(2)]
        wtiles += [(w_out[0], WT * j, f"wo.{j}.1") for j in range(2)]
        W_QKV, W_Z, W_FOX, W_MERGE, W_YA, W_YF, W_WO = 0, 6, 8, 14, 18, 20, 22

        block = ctx.enter_context(nc.Block())

        ss_x = [stats(NT) for _ in range(3)]
        rinv_x = [stats(NT) for _ in range(3)]
        u_s = stats(64).rearrange("p (n c) -> p n c", n=NT)
        l_s = stats(64).rearrange("p (n c) -> p n c", n=NT)
        t_s = stats(64).rearrange("p (n c) -> p n c", n=NT)
        beta = stats(16).rearrange("p (n c) -> p n c", n=NT)
        la = stats(48).rearrange("p (n c) -> p n c", n=NT)
        cs = stats(96)
        gb = stats(32)
        gtail = stats(16)
        eg_s = stats(16)
        et_s = stats(16)
        be_s = stats(16)
        cf = stats(32).rearrange("p (n c) -> p n c", n=NT)
        gbT = stats(256)
        qk_ss = stats(32).rearrange("p (n c) -> p n c", n=NT)
        qk_ri = stats(32).rearrange("p (n c) -> p n c", n=NT)
        cT = gbT
        mx = stats(64)
        o_ss, o_ri = stats(16), stats(16)
        f_ss = sb("f_ss", [P, NT, 32])
        f_ri = sb("f_ri", [P, NT, 32])
        den = sb("den", [P, 32])
        dri = sb("dri", [P, 32])
        smallw = wsm[:, :, :].rearrange("p c n -> p (c n)")
        sg = smallw[:, 0:NT * NE].rearrange("p (n e) -> p n e", n=NT)
        sel = smallw[:, NT * NE:2 * NT * NE].rearrange("p (n e) -> p n e", n=NT)
        gates = gbT[:, 0:NT * NE].rearrange("p (n e) -> p n e", n=NT)
        chosen = gbT[:, NT * NE:2 * NT * NE].rearrange("p (n e) -> p n e", n=NT)
        top = sb("top", [P, NT, 8])
        gsum = sb("gsum", [P, NT, 2])
        e_ss, e_ri = sb("e_ss", [P, NT]), sb("e_ri", [P, NT])

        @block.sync
        def _(sp):
            sp.dma_start(h[:, :, :], x[0].rearrange("(n p) d -> p n d", p=P)).then_inc(x_loaded, 16)
            rv = rows
            sp.dma_start(rv[R_CONV:R_NMIX, :], conv_w[0].rearrange("i (c q) -> (i c) q", q=P)).then_inc(rows_loaded, 16)
            for r, v in ((R_NMIX, norm_mix), (R_NPG, ple_gate_norm)):
                sp.dma_start(rv[r:r + 8, :], v.rearrange("a (c q) -> (a c) q", q=P)).then_inc(rows_loaded, 16)
            with nc.allow_non_contiguous_dma(reason="4 KB in all"):
                sp.dma_start(rv[R_NFFN:R_NFFN + 8, :], norm_ffn.rearrange("a (q c) -> (a c) q", q=P)).then_inc(rows_loaded, 16)
            sp.dma_start(rv[R_GDN:R_GDN + 1, :], gdn_norm).then_inc(rows_loaded, 16)
            for r, v in ((R_QN, q_norm), (R_KN, k_norm)):
                for half in range(2):
                    sp.dma_start(rv[r:r + 1, FD * half:FD * half + FD], v).then_inc(rows_loaded, 16)

            def load(t):
                src, c0, _ = wtiles[t]
                if t >= A_SLOTS:
                    wait_filled(sp, wtiles[t - A_SLOTS][2])
                sp.dma_start(wring[t % A_SLOTS], src.rearrange("(c q) n -> q c n", q=P)[:, :, c0:c0 + WT]).then_inc(w_loaded[t % A_SLOTS], 16)

            for t in range(3):
                load(t)
            sp.dma_start(bias3[:, 0:8], dt_bias.to_broadcast([P, 8])).then_inc(bias_loaded, 16)
            sp.dma_start(bias3[:, 16:32], fox_f_bias.to_broadcast([P, 16])).then_inc(bias_loaded, 16)
            sp.dma_start(nega[:, :], a_log.to_broadcast([P, 8])).then_inc(bias_loaded, 16)
            sp.dma_start(rbias[:, :], router_bias.to_broadcast([P, NE])).then_inc(bias_loaded, 16)
            wv = w_in2.rearrange("(c q) n -> q c n", q=P)
            sp.dma_start(wsm[:, :, 0:16], wv[:, :, C_AB:C_AB + 16]).then_inc(small_loaded, 16)
            sp.dma_start(wsm[:, :, 16:32], wv[:, :, C_F:C_F + 16]).then_inc(small_loaded, 16)
            sp.dma_start(wrt[:, :, :], w_router[0].rearrange("(q c) n -> q c n", q=P)).then_inc(small_loaded, 16)
            for t in range(3, len(wtiles)):
                load(t)

            for g in range(8):
                wait_drained(sp, f"pv.{g}")
            sp.dma_start(ngain, norm_ffn.to_broadcast([P, D])).then_inc(ngain_loaded, 16)

            def load_pair(s, pick, gu_free=None, d_free=None):
                if gu_free is not None:
                    sp.wait_ge(pgu_filled, gu_free)
                for m, w in enumerate((we_gate, we_up)):
                    sp.dma_start(gu_in[s][:, m], w[0, pick].rearrange("e (q c) f -> q e (c f)", c=KC)).then_inc(gu_loaded[s], 16)
                if d_free is not None:
                    sp.wait_ge(y_filled[1], d_free)
                sp.dma_start(d_in[s], we_down[0, pick].rearrange("e (q c) d -> q e (c d)", c=2)).then_inc(d_loaded[s], 16)

            for j in range(2):
                for n in range(NT):
                    wait_drained(sp, f"yf.{j}.{n}")
            load_pair(0, slice(0, 2))
            for n in range(NT):
                wait_drained(sp, f"mT.{n}.1")
            sp.dma_start(sgw, ws_gate[0].rearrange("(q c) f -> q c f", c=KC)).then_inc(shared_loaded, 16)
            sp.dma_start(suw, ws_up[0].rearrange("(q c) f -> q c f", c=KC)).then_inc(shared_loaded, 16)
            sp.dma_start(sdw, ws_down[0].rearrange("(q c) d -> q c d", c=2)).then_inc(shared_loaded, 16)
            sp.dma_start(p_t, p[0, 0].rearrange("(n q) c -> q n c", q=P)).then_inc(p_loaded, 16)
            sp.dma_start(wple, w_ple[0].rearrange("(c q) d -> q c d", q=P)).then_inc(p_loaded, 16)
            wait_filled(sp, "wo.1.0")
            wait_filled(sp, "wo.1.1")
            sp.dma_start(plen, ple_norm.to_broadcast([P, D])).then_inc(p_loaded, 16)
            load_pair(1, slice(2, 4))
            with sp.Fori(0, PAIRS // 2 - 1) as k:
                for s in range(2):
                    load_pair(s, bass.ds(k * 4 + (4 + 2 * s), 2), k * 2 + (s + 1), k * 2 + (s + 1))
            sp.wait_ge(passes_ready, 1)
            np_sp = sp.value_load(passes[0:1, 0:1], min_val=1, max_val=S // CAP)
            with sp.If(np_sp > 1):
                with sp.Fori(1, np_sp) as r:
                    with sp.Fori(0, PAIRS // 2) as k:
                        for s in range(2):
                            free = r * PAIRS + k * 2 + (s - 1)
                            load_pair(s, bass.ds(k * 4 + 2 * s, 2), free, free)
            for n in range(NT):
                sp.wait_ge(out_ready, n + 1)
                sp.dma_start(out[0, n * P:(n + 1) * P, :], gt[:, n, :]).then_inc(out_stored, 16)
            sp.wait_ge(out_stored, 32)

        @block.gpsimd
        def _(pool):
            g = nc.gpsimd
            steps = [0]

            def seq(ins):
                steps[0] += 1
                ins.then_inc(pool_step, 1)
                pool.wait_ge(pool_step, steps[0])

            def select(t, src, op, fill, base, pattern, mult):
                return g.affine_select(out=t, in_=src, compare_op=op, fill=fill, base=base, pattern=pattern, channel_multiplier=mult)

            g.memset(ident[:, :], 0.0).then_inc(pool_step, 1)
            g.memset(ones[:, :], 1.0).then_inc(pool_step, 1)
            g.memset(nhalf[:, :], -0.5).then_inc(pool_step, 1)
            g.memset(bias3[:, 8:16], 0.0).then_inc(pool_step, 1)
            g.memset(negm[:, :], 0.0).then_inc(pool_step, 1)
            steps[0] = 5
            pool.wait_ge(pool_step, 5)
            select(ident[:, :], ident[:, :], ALU.not_equal, 1.0, 0, [[-1, P]], 1).then_inc(consts, 1)
            g.iota(iota[:, :], [[1, CAP]], base=0, channel_multiplier=0, allow_small_or_imprecise_dtypes=True).then_inc(consts, 1)
            pool.wait_ge(consts, 1)

            def roots(k):
                for n in range(NT):
                    pool.wait_ge(sumsq, NT * k + n + 1)
                    seq(g.tensor_scalar(rinv_x[k][:, n:n + 1], ss_x[k][:, n:n + 1], 1.0 / D, EPS, ALU.mult, ALU.add))
                    g.tensor_tensor(rinv_x[k][:, n:n + 1], rinv_x[k][:, n:n + 1], nhalf[:, 0:1], ALU.pow).then_inc(rinv_made, 1)
            roots(0)
            g.tensor_copy(identb[:, :], ident[:, :]).then_inc(consts, 1)
            select(tri[:, :], ones[:, :], ALU.is_ge, 0.0, 0, [[1, P]], -1).then_inc(consts, 1)
            select(stri[:, :], ones[:, :], ALU.is_gt, 0.0, 0, [[1, P]], -1).then_inc(consts, 1)
            select(negm[:, :], negm[:, :], ALU.is_ge, MASKED, 0, [[-1, P]], 1).then_inc(consts, 1)
            for lv in range(LEVELS + 1):
                b = 1 << lv
                nb = P // b
                v = blocks[:, lv, :].rearrange("p (k w) -> p k w", w=b)
                seq(select(v, ones[:, :].rearrange("p (k w) -> p k w", w=b), ALU.is_ge, 0.0, 0, [[-b, nb], [0, b]], 1)) if lv < LEVELS else seq(g.tensor_copy(blocks[:, lv, :], ones[:, :]))
                if lv < LEVELS:
                    seq(select(v, v, ALU.is_ge, 0.0, b - 1, [[b, nb], [0, b]], -1))
            for lv in range(LEVELS):
                g.tensor_tensor(lmask[:, lv, :], blocks[:, lv + 1, :], blocks[:, lv, :], ALU.subtract).then_inc(masks_made, 1)
            wait_drained(pool, "gbT")
            pool.wait_ge(masks_made, LEVELS)
            for j in range(4):
                for n in range(NT):
                    i = NT * j + n
                    pool.wait_ge(qkss, i + 1)
                    v = qk_ri[:, n, 4 * j:4 * j + 4]
                    seq(g.tensor_scalar(v, qk_ss[:, n, 4 * j:4 * j + 4], 1.0, EPS, ALU.mult, ALU.add))
                    ins = g.tensor_tensor(v, v, nhalf[:, 0:4], ALU.pow)
                    if j < 2:
                        seq(ins)
                        ins = g.tensor_scalar(v, v, DK ** -0.5, 0.0, ALU.mult, ALU.add)
                    ins.then_inc(qkrinv, 1)
            for t, lo, s in ((gd, 0, gd_made), (bd, P, bd_made)):
                src = bc(gbT[0:16, lo:lo + P], 1, 16)
                select(t[0:16], src, ALU.is_equal, 0.0, 0, [[-1, 16], [0, P]], 1).then_inc(s, 1)
            for n in range(NT):
                pool.wait_ge(fss, n + 1)
                seq(g.tensor_scalar(f_ri[:, n, :], f_ss[:, n, :], 1.0 / FD, EPS, ALU.mult, ALU.add))
                g.tensor_tensor(f_ri[:, n, :], f_ri[:, n, :], nhalf[:, :], ALU.pow).then_inc(frinv, 1)
            pool.wait_ge(oss, 1)
            seq(g.tensor_scalar(o_ri, o_ss, 1.0 / DK, EPS, ALU.mult, ALU.add))
            g.tensor_tensor(o_ri, o_ri, nhalf[:, 0:16], ALU.pow).then_inc(orinv, 1)
            wait_drained(pool, "cT")
            for j in range(2):
                wait_filled(pool, f"o1.{j}")
            select(cd[0:16], bc(cT[0:16, :], 1, 16), ALU.is_equal, 0.0, 0, [[-1, 16], [0, S]], 1).then_inc(cd_made, 1)
            roots(1)
            for n in range(NT):
                pool.wait_ge(ess, n + 1)
                seq(g.tensor_scalar(e_ri[:, n:n + 1], e_ss[:, n:n + 1], 1.0 / D, EPS, ALU.mult, ALU.add))
                g.tensor_tensor(e_ri[:, n:n + 1], e_ri[:, n:n + 1], nhalf[:, 0:1], ALU.pow).then_inc(erinv, 1)
            roots(2)

        @block.scalar
        def _(act):
            a = nc.scalar
            steps = [0]

            def seq(ins):
                steps[0] += 1
                ins.then_inc(act_step, 1)
                act.wait_ge(act_step, steps[0])

            def squares(k, src, junk):
                for n in range(NT):
                    a.activation(junk[:, n, :], src[:, n, :], ACT.Square, accum_out=ss_x[k][:, n:n + 1]).then_inc(sumsq, 1)

            def drain(name, dst, func=ACT.Copy, cols_used=512, **kw):
                wait_filled(act, name)
                a.activation(dst, ps(name)[:, 0:cols_used] if len(dst.shape) == 2 else
                             ps(name)[:, 0:cols_used].rearrange("p (a b) -> p a b", a=dst.shape[1]), func, **kw).then_inc(drained[place[name][0]], 1)

            act.wait_ge(x_loaded, 16)
            squares(0, h, xn)
            for c in range(12):
                wait_drained(act, f"qkv.{c}")
                v = qkvT[:, 2 * c:2 * c + 2, :]
                a.activation(v, v, ACT.Silu).then_inc(conv_done, 1)
            for j in range(2):
                for n in range(NT):
                    drain(f"z.{j}.{n}", zs[:, n, WT * j:WT * j + WT], ACT.Silu)
            act.wait_ge(logs_ready, 1)
            seq(a.activation(t_s, t_s, ACT.Exp, scale=-1.0))
            a.activation(l_s, t_s, ACT.Ln, bias=1.0).then_inc(soft, 1)
            a.activation(beta, u_s[:, :, 8:16], ACT.Exp, scale=-1.0).then_inc(soft, 1)
            a.activation(nega[:, :], nega[:, :], ACT.Exp).then_inc(soft, 1)
            for j in range(4):
                for n in range(NT):
                    drain(f"tq.{n}.{j}", qk[:, n, WT * j:WT * j + WT])
            act.wait_ge(gstat, 1)
            a.activation(eg_s, gb[:, 0:16], ACT.Exp).then_inc(geg, 1)
            a.activation(et_s, gtail, ACT.Exp).then_inc(geg, 1)
            for j in range(6):
                for n in range(NT):
                    drain(f"fox.{j}.{n}", fox[:, n, WT * j:WT * j + WT])
            for n in range(NT):
                for j in range(4):
                    drain(f"tk.{n}.{j}", qkvT[:, 4 * j:4 * j + 4, n * P:n * P + P])
            for j in range(4):
                act.wait_ge(d_ready, j + 1)
                a.activation(dT[:, 4 * j:4 * j + 4, :], dT[:, 4 * j:4 * j + 4, :], ACT.Exp).then_inc(dexp_ready, 1)
            for lv in range(1, LEVELS):
                for j in range(4):
                    drain(f"P.{lv}.{j}", pb[:, 4 * j:4 * j + 4, :])
            for j in range(2):
                hs = slice(4 * j, 4 * j + 4)
                drain(f"tg.{j}", qgT[:, hs, :])
                drain(f"wT.{j}", wTn[:, hs, :], scale=-1.0)
                drain(f"u0.{j}", u0[:, hs, :])
            for j in range(2):
                drain(f"o0.{j}", oa[:, 0, WT * j:WT * j + WT])
                drain(f"s1.{j}", s1[:, 4 * j:4 * j + 4, :])
            for j in range(2):
                drain(f"u1.{j}", u1[:, 4 * j:4 * j + 4, :])
            for j in range(2):
                drain(f"o1.{j}", oa[:, 1, WT * j:WT * j + WT])
            for j in range(4):
                for n in range(NT):
                    drain(f"merge.{j}.{n}", merge[:, n, WT * j:WT * j + WT], ACT.Sigmoid)
            for n in range(NT):
                for j in range(2):
                    drain(f"oT.{n}.{j}", oT[:, 4 * j:4 * j + 4, n * P:n * P + P], scale=cols[:, R_GDN:R_GDN + 1])
            for n in range(NT):
                for j in range(4):
                    r = R_QN if j < 2 else R_KN
                    drain(f"fT.{n}.{j}", foxT[:, 4 * j:4 * j + 4, n * P:n * P + P], scale=cols[:, r:r + 1])
            for g in range(9):
                if g < 8:
                    for f in (2 * g, 2 * g + 1):
                        act.wait_ge(smax, 2 * f + 2)
                        for n in range(NT):
                            v = scores[f % 2][:, P:3 * P] if n else scores[f % 2][:, 0:P]
                            a.activation(v, v, ACT.Exp, bias=mx[:, 2 * f + n:2 * f + n + 1], accum_out=den[:, 2 * f + n:2 * f + n + 1]).then_inc(sexp, 1)
                if g > 0:
                    for f in (2 * g - 2, 2 * g - 1):
                        drain(f"pT.{f}", probsT[f % 2], cols_used=384)
                    drain(f"pv.{g - 1}", ofT[:, g - 1, :], cols_used=S)
            for n in range(NT):
                for j in range(2):
                    drain(f"mT.{n}.{j}", mixT[:, 4 * j:4 * j + 4, n * P:n * P + P])
            act.wait_ge(h_ready, 4)
            squares(1, h, hn)
            for n in range(NT):
                act.wait_ge(xn_ready, NT + n + 1)
                a.activation(hparts[:, 0, n, :], hn[:, n, :], ACT.Copy).then_inc(parts_ready, 1)
            for n in range(NT):
                for j in range(2):
                    drain(f"hT.{n}.{j}", actT[:, 4 * j:4 * j + 4, n * P:n * P + P])
            drain("router", sg[:, :, :], ACT.Sigmoid, cols_used=P)
            for n in range(NT):
                drain(f"pT2.{n}", pT[:, :, n * P:n * P + P], cols_used=S)
            for n in range(NT):
                for j in range(2):
                    drain(f"e.{n}.{j}", e_t[:, n, WT * j:WT * j + WT])
            act.wait_ge(parts_ready, 2 * NT + 1)
            for n in range(NT):
                for j in range(2):
                    wait_drained(act, f"e.{n}.{j}")
                a.activation(hn[:, n, :], e_t[:, n, :], ACT.Square, accum_out=e_ss[:, n:n + 1]).then_inc(ess, 1)
            for n in range(NT):
                act.wait_ge(gu_filled, n + 1)
                a.activation(ssil[n], bank[4 + n][:, 0:DE], ACT.Silu).then_inc(gu_silu, 1)
            for n in range(NT):
                act.wait_ge(hidT_filled, n + 1)
                a.activation(shidT[n], bank[6 + n][:, 0:DE].rearrange("p (c t) -> p c t", c=2), ACT.Copy).then_inc(hidT_ready, 1)
            act.wait_ge(shared_done, 1)
            act.wait_ge(e_ready, NT)
            for j in range(2):
                act.dma_start(wpg[j], w_ple_gate[0].rearrange("(c q) n -> q c n", q=P)[:, :, WT * j:WT * j + WT]).then_inc(wpg_loaded, 16)

            def gathered(t):
                act.wait_ge(xa_filled, t)
                a.activation(xg[:, 0:4, :], bank[5][:, :].rearrange("p (c s) -> p c s", c=4), ACT.Copy).then_inc(xa_ready, 1)

            gathered(1)
            act.wait_ge(passes_ready, 1)
            np_act = act.value_load(passes[0:1, 1:2], min_val=PAIRS // 2, max_val=PAIRS // 2 * (S // CAP))
            with act.Fori(0, np_act) as k:
                for s in range(2):
                    t = k * 2 + (s + 1)
                    act.wait_ge(pgu_filled, t)
                    a.activation(sil, bank[4][:, 0:DE], ACT.Silu).then_inc(psilu, 1)
                    act.wait_ge(phidT_filled, t)
                    a.activation(hidT, bank[7][:, 0:DE].rearrange("p (c t) -> p c t", c=2), ACT.Copy).then_inc(phidT_ready, 1)
                    gathered(k * 2 + (s + 2))
                    act.wait_ge(y_filled[0], t)
                    a.activation(y[:, 0:WT], bank[4][:, :], ACT.Copy).then_inc(y_ready[0], 1)
            act.wait_ge(h_ready, 8)
            squares(2, h, hn)
            for j in range(2):
                for n in range(NT):
                    act.wait_ge(pg_filled, NT * j + n + 1)
                    a.activation(gt[:, n, WT * j:WT * j + WT], bank[4 + NT * j + n][:, :], ACT.Sigmoid).then_inc(sg_ready, 1)

        @block.tensor
        def _(pe):
            t = nc.tensor

            def open_bank(name):
                b, turn = place[name]
                if turn > 0:
                    pe.wait_ge(drained[b], turn)
                return bank[b]

            def close(ins, name):
                ins.then_inc(filled[place[name][0]], 1)

            def transposes(name, srcs, rows_in=P):
                o = open_bank(name)
                for i, v in enumerate(srcs):
                    w = v.shape[1]
                    ins = t.transpose(o[0:w, i * P:i * P + rows_in], v, ident[0:rows_in, 0:rows_in])
                close(ins, name)

            def project(name, w, n, lhs=actT):
                o = open_bank(name)
                for c in range(KC):
                    ins = t.matmul(o[:, :], lhs[:, c, n * P:n * P + P], w[:, c, :], start=(c == 0), stop=(c == KC - 1))
                close(ins, name)

            def weights(k):
                pe.wait_ge(w_loaded[k % A_SLOTS], 16 * (k // A_SLOTS + 1))
                return wring[k % A_SLOTS]

            pe.wait_ge(consts, 1)
            pe.wait_ge(rows_loaded, 16 * 9)
            transposes("cols", [rows[0:R_ALL, :]], R_ALL)
            for n in range(NT):
                pe.wait_ge(xn_ready, n + 1)
                for j in range(2):
                    transposes(f"xT.{n}.{j}", [xn[:, n, P * c:P * c + P] for c in range(4 * j, 4 * j + 4)])
            for n in range(NT):
                for j in range(2):
                    wait_drained(pe, f"xT.{n}.{j}")
            for c2 in range(12):
                w = weights(W_QKV + c2 // 2)
                o = open_bank(f"qkv.{c2}")
                for i in range(2):
                    col = (2 * c2 + i) % 4 * P
                    for c in range(KC):
                        ins = t.matmul(o[:, i * S:i * S + S], w[:, c, col:col + P], actT[:, c, :], start=(c == 0), stop=(c == KC - 1))
                close(ins, f"qkv.{c2}")
            pe.wait_ge(small_loaded, 48)
            o = open_bank("small")
            for n in range(NT):
                for c in range(KC):
                    ins = t.matmul(o[:, 32 * n:32 * n + 32], actT[:, c, n * P:n * P + P], wsm[:, c, :], start=(c == 0), stop=(c == KC - 1))
            close(ins, "small")
            for j in range(2):
                w = weights(W_Z + j)
                for n in range(NT):
                    project(f"z.{j}.{n}", w, n)
            pe.wait_ge(logs_ready, 2)
            pe.wait_ge(consts, 6)
            o = open_bank("cum")
            for k, m in enumerate((tri, ones)):
                for n in range(NT):
                    lo = 48 * k + 24 * n
                    ins = t.matmul(o[:, lo:lo + 24], m[:, :], la[:, n, :], start=True, stop=True)
            close(ins, "cum")
            pe.wait_ge(gstat, 1)
            transposes("gbT", [gb[:, 0:16], gb[:, 16:32]])
            for j in range(6):
                pe.wait_ge(conv_done, 2 * j + 2)
                for n in range(NT):
                    transposes(f"tq.{n}.{j}", [qkvT[:, c, n * P:n * P + P] for c in range(4 * j, 4 * j + 4)])
            for j in range(6):
                w = weights(W_FOX + j)
                for n in range(NT):
                    project(f"fox.{j}.{n}", w, n)
            pe.wait_ge(qk_normed, 8)
            for n in range(NT):
                for j in range(4):
                    transposes(f"tk.{n}.{j}", [qk[:, n, P * c:P * c + P] for c in range(4 * j, 4 * j + 4)])
            for nm, src, s in (("gb", gd, gd_made), ("bb", bd, bd_made)):
                pe.wait_ge(s, 1)
                for j in range(4):
                    o = open_bank(f"{nm}.{j}")
                    close(t.matmul(o[:, :], ones[0:16, :], src[0:16, 4 * j:4 * j + 4, :], start=True, stop=True), f"{nm}.{j}")

            def problems(name, lhs, rhs, hs=range(4)):
                o = open_bank(name)
                for i, b in enumerate(hs):
                    ins = t.matmul(o[:, i * P:i * P + P], lhs(b), rhs(b), start=True, stop=True)
                close(ins, name)

            def qTb(b):
                return qkvT[:, b % GH, b // GH * P:b // GH * P + P]

            def kTb(b):
                return qkvT[:, GH + b % GH, b // GH * P:b // GH * P + P]

            for n in range(NT):
                for j in range(4):
                    wait_drained(pe, f"tk.{n}.{j}")
            for j in range(4):
                bs = range(4 * j, 4 * j + 4)
                problems(f"kk.{j}", kTb, kTb, bs)
                problems(f"qk.{j}", kTb, qTb, bs)
            for lv in range(LEVELS):
                for j in range(4):
                    bs = range(4 * j, 4 * j + 4)
                    pe.wait_ge(m_ready, 4 * lv + j + 1)
                    if lv > 1:
                        wait_drained(pe, f"X.{lv - 1}.{j}")
                    if lv == 1:
                        wait_drained(pe, f"P.0.{j}")
                    problems(f"P.{lv}.{j}", lambda b: mT[:, b, :], (lambda b: xi[:, b, :]) if lv else (lambda b: ident[:, :]), bs)
                if lv == 0:
                    continue
                for j in range(4):
                    bs = range(4 * j, 4 * j + 4)
                    wait_drained(pe, f"P.{lv}.{j}")
                    if lv > 1:
                        wait_drained(pe, f"V.{lv - 1}.{j}")
                    if lv < LEVELS - 1:
                        problems(f"X.{lv}.{j}", lambda b: vi[:, b, :], lambda b: pb[:, b, :], bs)
                    problems(f"V.{lv}.{j}", lambda b: pb[:, b, :], lambda b: vi[:, b, :], bs)
            for j in range(4):
                wait_drained(pe, f"V.{LEVELS - 1}.{j}")
            pe.wait_ge(scaled, 3)
            for j in range(2):
                hs = range(4 * j, 4 * j + 4)
                transposes(f"tg.{j}", [qk[:, 1, P * c:P * c + P] for c in hs])
                problems(f"wT.{j}", lambda b: kbe[:, b, :], lambda b: vi[:, GH + b, :], hs)
                problems(f"u0.{j}", lambda b: vi[:, b, :], lambda b: vbeta[:, b, :], hs)
            for j in range(2):
                hs = range(4 * j, 4 * j + 4)
                wait_drained(pe, f"u0.{j}")
                problems(f"o0.{j}", lambda b: dT[:, b, :], lambda b: u0[:, b, :], hs)
                problems(f"s1.{j}", lambda b: qk[:, 0, D + P * b:D + P * b + P], lambda b: u0[:, b, :], hs)

            def two(name, terms, hs):
                o = open_bank(name)
                for i, b in enumerate(hs):
                    for k, (lhs, rhs) in enumerate(terms):
                        ins = t.matmul(o[:, i * P:i * P + P], lhs(b), rhs(b), start=(k == 0), stop=(k == 1))
                close(ins, name)

            for j in range(2):
                wait_drained(pe, f"wT.{j}")
                wait_drained(pe, f"s1.{j}")
                two(f"u1.{j}", [(lambda b: vi[:, GH + b, :], lambda b: vbeta[:, GH + b, :]),
                                (lambda b: wTn[:, b, :], lambda b: s1[:, b, :])], range(4 * j, 4 * j + 4))
            for j in range(2):
                wait_drained(pe, f"tg.{j}")
                wait_drained(pe, f"u1.{j}")
                two(f"o1.{j}", [(lambda b: qgT[:, b, :], lambda b: s1[:, b, :]),
                                (lambda b: dT[:, GH + b, :], lambda b: u1[:, b, :])], range(4 * j, 4 * j + 4))
            for j in range(4):
                w = weights(W_MERGE + j)
                for n in range(NT):
                    project(f"merge.{j}.{n}", w, n)
            for n in range(NT):
                pe.wait_ge(o_normed, n + 1)
                for j in range(2):
                    transposes(f"oT.{n}.{j}", [oa[:, n, P * c:P * c + P] for c in range(4 * j, 4 * j + 4)])
            for n in range(NT):
                pe.wait_ge(f_normed, n + 1)
                for j in range(4):
                    transposes(f"fT.{n}.{j}", [fox[:, n, P * c:P * c + P] for c in range(4 * j, 4 * j + 4)])
            o = open_bank("cT")
            for n in range(NT):
                ins = t.transpose(o[0:16, n * P:n * P + P], cf[:, n, :], ident[:, :])
            close(ins, "cT")
            pe.wait_ge(cd_made, 1)
            for j in range(8):
                o = open_bank(f"cb.{j}")
                close(t.matmul(o[:, :], ones[0:16, :], cd[0:16, 2 * j:2 * j + 2, :], start=True, stop=True), f"cb.{j}")
            for n in range(NT):
                for j in range(2):
                    wait_drained(pe, f"oT.{n}.{j}")
            for j in range(2):
                w = weights(W_YA + j)
                for n in range(NT):
                    project(f"ya.{j}.{n}", w, n, oT)
            for n in range(NT):
                for j in range(4):
                    wait_drained(pe, f"fT.{n}.{j}")
            for g in range(9):
                if g < 8:
                    for i in range(2):
                        lo = FD * i
                        o = open_bank(f"s.{2 * g + i}")
                        t.matmul(o[:, 0:P], foxT[lo:lo + FD, g, 0:P], foxT[lo:lo + FD, 8 + g, 0:P], start=True, stop=True)
                        close(t.matmul(o[:, P:P + S], foxT[lo:lo + FD, g, P:S], foxT[lo:lo + FD, 8 + g, :], start=True, stop=True), f"s.{2 * g + i}")
                if g > 0:
                    for i in range(2):
                        f = 2 * g - 2 + i
                        pe.wait_ge(sdiv, f + 1)
                        transposes(f"pT.{f}", [scores[f % 2][:, k * P:k * P + P] for k in range(3)])
                    name = f"pv.{g - 1}"
                    o = open_bank(name)
                    for i in range(2):
                        f = 2 * g - 2 + i
                        lo = FD * i
                        wait_drained(pe, f"pT.{f}")
                        v = [fox[:, n, 2 * D + FD * f:2 * D + FD * f + FD] for n in range(NT)]
                        t.matmul(o[lo:lo + FD, 0:P], v[0], probsT[i][:, 0:P], start=True, stop=True)
                        t.matmul(o[lo:lo + FD, P:S], v[0], probsT[i][:, P:2 * P], start=True, stop=False)
                        ins = t.matmul(o[lo:lo + FD, P:S], v[1], probsT[i][:, 2 * P:3 * P], start=False, stop=True)
                    close(ins, name)
            for g in range(8):
                wait_drained(pe, f"pv.{g}")
            for j in range(2):
                w = weights(W_YF + j)
                for n in range(NT):
                    project(f"yf.{j}.{n}", w, n, ofT)
            for n in range(NT):
                pe.wait_ge(mixed, 2 * NT)
                for j in range(2):
                    transposes(f"mT.{n}.{j}", [mix[:, n, P * c:P * c + P] for c in range(4 * j, 4 * j + 4)])
            for n in range(NT):
                for j in range(2):
                    wait_drained(pe, f"mT.{n}.{j}")
            for j in range(2):
                w = weights(W_WO + j)
                for n in range(NT):
                    project(f"wo.{j}.{n}", w, n, mixT)
            for n in range(NT):
                pe.wait_ge(xn_ready, NT + n + 1)
                for j in range(2):
                    transposes(f"hT.{n}.{j}", [hn[:, n, P * c:P * c + P] for c in range(4 * j, 4 * j + 4)])
            for n in range(NT):
                for j in range(2):
                    wait_drained(pe, f"hT.{n}.{j}")
            o = open_bank("router")
            for n in range(NT):
                for c in range(KC):
                    ins = t.matmul(o[:, NE * n:NE * n + NE], actT[:, c, n * P:n * P + P], wrt[:, c, :], start=(c == 0), stop=(c == KC - 1))
            close(ins, "router")
            pe.wait_ge(p_loaded, 48)
            pe.wait_ge(onehot_ready, 1)
            o = open_bank("rank")
            for n in range(NT):
                lo = n * NE
                ins = t.matmul(o[:, lo:lo + NE], stri[:, :], chosen[:, n, :], start=True, stop=(n == 0))
                if n == 1:
                    ins = t.matmul(o[:, lo:lo + NE], ones[:, :], chosen[:, 0, :], start=False, stop=True)
            for n in range(NT):
                ins = t.matmul(o[:, 2 * NE:3 * NE], ones[:, :], chosen[:, n, :], start=(n == 0), stop=(n == 1))
            close(ins, "rank")
            for n in range(NT):
                transposes(f"pT2.{n}", [p_t[:, n, 0:P], p_t[:, n, P:S]])
            for n in range(NT):
                wait_drained(pe, f"pT2.{n}")
            for n in range(NT):
                for j in range(2):
                    o = open_bank(f"e.{n}.{j}")
                    for c in range(2):
                        ins = t.matmul(o[:, :], pT[:, c, n * P:n * P + P], wple[:, c, WT * j:WT * j + WT], start=(c == 0), stop=(c == 1))
                    close(ins, f"e.{n}.{j}")
            for b in range(8):
                pe.wait_ge(drained[b], len([1 for q in fills if place[q][0] == b]))
            pe.wait_ge(shared_loaded, 48)
            for n in range(NT):
                for w, part in ((sgw, 0), (suw, DE)):
                    for c in range(KC):
                        ins = t.matmul(bank[4 + n][:, part:part + DE], actT[:, c, n * P:n * P + P], w[:, c, :],
                                       start=(c == 0), stop=(c == KC - 1))
                ins.then_inc(gu_filled, 1)
            for n in range(NT):
                pe.wait_ge(hid_ready, n + 1)
                for c in range(2):
                    ins = t.transpose(bank[6 + n][:, c * P:c * P + P], shid[n][:, c * P:c * P + P], ident[:, :])
                ins.then_inc(hidT_filled, 1)
            for n in range(NT):
                pe.wait_ge(hidT_ready, n + 1)
                for j in range(2):
                    for c in range(2):
                        ins = t.matmul(bank[2 * n + j][:, :], shidT[n][:, c, :], sdw[:, c, WT * j:WT * j + WT],
                                       start=(c == 0), stop=False, skip_group_check=True)
            ins.then_inc(shared_done, 1)

            def gather(t_):
                pe.wait_ge(onehot_ready, t_ + 1)
                for half, s in ((0, xa_filled), (1, xb_filled)):
                    for c in range(4):
                        for i, (k, n) in enumerate((k, n) for k in range(3) for n in range(NT)):
                            ins = t.matmul(bank[5 + half][:, c * P:c * P + P], hparts[:, k, n, (4 * half + c) * P:(4 * half + c + 1) * P],
                                           onehot[:, n, :], start=(i == 0), stop=(i == 5))
                    ins.then_inc(s, 1)

            def places(e2):
                b16 = bank[7][:, DE:DE + P].bitcast(BF16)
                for n in range(NT):
                    t.transpose(b16[:, n * P:n * P + P], onehot[:, n, :], identb[:, :])
                for n in range(NT):
                    ins = t.matmul(bank[7][:, 400:406], onehot[:, n, :], gparts[:, n, e2, :], start=(n == 0), stop=(n == 1))
                ins.then_inc(place_filled, 1)

            def add_to_tokens(s):
                for n in range(NT):
                    for j in range(2):
                        ins = t.matmul(bank[2 * n + j][:, :], spread[s][:, n, :], y[:, WT * j:WT * j + WT],
                                       start=False, stop=False, skip_group_check=True)
                ins.then_inc(added, 1)

            pe.wait_ge(parts_ready, 2 * NT + 1)
            gather(1)
            places(slice(0, 2))
            pe.wait_ge(passes_ready, 1)
            np_pe = pe.value_load(passes[0:1, 0:1], min_val=1, max_val=S // CAP)
            with pe.Fori(0, np_pe) as r:
                with pe.Fori(0, PAIRS // 2) as k:
                    for s in range(2):
                        before = r * PAIRS + k * 2 + s
                        turn = r * (PAIRS // 2) + k + 1
                        pe.wait_ge(gu_loaded[s], turn * 32)
                        pe.wait_ge(xa_ready, before + 1)
                        pe.wait_ge(xb_ready, before + 1)
                        pe.wait_ge(y_ready[0], before + 1)
                        for c in range(KC):
                            for e in range(2):
                                w = gu_in[s][:, :, e, c * DE:c * DE + DE]
                                ins = t.matmul(bank[4][e * CAP:e * CAP + CAP, :], xg[:, c, e * CAP:e * CAP + CAP], w, start=(c == 0), stop=(c == KC - 1))
                        ins.then_inc(pgu_filled, 1)
                        pe.wait_ge(y_ready[1], before + 1)
                        pe.wait_ge(place_ready, before + 1)
                        add_to_tokens(1 - s)
                        pe.wait_ge(phid_ready, before + 1)
                        for c in range(2):
                            ins = t.transpose(bank[7][:, c * P:c * P + P], hid[:, c * P:c * P + P], ident[:, :])
                        ins.then_inc(phidT_filled, 1)
                        gather(before + 2)
                        pe.wait_ge(phidT_ready, before + 1)
                        places(bass.ds(k * 4 + (2 * s + 2), 2))
                        pe.wait_ge(d_loaded[s], turn * 16)
                        for j in range(2):
                            if j == 1:
                                pe.wait_ge(xa_ready, before + 2)
                            for c in range(2):
                                for e in range(2):
                                    ins = t.matmul(bank[4 + j][e * CAP:e * CAP + CAP, :], hidT[:, c, e * CAP:e * CAP + CAP],
                                                   d_in[s][:, e, c * D + WT * j:c * D + WT * j + WT], start=(c == 0), stop=(c == 1))
                            ins.then_inc(y_filled[j], 1)
            last = np_pe * PAIRS
            pe.wait_ge(y_ready[0], last + 1)
            pe.wait_ge(y_ready[1], last + 1)
            pe.wait_ge(place_ready, last + 1)
            for n in range(NT):
                for j in range(2):
                    ins = t.matmul(bank[2 * n + j][:, :], spread[1][:, n, :], y[:, WT * j:WT * j + WT],
                                   start=False, stop=True, skip_group_check=True)
            ins.then_inc(added, 1)
            for n in range(NT):
                pe.wait_ge(xn_ready, 2 * NT + n + 1)
                for j in range(2):
                    for c in range(4):
                        ins = t.transpose(bank[2 * n + j][:, c * P:c * P + P], hn[:, n, (4 * j + c) * P:(4 * j + c + 1) * P], ident[:, :])
                    ins.then_inc(hidT_filled, 1)
            pe.wait_ge(wpg_loaded, 32)
            pe.wait_ge(e_ready, NT + 2 * NT)
            for j in range(2):
                for n in range(NT):
                    for c in range(KC):
                        ins = t.matmul(bank[4 + NT * j + n][:, :], actT[:, c, n * P:n * P + P], wpg[j][:, c, :], start=(c == 0), stop=(c == KC - 1))
                    ins.then_inc(pg_filled, 1)

        @block.vector
        def _(dve):
            v = nc.vector
            steps = [0]

            def step(ins):
                steps[0] += 1
                ins.then_inc(dve_step, 1)
                return steps[0]

            def seq(ins):
                dve.wait_ge(dve_step, step(ins))

            def close(ins, name):
                ins.then_inc(drained[place[name][0]], 1)

            def blocks4(name, n=4):
                return ps(name)[:, 0:n * P].rearrange("p (a b) -> p a b", a=n)

            def norm(k, dst):
                for n in range(NT):
                    dve.wait_ge(rinv_made, NT * k + n + 1)
                    v.tensor_scalar(dst[:, n, :], h[:, n, :], rinv_x[k][:, n:n + 1], None, ALU.mult).then_inc(xn_ready, 1)

            wait_filled(dve, "cols")
            seq(v.tensor_copy(cols[:, 0:R_ALL], ps("cols")[:, 0:R_ALL]))
            close(v.tensor_scalar(cols[:, R_QN:R_QN + 1], cols[:, R_QN:R_QN + 1], FD ** -0.5, None, ALU.mult), "cols")
            norm(0, xn)
            wait_drained(dve, "cols")
            for n in range(NT):
                for j in range(2):
                    nm = f"xT.{n}.{j}"
                    wait_filled(dve, nm)
                    close(v.tensor_tensor(actT[:, 4 * j:4 * j + 4, n * P:n * P + P], blocks4(nm), bc(cols[:, R_NMIX + 4 * j:R_NMIX + 4 * j + 4], 2, P), ALU.mult), nm)
            for c2 in range(12):
                nm = f"qkv.{c2}"
                wait_filled(dve, nm)
                for s in range(4):
                    for i in range(2):
                        ct = 2 * c2 + i
                        wcol = cols[:, R_CONV + 24 * (3 - s) + ct:R_CONV + 24 * (3 - s) + ct + 1]
                        src = ps(nm)[:, i * S:i * S + S - s]
                        dst = qkvT[:, ct, s:S]
                        if s == 0:
                            k = step(v.tensor_scalar(dst, src, wcol, None, ALU.mult))
                        else:
                            dve.wait_ge(dve_step, k - 1 + i if s == 1 else k - 1)
                            ins = v.scalar_tensor_tensor(out=dst, in0=src, scalar=wcol, in1=dst, op0=ALU.mult, op1=ALU.add)
                            if s == 3 and i == 1:
                                close(ins, nm)
                            else:
                                k = step(ins)
            dve.wait_ge(bias_loaded, 64)
            dve.wait_ge(consts, 1)
            wait_filled(dve, "small")
            close(v.tensor_tensor(u_s, ps("small")[:, 0:64].rearrange("p (n c) -> p n c", n=NT), bc(bias3[:, :], 1, NT), ALU.add), "small")
            wait_drained(dve, "small")
            seq(v.tensor_scalar(t_s, u_s, -1.0, None, ALU.mult))
            v.tensor_tensor(t_s, t_s, u_s, ALU.max).then_inc(logs_ready, 1)
            dve.wait_ge(soft, 3)
            seq(v.tensor_scalar(t_s[:, :, 0:8], u_s[:, :, 0:8], 0.0, None, ALU.max))
            seq(v.tensor_tensor(t_s[:, :, 0:8], t_s[:, :, 0:8], l_s[:, :, 0:8], ALU.add))
            seq(v.tensor_scalar(nega[:, :], nega[:, :], -1.0, None, ALU.mult))
            seq(v.tensor_tensor(la[:, :, 0:8], t_s[:, :, 0:8], bc(nega[:, :], 1, NT), ALU.mult))
            seq(v.tensor_scalar(t_s[:, :, 16:32], u_s[:, :, 16:32], 0.0, None, ALU.min))
            v.tensor_tensor(la[:, :, 8:24], t_s[:, :, 16:32], l_s[:, :, 16:32], ALU.subtract).then_inc(logs_ready, 1)
            seq(v.tensor_scalar(beta, beta, 1.0, None, ALU.add))
            seq(v.reciprocal(beta, beta))
            wait_filled(dve, "cum")
            close(v.tensor_copy(cs, ps("cum")[:, 0:96]), "cum")
            wait_drained(dve, "cum")
            run = cs[:, 0:48].rearrange("p (n c) -> p n c", n=NT)
            tot = cs[:, 48:96].rearrange("p (n c) -> p n c", n=NT)
            seq(v.tensor_tensor(gtail.rearrange("p (n c) -> p n c", n=NT), tot[:, :, 0:8], run[:, :, 0:8], ALU.subtract))
            seq(v.tensor_scalar(cf[:, 0, :], run[:, 0, 8:24], -1.0, None, ALU.mult))
            seq(v.tensor_tensor(cf[:, 1, :], run[:, 1, 8:24], tot[:, 0, 8:24], ALU.add))
            seq(v.tensor_scalar(cf[:, 1, :], cf[:, 1, :], -1.0, None, ALU.mult))
            seq(v.tensor_copy(gb[:, 16:32].rearrange("p (n c) -> p n c", n=NT), beta))
            v.tensor_copy(gb[:, 0:16].rearrange("p (n c) -> p n c", n=NT), run[:, :, 0:8]).then_inc(gstat, 1)
            wait_filled(dve, "gbT")
            close(v.tensor_copy(gbT[0:16, :], ps("gbT")[0:16, 0:256]), "gbT")
            for j in range(4):
                for n in range(NT):
                    nm = f"tq.{n}.{j}"
                    wait_drained(dve, nm)
                    src = qk[:, n, WT * j:WT * j + WT]
                    seq(v.tensor_tensor(sq[:, 0:WT], src, src, ALU.mult))
                    v.tensor_reduce(qk_ss[:, n, 4 * j:4 * j + 4], sq[:, 0:WT].rearrange("p (a b) -> p a b", a=4), AX.X, ALU.add).then_inc(qkss, 1)
                    dve.wait_ge(qkss, NT * j + n + 1)
            for j in range(2):
                for n in range(NT):
                    nm = f"tq.{n}.{4 + j}"
                    wait_filled(dve, nm)
                    close(v.tensor_tensor(vbeta[:, GH * n + 4 * j:GH * n + 4 * j + 4, :], blocks4(nm), bc(beta[:, n, 4 * j:4 * j + 4], 2, P), ALU.mult), nm)
            for j in range(4):
                for n in range(NT):
                    dve.wait_ge(qkrinv, NT * j + n + 1)
                    src = qk[:, n, WT * j:WT * j + WT].rearrange("p (a b) -> p a b", a=4)
                    v.tensor_tensor(src, src, bc(qk_ri[:, n, 4 * j:4 * j + 4], 2, P), ALU.mult).then_inc(qk_normed, 1)
            dve.wait_ge(qk_normed, 8)
            dve.wait_ge(consts, 6)
            for j in range(4):
                nm = f"gb.{j}"
                wait_filled(dve, nm)
                d4 = dT[:, 4 * j:4 * j + 4, :]
                close(v.tensor_tensor(d4, blocks4(nm), bc(gb[:, 4 * j:4 * j + 4], 2, P), ALU.subtract), nm)
                wait_drained(dve, nm)
                v.tensor_scalar(d4, d4, 0.0, None, ALU.min).then_inc(d_ready, 1)
            for j in range(4):
                dve.wait_ge(dexp_ready, j + 1)
                d4 = dT[:, 4 * j:4 * j + 4, :]
                v.tensor_tensor(d4, d4, bc(tri[:, :], 1, 4), ALU.mult).then_inc(d_masked, 1)
            for j in range(4):
                dve.wait_ge(d_masked, j + 1)
                nm = f"bb.{j}"
                l4, d4 = lT[:, 4 * j:4 * j + 4, :], dT[:, 4 * j:4 * j + 4, :]
                seq(v.tensor_tensor(l4, d4, bc(stri[:, :], 1, 4), ALU.mult))
                wait_filled(dve, nm)
                close(v.tensor_tensor(l4, l4, blocks4(nm), ALU.mult), nm)
            for j in range(4):
                l4, d4 = lT[:, 4 * j:4 * j + 4, :], dT[:, 4 * j:4 * j + 4, :]
                wait_drained(dve, f"bb.{j}")
                wait_filled(dve, f"kk.{j}")
                close(v.tensor_tensor(l4, l4, blocks4(f"kk.{j}"), ALU.mult), f"kk.{j}")
                wait_filled(dve, f"qk.{j}")
                close(v.tensor_tensor(d4, d4, blocks4(f"qk.{j}"), ALU.mult), f"qk.{j}")

            dve.wait_ge(masks_made, LEVELS)

            def coupling(lv):
                for j in range(4):
                    if lv == 0:
                        wait_drained(dve, f"kk.{j}")
                    else:
                        wait_filled(dve, f"P.{lv - 1}.{j}")
                    v.tensor_tensor(mT[:, 4 * j:4 * j + 4, :], lT[:, 4 * j:4 * j + 4, :], bc(lmask[:, lv, :], 1, 4), ALU.mult).then_inc(m_ready, 1)

            coupling(0)
            for j in range(4):
                dve.wait_ge(m_ready, j + 1)
                wait_filled(dve, f"gb.{j}")
                wait_filled(dve, f"bb.3")
                seq(v.tensor_tensor(vi[:, 4 * j:4 * j + 4, :], bc(ident[:, :], 1, 4), mT[:, 4 * j:4 * j + 4, :], ALU.subtract))
                nm = f"P.0.{j}"
                wait_filled(dve, nm)
                close(v.tensor_tensor(xi[:, 4 * j:4 * j + 4, :], bc(ident[:, :], 1, 4), blocks4(nm), ALU.subtract), nm)
            for lv in range(1, LEVELS):
                coupling(lv)
                for j in range(4):
                    for t, nm in ((xi, f"X.{lv}.{j}"), (vi, f"V.{lv}.{j}")):
                        if t is xi and lv == LEVELS - 1:
                            continue
                        wait_filled(dve, nm)
                        if t is xi and lv > 1:
                            wait_drained(dve, f"X.{lv - 1}.{j}")
                        elif t is xi:
                            wait_drained(dve, f"P.0.{j}")
                        elif lv > 1:
                            wait_drained(dve, f"V.{lv - 1}.{j}")
                        t4 = t[:, 4 * j:4 * j + 4, :]
                        close(v.tensor_tensor(t4, t4, blocks4(nm), ALU.subtract), nm)
            dve.wait_ge(geg, 2)
            seq(v.tensor_tensor(be_s, eg_s, gb[:, 16:32], ALU.mult))
            q1 = qk[:, 1, 0:D].rearrange("p (h d) -> p h d", h=GH)
            k0 = qk[:, 0, D:2 * D].rearrange("p (h d) -> p h d", h=GH)
            k1 = qk[:, 1, D:2 * D].rearrange("p (h d) -> p h d", h=GH)
            for n in range(NT):
                for j in range(4):
                    wait_drained(dve, f"tk.{n}.{j}")
            v.tensor_tensor(q1, q1, bc(eg_s[:, 8:16], 2, P), ALU.mult).then_inc(scaled, 1)
            wait_filled(dve, f"P.{LEVELS - 1}.3")
            v.tensor_tensor(kbe, k1, bc(be_s[:, 8:16], 2, P), ALU.mult).then_inc(scaled, 1)
            v.tensor_tensor(k0, k0, bc(et_s[:, 0:8], 2, P), ALU.mult).then_inc(scaled, 1)
            for n in range(NT):
                for part in range(2):
                    for j in range(2):
                        wait_drained(dve, f"fox.{2 * part + j}.{n}")
                    wait_filled(dve, "o1.1")
                    src = fox[:, n, D * part:D * part + D]
                    seq(v.tensor_tensor(at(TPB, 1024), src, src, ALU.mult))
                    ins = v.tensor_reduce(f_ss[:, n, 16 * part:16 * part + 16], at(TPB, 1024).rearrange("p (a b) -> p a b", a=16), AX.X, ALU.add)
                    if part:
                        ins.then_inc(fss, 1)
                        dve.wait_ge(fss, n + 1)
                    else:
                        seq(ins)
            for nm in ("o0.0", "o0.1", "o1.0", "o1.1"):
                wait_drained(dve, nm)
            o16 = oa.rearrange("p n (h v) -> p (n h) v", h=GH)
            for n in range(NT):
                seq(v.tensor_tensor(at(TPB, 1024), oa[:, n, :], oa[:, n, :], ALU.mult))
                ins = v.tensor_reduce(o_ss[:, 8 * n:8 * n + 8], at(TPB, 1024).rearrange("p (a b) -> p a b", a=8), AX.X, ALU.add)
                if n:
                    ins.then_inc(oss, 1)
                else:
                    seq(ins)
            for n in range(NT):
                dve.wait_ge(frinv, n + 1)
                src = fox[:, n, 0:2 * D].rearrange("p (a b) -> p a b", a=32)
                v.tensor_tensor(src, src, bc(f_ri[:, n, :], 2, FD), ALU.mult).then_inc(f_normed, 1)
            dve.wait_ge(orinv, 1)
            for j in range(2):
                for n in range(NT):
                    wait_drained(dve, f"z.{j}.{n}")
            for n in range(NT):
                o8 = o16[:, 8 * n:8 * n + 8, :]
                seq(v.tensor_tensor(o8, o8, bc(o_ri[:, 8 * n:8 * n + 8], 2, P), ALU.mult))
                v.tensor_tensor(oa[:, n, :], oa[:, n, :], zs[:, n, :], ALU.mult).then_inc(o_normed, 1)
            wait_filled(dve, "cT")
            dve.wait_ge(bd_made, 1)
            close(v.tensor_copy(cT[0:16, :], ps("cT")[0:16, 0:256]), "cT")
            for n in range(NT):
                for j in range(2):
                    wait_filled(dve, f"oT.{n}.{j}")
            for j in range(8):
                nm = f"cb.{j}"
                wait_filled(dve, nm)
                src = ps(nm)[:, :].rearrange("p (f k) -> p f k", f=2)
                dst = cbm[:, 2 * j:2 * j + 2, :]
                v.tensor_tensor(dst[:, :, 0:P], src[:, :, 0:P], bc(negm[:, :], 1, 2), ALU.add).then_inc(dve_step, 1)
                v.tensor_copy(dst[:, :, P:2 * P], src[:, :, 0:P]).then_inc(dve_step, 1)
                steps[0] += 2
                close(v.tensor_tensor(dst[:, :, 2 * P:3 * P], src[:, :, P:S], bc(negm[:, :], 1, 2), ALU.add), nm)
            wait_filled(dve, "cb.7")
            for j in range(2):
                for n in range(NT):
                    nm = f"ya.{j}.{n}"
                    wait_filled(dve, nm)
                    for jm in range(4):
                        wait_drained(dve, f"merge.{jm}.{n}")
                    close(v.tensor_tensor(mix[:, n, WT * j:WT * j + WT], ps(nm)[:, :], merge[:, n, WT * j:WT * j + WT], ALU.mult), nm)
            for g in range(8):
                wait_drained(dve, f"cb.{g}")
            for g in range(9):
                if g < 8:
                    for f in (2 * g, 2 * g + 1):
                        nm = f"s.{f}"
                        wait_filled(dve, nm)
                        if g > 0:
                            wait_filled(dve, f"pT.{f - 2}")
                        sc = scores[f % 2]
                        close(v.tensor_tensor(sc, ps(nm)[:, 0:384], cbm[:, f, :], ALU.add), nm)
                        wait_drained(dve, nm)
                        v.tensor_reduce(mx[:, 2 * f:2 * f + 1], sc[:, 0:P], AX.X, ALU.max, negate=True).then_inc(smax, 1)
                        v.tensor_reduce(mx[:, 2 * f + 1:2 * f + 2], sc[:, P:3 * P], AX.X, ALU.max, negate=True).then_inc(smax, 1)
                    for f in (2 * g, 2 * g + 1):
                        dve.wait_ge(sexp, 2 * f + 2)
                        sc = scores[f % 2]
                        seq(v.reciprocal(dri[:, 2 * f:2 * f + 2], den[:, 2 * f:2 * f + 2]))
                        seq(v.tensor_scalar(sc[:, 0:P], sc[:, 0:P], dri[:, 2 * f:2 * f + 1], None, ALU.mult))
                        v.tensor_scalar(sc[:, P:3 * P], sc[:, P:3 * P], dri[:, 2 * f + 1:2 * f + 2], None, ALU.mult).then_inc(sdiv, 1)
            for j in range(2):
                for n in range(NT):
                    nm = f"yf.{j}.{n}"
                    wait_filled(dve, nm)
                    close(v.tensor_tensor(mixf[:, n, WT * j:WT * j + WT], ps(nm)[:, :], merge[:, n, D + WT * j:D + WT * j + WT], ALU.mult), nm)
                    wait_drained(dve, nm)
                    wait_drained(dve, f"ya.{j}.{n}")
                    m = mix[:, n, WT * j:WT * j + WT]
                    v.tensor_tensor(m, m, mixf[:, n, WT * j:WT * j + WT], ALU.add).then_inc(mixed, 1)
            for j in range(2):
                for n in range(NT):
                    nm = f"wo.{j}.{n}"
                    wait_filled(dve, nm)
                    hv = h[:, n, WT * j:WT * j + WT]
                    close(v.tensor_tensor(hv, hv, ps(nm)[:, :], ALU.add), nm)
                    wait_drained(dve, nm)
                    v.memset(stat[:, 990 + 2 * j + n:991 + 2 * j + n], 0.0).then_inc(h_ready, 1)

            dve.wait_ge(ngain_loaded, 16)
            for n in range(NT):
                dve.wait_ge(rinv_made, NT + n + 1)
                v.scalar_tensor_tensor(out=hn[:, n, :].rearrange("p (c q) -> p c q", c=KC), in0=h[:, n, :].rearrange("p (q c) -> p c q", c=KC),
                                       scalar=rinv_x[1][:, n:n + 1], in1=ngain.rearrange("p (q c) -> p c q", c=KC),
                                       op0=ALU.mult, op1=ALU.mult).then_inc(xn_ready, 1)
            for n in range(NT):
                dve.wait_ge(parts_ready, n + 1)
                for j in range(2):
                    wait_filled(dve, f"hT.{n}.{j}")
                seq(v.tensor_tensor(hn[:, n, :], hn[:, n, :], hparts[:, 0, n, :], ALU.subtract))
            wait_drained(dve, "router")
            for n in range(NT):
                seq(v.tensor_tensor(sel[:, n, :], sg[:, n, :], rbias[:, :], ALU.add))
                seq(v.max(top[:, n, :], sel[:, n, :]))
                seq(v.match_replace(out=gates[:, n, :], in_to_replace=top[:, n, :], in_values=sel[:, n, :], imm_value=-1e30))
                ins = v.tensor_tensor(chosen[:, n, :], gates[:, n, :], sel[:, n, :], ALU.not_equal)
                if n == 1:
                    ins.then_inc(onehot_ready, 1)
                else:
                    seq(ins)
            dve.wait_ge(onehot_ready, 1)
            for n in range(NT):
                seq(v.tensor_tensor(gates[:, n, :], chosen[:, n, :], sg[:, n, :], ALU.mult))
                seq(v.tensor_reduce(gsum[:, n, 0:1], gates[:, n, :], AX.X, ALU.add))
                seq(v.reciprocal(gsum[:, n, 1:2], gsum[:, n, 0:1]))
                seq(v.tensor_scalar(gates[:, n, :], gates[:, n, :], gsum[:, n, 1:2], ROUTED_SCALE, ALU.mult, ALU.mult))
            wait_filled(dve, "rank")
            px = posx[:, :, 0:NE]
            seq(v.tensor_scalar(px, ps("rank")[:, 0:2 * NE].rearrange("p (n c) -> p n c", n=NT), 1.0, None, ALU.add))
            seq(v.tensor_tensor(px, px, chosen[:, :, :], ALU.mult))
            seq(v.tensor_scalar(px, px, -1.0, None, ALU.add))
            seq(v.tensor_scalar(posx[:, :, NE:NX], posx[:, :, 0:LOOKAHEAD], -float(CAP), None, ALU.add))
            close(v.tensor_reduce(gsum[:, 0, 0:1], ps("rank")[:, 2 * NE:3 * NE], AX.X, ALU.max), "rank")
            wait_drained(dve, "rank")
            m, q = gsum[:, 0, 0:1], gsum[:, 0, 1:2]
            seq(v.tensor_scalar(q, m, float(CAP), 1.0, ALU.is_gt, ALU.add))
            for k in range(2, S // CAP):
                seq(v.scalar_tensor_tensor(out=q, in0=m, scalar=float(CAP * k), in1=q, op0=ALU.is_gt, op1=ALU.add))
            seq(v.tensor_copy(passes[:, 0:1], q))
            v.tensor_scalar(passes[:, 1:2], q, float(PAIRS // 2), None, ALU.mult).then_inc(passes_ready, 1)
            r1 = sel[:, :, :]
            gp = lambda k: gparts[:, :, 0:NE, k]
            seq(v.tensor_copy(gp(0), gates[:, :, :]))
            seq(v.tensor_tensor(r1, gates[:, :, :], gp(0), ALU.subtract))
            seq(v.tensor_copy(gp(1), r1))
            seq(v.tensor_tensor(gp(2), r1, gp(1), ALU.subtract))
            v.tensor_copy(gparts[:, :, NE:NX, :], gparts[:, :, 0:LOOKAHEAD, :]).then_inc(parts_ready, 1)
            for n in range(NT):
                seq(v.tensor_copy(hparts[:, 1, n, :], hn[:, n, :]))
                v.tensor_tensor(hparts[:, 2, n, :], hn[:, n, :], hparts[:, 1, n, :], ALU.subtract).then_inc(parts_ready, 1)
            dve.wait_ge(passes_ready, 1)

            def place_tokens(e2):
                for n in range(NT):
                    dst = onehot[:, n, :].rearrange("p (e s) -> p e s", e=2)
                    ins = v.tensor_tensor(dst, bc(iota[:, :], 1, 2), bc(posx[:, n, e2], 2, CAP), ALU.is_equal)
                    if n == 0:
                        seq(ins)
                ins.then_inc(onehot_ready, 1)

            place_tokens(slice(0, 2))
            for n in range(NT):
                dve.wait_ge(erinv, n + 1)
                seq(v.tensor_scalar(e_t[:, n, :], e_t[:, n, :], e_ri[:, n:n + 1], None, ALU.mult))
                v.tensor_tensor(e_t[:, n, :], e_t[:, n, :], plen, ALU.mult).then_inc(e_ready, 1)
            for n in range(NT):
                dve.wait_ge(gu_silu, n + 1)
                up = bank[4 + n][:, DE:2 * DE].rearrange("p (q c) -> p c q", c=2)
                v.tensor_tensor(shid[n].rearrange("p (c q) -> p c q", c=2), ssil[n].rearrange("p (q c) -> p c q", c=2), up, ALU.mult).then_inc(hid_ready, 1)

            for j in range(2):
                v.memset(y[:, WT * j:WT * j + WT], 0.0).then_inc(y_ready[j], 1)
            seq(v.memset(spread[1], 0.0))

            def gathered(t, s):
                dve.wait_ge(xb_filled, t)
                v.tensor_copy(xg[:, 4:8, :], bank[6][:, :].rearrange("p (c s) -> p c s", c=4)).then_inc(xb_ready, 1)
                dve.wait_ge(place_filled, t)
                seq(v.tensor_copy(spread[s], bank[7][:, DE:DE + P].bitcast(BF16).rearrange("p (n t) -> p n t", n=NT)))
                for e in range(2):
                    lo = e * CAP
                    ins = v.tensor_reduce(gslot[lo:lo + CAP, :], bank[7][lo:lo + CAP, 400 + 3 * e:403 + 3 * e], AX.X, ALU.add)
                    if e == 0:
                        seq(ins)
                ins.then_inc(place_ready, 1)

            gathered(1, 0)
            place_tokens(slice(2, 4))
            np_dve = dve.value_load(passes[0:1, 0:1], min_val=1, max_val=S // CAP)
            with dve.Fori(0, np_dve) as r:
                with dve.Fori(0, PAIRS // 2) as k:
                    for s in range(2):
                        before = r * PAIRS + k * 2 + s
                        dve.wait_ge(psilu, before + 1)
                        dve.wait_ge(place_ready, before + 1)
                        up = bank[4][:, DE:2 * DE].rearrange("p (q c) -> p c q", c=2)
                        v.scalar_tensor_tensor(out=hid.rearrange("p (c q) -> p c q", c=2), in0=sil.rearrange("p (q c) -> p c q", c=2),
                                               scalar=gslot[:, 0:1], in1=up, op0=ALU.mult, op1=ALU.mult).then_inc(phid_ready, 1)
                        dve.wait_ge(xb_filled, before + 2)
                        v.tensor_copy(xg[:, 4:8, :], bank[6][:, :].rearrange("p (c s) -> p c s", c=4)).then_inc(xb_ready, 1)
                        dve.wait_ge(place_filled, before + 2)
                        dve.wait_ge(phid_ready, before + 1)
                        v.tensor_copy(spread[1 - s], bank[7][:, DE:DE + P].bitcast(BF16).rearrange("p (n t) -> p n t", n=NT)).then_inc(spread_made, 1)
                        for e in range(2):
                            lo = e * CAP
                            v.tensor_reduce(gslot[lo:lo + CAP, :], bank[7][lo:lo + CAP, 400 + 3 * e:403 + 3 * e], AX.X, ALU.add).then_inc(place_half if e == 0 else place_ready, 1)
                        ahead = bass.ds(k * 4 + (2 * s + 4), 2)
                        for n in range(NT):
                            dst = onehot[:, n, :].rearrange("p (e s) -> p e s", e=2)
                            v.tensor_tensor(dst, bc(iota[:, :], 1, 2), bc(posx[:, n, ahead], 2, CAP), ALU.is_equal).then_inc(onehot_half if n == 0 else onehot_ready, 1)
                        dve.wait_ge(y_filled[1], before + 1)
                        v.tensor_copy(y[:, WT:D], bank[5][:, :]).then_inc(y_ready[1], 1)
                dve.wait_ge(onehot_ready, r * PAIRS + (PAIRS + 3))
                v.tensor_scalar(iota[:, :], iota[:, :], float(CAP), None, ALU.add).then_inc(iota_moved, 1)
                dve.wait_ge(iota_moved, r + 1)
            dve.wait_ge(added, np_dve * PAIRS + 1)
            for n in range(NT):
                for j in range(2):
                    hv = h[:, n, WT * j:WT * j + WT]
                    v.tensor_tensor(hv, hv, bank[2 * n + j][:, :], ALU.add).then_inc(h_ready, 1)
            dve.wait_ge(h_ready, 8)
            norm(2, hn)
            for n in range(NT):
                for j in range(2):
                    dve.wait_ge(hidT_filled, NT + 2 * n + j + 1)
                    src = bank[2 * n + j][:, :].rearrange("p (a b) -> p a b", a=4)
                    v.tensor_tensor(actT[:, 4 * j:4 * j + 4, n * P:n * P + P], src, bc(cols[:, R_NPG + 4 * j:R_NPG + 4 * j + 4], 2, P), ALU.mult).then_inc(e_ready, 1)
            for n in range(NT):
                dve.wait_ge(sg_ready, NT + n + 1)
                seq(v.tensor_tensor(gt[:, n, :], gt[:, n, :], e_t[:, n, :], ALU.mult))
                v.tensor_tensor(gt[:, n, :], gt[:, n, :], h[:, n, :], ALU.add).then_inc(out_ready, 1)


_INS = ['x', 'p', 'norm_mix', 'w_in', 'conv_w', 'a_log', 'dt_bias', 'gdn_norm', 'fox_f_bias', 'q_norm', 'k_norm',
        'w_branch_gdn', 'w_branch_fox', 'w_out', 'norm_ffn', 'w_router', 'router_bias', 'we_gate', 'we_up', 'we_down',
        'ws_gate', 'ws_up', 'ws_down', 'w_ple', 'ple_norm', 'ple_gate_norm', 'w_ple_gate']


def kernel(**inputs):
    import numpy as np
    import concourse.bacc as bacc
    from concourse.bass_utils import run_bass_kernel_spmd

    nc = bacc.Bacc("TRN2", target_bir_lowering=False, num_devices=1)
    arrays, args = {}, []
    for name in _INS:
        a = np.ascontiguousarray(inputs[name])
        arrays[f"in_{name}"] = a
        args.append(nc.dram_tensor(f"in_{name}", a.shape, mybir.dt.from_np(a.dtype), kind="ExternalInput").ap())
    res = nc.dram_tensor("out_0", (1, S, D), F32, kind="ExternalOutput").ap()
    program(nc, *args, res)
    r = run_bass_kernel_spmd(nc, [arrays], core_ids=[0])
    return r.results[0]["out_0"]
```

```python
from contextlib import ExitStack

import concourse.bass as bass
from concourse import mybir

P = 128
F32 = mybir.dt.float32
BF16 = mybir.dt.bfloat16
ALU = mybir.AluOpType
ACT = mybir.ActivationFunctionType
AX = mybir.AxisListType

S, D = 256, 1024
NT = S // P
KC = D // P
GH, DK = 8, 128
FH, FD = 16, 64
NE, TOPK, DE = 64, 8, 256
ROUTED_SCALE = 2.5
EPS = 1e-6
LEVELS = 7
MASKED = -1e30

C_QKV, C_Z, C_AB, C_FOX, C_F, C_MERGE = 0, 3072, 4096, 4112, 7184, 7200
WT = 512
A_SLOTS = 3
CAP = 64
PAIRS = NE // 2
EW = KC * DE
PAIR_WORDS = 6 * EW
LOOKAHEAD = 4

R_CONV, R_NMIX, R_NFFN, R_NPG, R_GDN, R_QN, R_KN, R_ALL = 0, 96, 104, 112, 120, 121, 122, 123


def bc(ap, axis, n):
    v = ap.unsqueeze(axis)
    shape = list(v.shape)
    shape[axis] = n
    return v.to_broadcast(shape)


XV_ORDER = (("X", 0), ("X", 1), ("X", 2), ("V", 0), ("X", 3), ("V", 1), ("V", 2), ("V", 3))


BESIDE_FOX = {(0, 0): ["tq.0.5", "tq.1.5"], (2, 0): ["gb.0"], (2, 1): ["gb.1"], (3, 0): ["gb.2"], (3, 1): ["gb.3"],
              (4, 0): ["bb.0"], (4, 1): ["bb.1"], (5, 0): ["bb.2"], (5, 1): ["bb.3"]}
BESIDE_ATTENTION = ("merge.2.1", "merge.3.0", "merge.3.1", "ya.0.0", "ya.0.1", "ya.1.0", "ya.1.1")


def bank_fills():
    f = ["xT.0.0", "xT.0.1", "cols", "xT.1.0", "xT.1.1"]
    f += ["qkv.0", "qkv.1", "small", "qkv.2", "cum", "qkv.3", "gbT"]
    f += [f"qkv.{c}" for c in range(4, 12)]
    f += [f"tq.{n}.{j}" for j in range(5) for n in range(NT)]
    for j in range(6):
        for n in range(NT):
            f += [f"fox.{j}.{n}"] + BESIDE_FOX.get((j, n), [])
    f += ["cT"] + [f"tk.{n}.{j}" for n in range(NT) for j in range(4)]
    for j in range(4):
        f += [f"kk.{j}", f"qk.{j}"]
    f += ["z.0.0"]
    for lv in range(LEVELS):
        f += [f"P.{lv}.{j}" for j in range(4)]
        if lv == 0:
            f += ["z.0.1"]
        elif lv < LEVELS - 1:
            f += [f"{q}.{lv}.{j}" for q, j in XV_ORDER]
        else:
            f += [f"V.{lv}.{j}" for j in range(4)]
    f += [f"z.1.{n}" for n in range(NT)]
    for j in range(2):
        f += [f"tg.{j}", f"wT.{j}", f"u0.{j}"]
    for j in range(2):
        f += [f"o0.{j}", f"s1.{j}"]
    for j in range(2):
        f += [f"u1.{j}"]
    for j in range(2):
        f += [f"o1.{j}"]
    f += ["merge.0.0", "merge.0.1", "cb.0", "merge.1.0", "cb.1", "cb.2", "merge.1.1", "cb.3", "cb.4"]
    f += [f"oT.{n}.{j}" for n in range(NT) for j in range(2)]
    f += [f"fT.{n}.{j}" for n in range(NT) for j in range(4)]
    f += ["cb.5", "merge.2.0", "cb.6", "cb.7"]
    f += [f"s.{i}" for i in range(4)]
    for g in range(8):
        if g < 7:
            f += [BESIDE_ATTENTION[g]]
        f += [f"pT.{2 * g}", f"pT.{2 * g + 1}"]
        if g < 6:
            f += [f"s.{2 * g + 4}", f"s.{2 * g + 5}"]
        f += [f"pv.{g}"]
    f += [f"yf.{j}.{n}" for j in range(2) for n in range(NT)]
    f += [f"pT2.{n}" for n in range(NT)] + ["e.0.0"]
    f += [f"mT.{n}.{j}" for n in range(NT) for j in range(2)]
    f += [f"wo.{j}.{n}" for j in range(2) for n in range(NT)]
    f += ["e.0.1", "e.1.0"]
    f += [f"hT.{n}.{j}" for n in range(NT) for j in range(2)]
    f += ["e.1.1", "router"] + [f"sh.{n}" for n in range(NT)] + ["rank"]
    return f


def program(nc, x, p, norm_mix, w_in, conv_w, a_log, dt_bias, gdn_norm, fox_f_bias, q_norm, k_norm,
            w_branch_gdn, w_branch_fox, w_out, norm_ffn, w_router, router_bias, we_gate, we_up, we_down,
            ws_gate, ws_up, ws_down, w_ple, ple_norm, ple_gate_norm, w_ple_gate, out):
    ctx = ExitStack()
    with ctx:
        def sb(name, shape, dt=F32):
            return ctx.enter_context(nc.sbuf_tensor(name, shape, dt))

        def sem(name):
            return ctx.enter_context(nc.semaphore(name))

        bank = [ctx.enter_context(nc.psum_tensor(f"bank{i}", [P, 512], F32)) for i in range(8)]

        h = sb("h", [P, NT, D])
        actT = sb("actT", [P, KC, S])
        ident = sb("ident", [P, P])
        ones = sb("ones", [P, P])
        tri = sb("tri", [P, P])
        stri = sb("stri", [P, P])
        negm = sb("negm", [P, P])
        lmask = sb("lmask", [P, LEVELS, P], BF16)
        nhalf = sb("nhalf", [P, 32])
        cols = sb("cols", [P, P])
        bias3 = sb("bias3", [P, 32])
        nega = sb("nega", [P, GH])
        rbias = sb("rbias", [P, NE])
        NX = NE + LOOKAHEAD
        posx = sb("posx", [P, NT, NX])
        gparts = sb("gparts", [P, NT, NX, 3], BF16)
        iota = sb("iota", [P, CAP])
        onehot = sb("onehot", [P, NT, 2 * CAP], BF16)
        identb = sb("identb", [P, P], BF16)
        passes = sb("passes", [P, 2], mybir.dt.int32)
        gslot = sb("gslot", [P, 1])
        wsm = sb("wsm", [P, KC, 32])
        wrt = sb("wrt", [P, KC, NE])

        stat_used = [0]
        stat = sb("stat", [P, 1000])

        def stats(n):
            lo = stat_used[0]
            stat_used[0] += n
            assert stat_used[0] <= 1000
            return stat[:, lo:lo + n]

        A_WORDS = 45056
        arena = sb("arena", [P, A_WORDS])

        def at(lo, n):
            assert lo + n <= A_WORDS
            return arena[:, lo:lo + n]

        wring = [at(i * KC * WT, KC * WT).rearrange("p (c n) -> p c n", c=KC) for i in range(A_SLOTS)]
        R1 = A_SLOTS * KC * WT
        R2, RZ, RF = R1 + 6144, R1 + 12288, R1 + 14336
        TDT = RF + 6144
        TLT, TMT, TX, TV, TPB = (TDT + 2048 * i for i in range(1, 6))

        def prob(lo, n=16):
            return at(lo, n * P).rearrange("p (b t) -> p b t", b=n)

        qkvT = prob(R1, 48).rearrange("p (c n) t -> p c (n t)", n=NT)
        qk = at(R2, 4096).rearrange("p (n c) -> p n c", n=NT)
        vbeta = prob(R2 + 4096)
        zs = at(RZ, 2048).rearrange("p (n c) -> p n c", n=NT)
        fox = at(RF, 6144).rearrange("p (n c) -> p n c", n=NT)
        dT, lT, mT, xi, vi, pb = (prob(t) for t in (TDT, TLT, TMT, TX, TV, TPB))
        rows = at(TMT, P)
        xn = at(TPB, 2048).rearrange("p (n c) -> p n c", n=NT)
        sq = at(TMT, 2048)
        gd, bd = prob(TX), prob(TV)
        blocks = prob(TV, 8)
        kbe = prob(TLT, 8)
        s1 = prob(TLT + 1024, 8)
        qgT, wTn = prob(TX, 8), prob(TX + 1024, 8)
        u0, u1 = prob(TPB, 8), prob(TPB + 1024, 8)
        oa = at(TMT, 2048).rearrange("p (n c) -> p n c", n=NT)
        oT = at(R2 + 4096, 2048).rearrange("p (c t) -> p c t", c=KC)
        merge = at(R2, 4096).rearrange("p (n c) -> p n c", n=NT)
        foxT = at(R1, 4096).rearrange("p (c t) -> p c t", c=16)
        scores = [at(RF + 384 * i, 384) for i in range(4)]
        probsT = [at(RF + 3072 + 384 * i, 384) for i in range(2)]
        cbm = at(TDT, 6144).rearrange("p (f k) -> p f k", f=FH)
        cd = at(TX, 4096).rearrange("p (f k) -> p f k", f=FH)
        ofT = at(RZ, 2048).rearrange("p (c t) -> p c t", c=KC)
        mix = at(R1 + 4096, 2048).rearrange("p (n c) -> p n c", n=NT)
        mixf = at(TV, 2048).rearrange("p (n c) -> p n c", n=NT)
        mixT = at(TPB, 2048).rearrange("p (c t) -> p c t", c=KC)

        pair_at = [PAIR_WORDS, 0]
        ering = [at(lo, PAIR_WORDS) for lo in pair_at]
        gu_in = [r[:, 0:4 * EW].rearrange("p (m e w) -> p m e w", m=2, e=2) for r in ering]
        d_in = [r[:, 4 * EW:6 * EW].rearrange("p (e w) -> p e w", e=2) for r in ering]
        B0 = 2 * PAIR_WORDS
        hparts = at(B0, 3072).bitcast(BF16).rearrange("p (k n c) -> p k n c", k=3, n=NT)
        e_t = at(B0 + 3072, 2048).rearrange("p (n c) -> p n c", n=NT)
        ngain = at(B0 + 2048, D)
        xg = at(B0 + 5120, D).rearrange("p (c s) -> p c s", c=KC)
        y = at(B0 + 6144, D)
        wple = at(B0 + 5120, 2048).rearrange("p (c d) -> p c d", c=2)
        spread = [at(B0 + 7168 + 256 * i, 256).rearrange("p (n t) -> p n t", n=NT) for i in range(2)]
        p_t = at(B0 + 7168, 512).rearrange("p (n c) -> p n c", n=NT)
        hid, sil = at(B0 + 7680, 256), at(B0 + 7936, 256)
        hidT = at(B0 + 8192, 256).rearrange("p (c t) -> p c t", c=2)
        hn = at(B0 + 8448, 2048).rearrange("p (n c) -> p n c", n=NT)
        gt = hn
        WPG = B0 + 10496
        wpg = [at(WPG + i * KC * WT, KC * WT).rearrange("p (c n) -> p c n", c=KC) for i in range(2)]
        sgw = at(WPG, EW).rearrange("p (c f) -> p c f", c=KC)
        suw = at(WPG + EW, EW).rearrange("p (c f) -> p c f", c=KC)
        sdw = at(WPG + 2 * EW, EW).rearrange("p (c d) -> p c d", c=2)
        shid = [at(WPG + 3 * EW + 256 * i, 256) for i in range(2)]
        ssil = [at(WPG + 3 * EW + 512 + 256 * i, 256) for i in range(2)]
        shidT = [at(WPG + 3 * EW + 1024 + 256 * i, 256).rearrange("p (c t) -> p c t", c=2) for i in range(2)]
        pT = at(B0 + 7680, 512).rearrange("p (c t) -> p c t", c=2)
        plen = at(WPG + 8704, 1024)

        x_loaded = [sem(f"x_loaded{n}") for n in range(NT)]
        rows_loaded, bias_loaded, small_loaded = (sem(s) for s in ("rows_loaded", "bias_loaded", "small_loaded"))
        w_loaded = [sem(f"w_loaded{i}") for i in range(A_SLOTS)]
        router_loaded = sem("router_loaded")
        first_loaded = sem("first_loaded")
        consts = sem("consts")
        masks_made = sem("masks_made")
        filled = [sem(f"filled{i}") for i in range(8)]
        drained = [sem(f"drained{i}") for i in range(8)]
        dve_step, act_step, pool_step = sem("dve_step"), sem("act_step"), sem("pool_step")
        sumsq = sem("sumsq")
        rinv_made = sem("rinv_made")
        xn_ready = sem("xn_ready")
        conv_done = sem("conv_done")
        soft = sem("soft")
        beta_ready = sem("beta_ready")
        logs_ready = sem("logs_ready")
        gstat = sem("gstat")
        geg = sem("geg")
        gd_made, bd_made, cd_made = sem("gd_made"), sem("bd_made"), sem("cd_made")
        qkss, qkrinv, qk_normed = sem("qkss"), sem("qkrinv"), sem("qk_normed")
        d_ready, dexp_ready = sem("d_ready"), sem("dexp_ready")
        d_masked = sem("d_masked")
        m_ready = sem("m_ready")
        scaled = sem("scaled")
        oss, orinv, o_normed = sem("oss"), sem("orinv"), sem("o_normed")
        fss, frinv, f_normed = sem("fss"), sem("frinv"), sem("f_normed")
        smax, sexp, sdiv = sem("smax"), sem("sexp"), sem("sdiv")
        mixed = sem("mixed")
        h_ready = sem("h_ready")
        sig_ready = sem("sig_ready")
        gates_ready = sem("gates_ready")
        p_loaded, plen_loaded = sem("p_loaded"), sem("plen_loaded")
        sdw_loaded = sem("sdw_loaded")
        ess, erinv, e_ready = sem("ess"), sem("erinv"), sem("e_ready")
        shared_loaded, ngain_loaded = sem("shared_loaded"), sem("ngain_loaded")
        gu_loaded = [sem(f"gu_loaded{i}") for i in range(2)]
        d_loaded = [sem(f"d_loaded{i}") for i in range(2)]
        gu_silu = sem("gu_silu")
        hidT_filled, hidT_ready, shared_done = sem("hidT_filled"), sem("hidT_ready"), sem("shared_done")
        parts_ready, gparts_ready = sem("parts_ready"), sem("gparts_ready")
        passes_ready = sem("passes_ready")
        onehot_ready = sem("onehot_ready")
        xa_filled, xb_filled = sem("xa_filled"), sem("xb_filled")
        xa_ready, xb_ready = sem("xa_ready"), sem("xb_ready")
        place_filled, place_ready = sem("place_filled"), sem("place_ready")
        pgu_filled, psilu, phid_ready = sem("pgu_filled"), sem("psilu"), sem("phid_ready")
        phidT_filled, phidT_ready = sem("phidT_filled"), sem("phidT_ready")
        y_filled = [sem("y0_filled"), sem("y1_filled")]
        y_ready = [sem("y0_ready"), sem("y1_ready")]
        spread_made, place_half, onehot_half, iota_moved = (sem(q) for q in ("spread_made", "place_half", "onehot_half", "iota_moved"))
        added = sem("added")
        wpg_loaded = sem("wpg_loaded")
        sg_ready, out_ready, out_stored = sem("sg_ready"), sem("out_ready"), sem("out_stored")
        pg_filled = sem("pg_filled")

        fills = bank_fills()
        place = {name: (i % 8, i // 8) for i, name in enumerate(fills)}

        def ps(name):
            return bank[place[name][0]]

        def wait_filled(eng, name):
            b, turn = place[name]
            eng.wait_ge(filled[b], turn + 1)

        def wait_drained(eng, name):
            b, turn = place[name]
            eng.wait_ge(drained[b], turn + 1)

        w_in2, = (w_in[0],)
        wtiles = [(w_in2, C_QKV + WT * t, f"qkv.{2 * t + 1}") for t in range(6)]
        wtiles += [(w_in2, C_FOX + WT * j, f"fox.{j}.1") for j in range(6)]
        wtiles += [(w_in2, C_Z + WT * j, f"z.{j}.1") for j in range(2)]
        wtiles += [(w_in2, C_MERGE + WT * j, f"merge.{j}.1") for j in range(4)]
        wtiles += [(w_branch_gdn[0], WT * j, f"ya.{j}.1") for j in range(2)]
        wtiles += [(w_branch_fox[0], WT * j, f"yf.{j}.1") for j in range(2)]
        wtiles += [(w_out[0], WT * j, f"wo.{j}.1") for j in range(2)]
        W_QKV, W_FOX, W_Z, W_MERGE, W_YA, W_YF, W_WO = 0, 6, 12, 14, 18, 20, 22

        block = ctx.enter_context(nc.Block())

        ss_x = [stats(NT) for _ in range(3)]
        rinv_x = [stats(NT) for _ in range(3)]
        u_s = stats(64).rearrange("p (n c) -> p n c", n=NT)
        l_s = stats(64).rearrange("p (n c) -> p n c", n=NT)
        t_s = stats(64).rearrange("p (n c) -> p n c", n=NT)
        beta = stats(16).rearrange("p (n c) -> p n c", n=NT)
        la = stats(48).rearrange("p (n c) -> p n c", n=NT)
        cs = stats(96)
        gb = stats(32)
        gtail = stats(16)
        eg_s = stats(16)
        et_s = stats(16)
        be_s = stats(16)
        cf = stats(32).rearrange("p (n c) -> p n c", n=NT)
        gbT = stats(256)
        qk_ss = stats(32).rearrange("p (n c) -> p n c", n=NT)
        qk_ri = stats(32).rearrange("p (n c) -> p n c", n=NT)
        cT = gbT
        mx = stats(64)
        o_ss, o_ri = stats(16), stats(16)
        f_ss = sb("f_ss", [P, NT, 32])
        f_ri = sb("f_ri", [P, NT, 32])
        den = sb("den", [P, 32])
        dri = sb("dri", [P, 32])
        smallw = wsm[:, :, :].rearrange("p c n -> p (c n)")
        sg = smallw[:, 0:NT * NE].rearrange("p (n e) -> p n e", n=NT)
        sel = smallw[:, NT * NE:2 * NT * NE].rearrange("p (n e) -> p n e", n=NT)
        gates = gbT[:, 0:NT * NE].rearrange("p (n e) -> p n e", n=NT)
        chosen = gbT[:, NT * NE:2 * NT * NE].rearrange("p (n e) -> p n e", n=NT)
        top = sb("top", [P, NT, 8])
        gsum = sb("gsum", [P, NT, 2])
        e_ss, e_ri = sb("e_ss", [P, NT]), sb("e_ri", [P, NT])

        @block.sync
        def _(sp):
            for n in range(NT):
                sp.dma_start(h[:, n, :], x[0, n * P:n * P + P, :]).then_inc(x_loaded[n], 16)
            rv = rows
            sp.dma_start(rv[R_CONV:R_NMIX, :], conv_w[0].rearrange("i (c q) -> (i c) q", q=P)).then_inc(rows_loaded, 16)
            for r, v in ((R_NMIX, norm_mix), (R_NPG, ple_gate_norm)):
                sp.dma_start(rv[r:r + 8, :], v.rearrange("a (c q) -> (a c) q", q=P)).then_inc(rows_loaded, 16)
            with nc.allow_non_contiguous_dma(reason="4 KB in all"):
                sp.dma_start(rv[R_NFFN:R_NFFN + 8, :], norm_ffn.rearrange("a (q c) -> (a c) q", q=P)).then_inc(rows_loaded, 16)
            sp.dma_start(rv[R_GDN:R_GDN + 1, :], gdn_norm).then_inc(rows_loaded, 16)
            for r, v in ((R_QN, q_norm), (R_KN, k_norm)):
                for half in range(2):
                    sp.dma_start(rv[r:r + 1, FD * half:FD * half + FD], v).then_inc(rows_loaded, 16)

            def load(t):
                src, c0, _ = wtiles[t]
                view = src.rearrange("(c q) n -> q c n", q=P)
                if t == 0:
                    sp.dma_start(wring[0][:, :, 0:S], view[:, :, c0:c0 + S]).then_inc(first_loaded, 16)
                    sp.dma_start(wring[0][:, :, S:WT], view[:, :, c0 + S:c0 + WT]).then_inc(w_loaded[0], 16)
                    return
                if t >= A_SLOTS:
                    wait_filled(sp, wtiles[t - A_SLOTS][2])
                sp.dma_start(wring[t % A_SLOTS], view[:, :, c0:c0 + WT]).then_inc(w_loaded[t % A_SLOTS], 16)

            load(0)
            wv = w_in2.rearrange("(c q) n -> q c n", q=P)
            sp.dma_start(wsm[:, :, 0:16], wv[:, :, C_AB:C_AB + 16]).then_inc(small_loaded, 16)
            sp.dma_start(wsm[:, :, 16:32], wv[:, :, C_F:C_F + 16]).then_inc(small_loaded, 16)
            sp.dma_start(bias3[:, 0:8], dt_bias.to_broadcast([P, 8])).then_inc(bias_loaded, 16)
            sp.dma_start(bias3[:, 16:32], fox_f_bias.to_broadcast([P, 16])).then_inc(bias_loaded, 16)
            sp.dma_start(nega[:, :], a_log.to_broadcast([P, 8])).then_inc(bias_loaded, 16)
            for t in (1, 2):
                load(t)
            sp.dma_start(wrt[:, :, :], w_router[0].rearrange("(q c) n -> q c n", q=P)).then_inc(router_loaded, 16)
            sp.dma_start(rbias[:, :], router_bias.to_broadcast([P, NE])).then_inc(router_loaded, 16)
            for t in range(3, len(wtiles) - 1):
                load(t)

            for g in range(8):
                wait_drained(sp, f"pv.{g}")
            sp.dma_start(p_t, p[0, 0].rearrange("(n q) c -> q n c", q=P)).then_inc(p_loaded, 16)
            sp.dma_start(wple, w_ple[0].rearrange("(c q) d -> q c d", q=P)).then_inc(p_loaded, 16)
            sp.dma_start(ngain, norm_ffn.to_broadcast([P, D])).then_inc(ngain_loaded, 16)
            sp.dma_start(sgw, ws_gate[0].rearrange("(q c) f -> q c f", c=KC)).then_inc(shared_loaded, 16)
            sp.dma_start(suw, ws_up[0].rearrange("(q c) f -> q c f", c=KC)).then_inc(shared_loaded, 16)
            load(len(wtiles) - 1)

            def load_pair(s, pick, gu_free=None, d_free=None):
                if gu_free is not None:
                    sp.wait_ge(pgu_filled, gu_free)
                for m, w in enumerate((we_gate, we_up)):
                    sp.dma_start(gu_in[s][:, m], w[0, pick].rearrange("e (q c) f -> q e (c f)", c=KC)).then_inc(gu_loaded[s], 16)
                if d_free is not None:
                    sp.wait_ge(y_filled[1], d_free)
                sp.dma_start(d_in[s], we_down[0, pick].rearrange("e (q c) d -> q e (c d)", c=2)).then_inc(d_loaded[s], 16)

            for n in range(NT):
                wait_drained(sp, f"mT.{n}.1")
            load_pair(0, slice(0, 2))
            sp.dma_start(sdw, ws_down[0].rearrange("(q c) d -> q c d", c=2)).then_inc(sdw_loaded, 16)
            wait_filled(sp, "wo.1.0")
            wait_filled(sp, "wo.1.1")
            sp.dma_start(plen, ple_norm.to_broadcast([P, D])).then_inc(plen_loaded, 16)
            load_pair(1, slice(2, 4))
            with sp.Fori(0, PAIRS // 2 - 1) as k:
                for s in range(2):
                    load_pair(s, bass.ds(k * 4 + (4 + 2 * s), 2), k * 2 + (s + 1), k * 2 + (s + 1))
            sp.wait_ge(passes_ready, 1)
            np_sp = sp.value_load(passes[0:1, 0:1], min_val=1, max_val=S // CAP)
            with sp.If(np_sp > 1):
                with sp.Fori(1, np_sp) as r:
                    with sp.Fori(0, PAIRS // 2) as k:
                        for s in range(2):
                            free = r * PAIRS + k * 2 + (s - 1)
                            load_pair(s, bass.ds(k * 4 + 2 * s, 2), free, free)
            for n in range(NT):
                for j in range(2):
                    sp.wait_ge(out_ready, 2 * n + j + 1)
                    sp.dma_start(out[0, n * P:(n + 1) * P, WT * j:WT * j + WT], gt[:, n, WT * j:WT * j + WT]).then_inc(out_stored, 16)
            sp.wait_ge(out_stored, 16 * 2 * NT)

        @block.gpsimd
        def _(pool):
            g = nc.gpsimd
            steps = [0]

            def seq(ins):
                steps[0] += 1
                ins.then_inc(pool_step, 1)
                pool.wait_ge(pool_step, steps[0])

            def select(t, src, op, fill, base, pattern, mult):
                return g.affine_select(out=t, in_=src, compare_op=op, fill=fill, base=base, pattern=pattern, channel_multiplier=mult)

            g.memset(ident[:, :], 0.0).then_inc(pool_step, 1)
            g.memset(ones[:, :], 1.0).then_inc(pool_step, 1)
            g.memset(nhalf[:, :], -0.5).then_inc(pool_step, 1)
            g.memset(bias3[:, 8:16], 0.0).then_inc(pool_step, 1)
            g.memset(negm[:, :], 0.0).then_inc(pool_step, 1)
            steps[0] = 5
            pool.wait_ge(pool_step, 5)
            select(ident[:, :], ident[:, :], ALU.not_equal, 1.0, 0, [[-1, P]], 1).then_inc(consts, 1)
            g.iota(iota[:, :], [[1, CAP]], base=0, channel_multiplier=0, allow_small_or_imprecise_dtypes=True).then_inc(consts, 1)
            pool.wait_ge(consts, 1)

            def roots(k):
                for n in range(NT):
                    pool.wait_ge(sumsq, NT * k + n + 1)
                    seq(g.tensor_scalar(rinv_x[k][:, n:n + 1], ss_x[k][:, n:n + 1], 1.0 / D, EPS, ALU.mult, ALU.add))
                    g.tensor_tensor(rinv_x[k][:, n:n + 1], rinv_x[k][:, n:n + 1], nhalf[:, 0:1], ALU.pow).then_inc(rinv_made, 1)
            roots(0)
            g.tensor_copy(identb[:, :], ident[:, :]).then_inc(consts, 1)
            select(tri[:, :], ones[:, :], ALU.is_ge, 0.0, 0, [[1, P]], -1).then_inc(consts, 1)
            select(stri[:, :], ones[:, :], ALU.is_gt, 0.0, 0, [[1, P]], -1).then_inc(consts, 1)
            select(negm[:, :], negm[:, :], ALU.is_ge, MASKED, 0, [[-1, P]], 1).then_inc(consts, 1)
            for lv in range(LEVELS + 1):
                b = 1 << lv
                nb = P // b
                v = blocks[:, lv, :].rearrange("p (k w) -> p k w", w=b)
                seq(select(v, ones[:, :].rearrange("p (k w) -> p k w", w=b), ALU.is_ge, 0.0, 0, [[-b, nb], [0, b]], 1)) if lv < LEVELS else seq(g.tensor_copy(blocks[:, lv, :], ones[:, :]))
                if lv < LEVELS:
                    seq(select(v, v, ALU.is_ge, 0.0, b - 1, [[b, nb], [0, b]], -1))
            for lv in range(LEVELS):
                g.tensor_tensor(lmask[:, lv, :], blocks[:, lv + 1, :], blocks[:, lv, :], ALU.subtract).then_inc(masks_made, 1)
            wait_drained(pool, "gbT")
            pool.wait_ge(masks_made, LEVELS)
            for j in range(4):
                for n in range(NT):
                    i = NT * j + n
                    pool.wait_ge(qkss, i + 1)
                    v = qk_ri[:, n, 4 * j:4 * j + 4]
                    seq(g.tensor_scalar(v, qk_ss[:, n, 4 * j:4 * j + 4], 1.0, EPS, ALU.mult, ALU.add))
                    ins = g.tensor_tensor(v, v, nhalf[:, 0:4], ALU.pow)
                    if j < 2:
                        seq(ins)
                        ins = g.tensor_scalar(v, v, DK ** -0.5, 0.0, ALU.mult, ALU.add)
                    ins.then_inc(qkrinv, 1)
            for t, lo, s in ((gd, 0, gd_made), (bd, P, bd_made)):
                src = bc(gbT[0:16, lo:lo + P], 1, 16)
                select(t[0:16], src, ALU.is_equal, 0.0, 0, [[-1, 16], [0, P]], 1).then_inc(s, 1)
            for n in range(NT):
                pool.wait_ge(fss, n + 1)
                seq(g.tensor_scalar(f_ri[:, n, :], f_ss[:, n, :], 1.0 / FD, EPS, ALU.mult, ALU.add))
                g.tensor_tensor(f_ri[:, n, :], f_ri[:, n, :], nhalf[:, :], ALU.pow).then_inc(frinv, 1)
            wait_drained(pool, "cT")
            for j in range(2):
                wait_filled(pool, f"o1.{j}")
            select(cd[0:16], bc(cT[0:16, :], 1, 16), ALU.is_equal, 0.0, 0, [[-1, 16], [0, S]], 1).then_inc(cd_made, 1)
            pool.wait_ge(oss, 1)
            seq(g.tensor_scalar(o_ri, o_ss, 1.0 / DK, EPS, ALU.mult, ALU.add))
            g.tensor_tensor(o_ri, o_ri, nhalf[:, 0:16], ALU.pow).then_inc(orinv, 1)
            roots(1)
            for n in range(NT):
                pool.wait_ge(ess, n + 1)
                seq(g.tensor_scalar(e_ri[:, n:n + 1], e_ss[:, n:n + 1], 1.0 / D, EPS, ALU.mult, ALU.add))
                g.tensor_tensor(e_ri[:, n:n + 1], e_ri[:, n:n + 1], nhalf[:, 0:1], ALU.pow).then_inc(erinv, 1)
            roots(2)

        @block.scalar
        def _(act):
            a = nc.scalar
            steps = [0]

            def seq(ins):
                steps[0] += 1
                ins.then_inc(act_step, 1)
                act.wait_ge(act_step, steps[0])

            def squares(k, src, junk, ready=None):
                for n in range(NT):
                    if ready is None:
                        act.wait_ge(x_loaded[n], 16)
                    else:
                        act.wait_ge(h_ready, ready[n])
                    a.activation(junk[:, n, :], src[:, n, :], ACT.Square, accum_out=ss_x[k][:, n:n + 1]).then_inc(sumsq, 1)

            def drain(name, dst, func=ACT.Copy, cols_used=512, **kw):
                wait_filled(act, name)
                a.activation(dst, ps(name)[:, 0:cols_used] if len(dst.shape) == 2 else
                             ps(name)[:, 0:cols_used].rearrange("p (a b) -> p a b", a=dst.shape[1]), func, **kw).then_inc(drained[place[name][0]], 1)

            squares(0, h, xn)
            act.wait_ge(logs_ready, 1)
            seq(a.activation(t_s, t_s, ACT.Exp, scale=-1.0))
            a.activation(l_s, t_s, ACT.Ln, bias=1.0).then_inc(soft, 1)
            a.activation(beta, u_s[:, :, 8:16], ACT.Exp, scale=-1.0).then_inc(soft, 1)
            a.activation(nega[:, :], nega[:, :], ACT.Exp).then_inc(soft, 1)
            for c in range(12):
                wait_drained(act, f"qkv.{c}")
                v = qkvT[:, 2 * c:2 * c + 2, :]
                a.activation(v, v, ACT.Silu).then_inc(conv_done, 1)
            for j in range(4):
                for n in range(NT):
                    drain(f"tq.{n}.{j}", qk[:, n, WT * j:WT * j + WT])
            act.wait_ge(gstat, 1)
            a.activation(eg_s, gb[:, 0:16], ACT.Exp).then_inc(geg, 1)
            a.activation(et_s, gtail, ACT.Exp).then_inc(geg, 1)
            for j in range(4):
                for n in range(NT):
                    drain(f"fox.{j}.{n}", fox[:, n, WT * j:WT * j + WT])
            for j in range(4):
                act.wait_ge(d_ready, j + 1)
                a.activation(dT[:, 4 * j:4 * j + 4, :], dT[:, 4 * j:4 * j + 4, :], ACT.Exp).then_inc(dexp_ready, 1)
            for j in range(4, 6):
                for n in range(NT):
                    drain(f"fox.{j}.{n}", fox[:, n, WT * j:WT * j + WT])
            for n in range(NT):
                for j in range(4):
                    drain(f"tk.{n}.{j}", qkvT[:, 4 * j:4 * j + 4, n * P:n * P + P])
            for n in range(NT):
                drain(f"z.0.{n}", zs[:, n, 0:WT], ACT.Silu)
            for lv in range(1, LEVELS):
                for j in range(4):
                    drain(f"P.{lv}.{j}", pb[:, 4 * j:4 * j + 4, :])
                if lv < LEVELS - 1:
                    for j in range(4):
                        wait_filled(act, f"X.{lv}.{j}")
                        drain(f"V.{lv}.{j}", vi[:, 4 * j:4 * j + 4, :])
            for n in range(NT):
                drain(f"z.1.{n}", zs[:, n, WT:2 * WT], ACT.Silu)
            for j in range(2):
                hs = slice(4 * j, 4 * j + 4)
                drain(f"tg.{j}", qgT[:, hs, :])
                drain(f"wT.{j}", wTn[:, hs, :], scale=-1.0)
                drain(f"u0.{j}", u0[:, hs, :])
            for j in range(2):
                drain(f"o0.{j}", oa[:, 0, WT * j:WT * j + WT])
                drain(f"s1.{j}", s1[:, 4 * j:4 * j + 4, :])
            for j in range(2):
                drain(f"u1.{j}", u1[:, 4 * j:4 * j + 4, :])
            for j in range(2):
                drain(f"o1.{j}", oa[:, 1, WT * j:WT * j + WT])
            def gate(j, n):
                drain(f"merge.{j}.{n}", merge[:, n, WT * j:WT * j + WT], ACT.Sigmoid)

            for j in range(2):
                for n in range(NT):
                    gate(j, n)
            for n in range(NT):
                for j in range(2):
                    drain(f"oT.{n}.{j}", oT[:, 4 * j:4 * j + 4, n * P:n * P + P], scale=cols[:, R_GDN:R_GDN + 1])
            for n in range(NT):
                for j in range(4):
                    r = R_QN if j < 2 else R_KN
                    drain(f"fT.{n}.{j}", foxT[:, 4 * j:4 * j + 4, n * P:n * P + P], scale=cols[:, r:r + 1])
            def exponentials(g):
                for f in (2 * g, 2 * g + 1):
                    act.wait_ge(smax, 2 * f + 2)
                    for n in range(NT):
                        v = scores[f % 4][:, P:3 * P] if n else scores[f % 4][:, 0:P]
                        a.activation(v, v, ACT.Exp, bias=mx[:, 2 * f + n:2 * f + n + 1], accum_out=den[:, 2 * f + n:2 * f + n + 1]).then_inc(sexp, 1)

            gate(2, 0)
            exponentials(0)
            for g in range(8):
                if g < 7:
                    exponentials(g + 1)
                if g < 3:
                    gate(*((2, 1), (3, 0), (3, 1))[g])
                for f in (2 * g, 2 * g + 1):
                    if g > 0:
                        wait_filled(act, f"pv.{g - 1}")
                    drain(f"pT.{f}", probsT[f % 2], cols_used=384)
                drain(f"pv.{g}", ofT[:, g, :], cols_used=S)
            for n in range(NT):
                drain(f"pT2.{n}", pT[:, :, n * P:n * P + P], cols_used=S)

            def embedding(n, j):
                drain(f"e.{n}.{j}", e_t[:, n, WT * j:WT * j + WT])

            embedding(0, 0)
            for n in range(NT):
                for j in range(2):
                    drain(f"mT.{n}.{j}", mixT[:, 4 * j:4 * j + 4, n * P:n * P + P])
            squares(1, h, hn, (3, 4))
            embedding(0, 1)
            embedding(1, 0)
            for n in range(NT):
                for j in range(2):
                    drain(f"hT.{n}.{j}", actT[:, 4 * j:4 * j + 4, n * P:n * P + P])
            embedding(1, 1)
            drain("router", sg[:, :, :], ACT.Sigmoid, cols_used=P)
            for n in range(NT):
                act.wait_ge(xn_ready, NT + n + 1)
                a.activation(hparts[:, 0, n, :], hn[:, n, :], ACT.Copy).then_inc(parts_ready, 1)
            for n in range(NT):
                wait_filled(act, f"sh.{n}")
                a.activation(ssil[n], ps(f"sh.{n}")[:, 0:DE], ACT.Silu).then_inc(gu_silu, 1)
            act.wait_ge(parts_ready, 2 * NT)
            for n in range(NT):
                for j in range(2):
                    wait_drained(act, f"e.{n}.{j}")
                a.activation(hn[:, n, :], e_t[:, n, :], ACT.Square, accum_out=e_ss[:, n:n + 1]).then_inc(ess, 1)
            for n in range(NT):
                act.wait_ge(hidT_filled, n + 1)
                a.activation(shidT[n], bank[6 + n][:, 0:DE].rearrange("p (c t) -> p c t", c=2), ACT.Copy).then_inc(hidT_ready, 1)
            def gathered(t):
                act.wait_ge(xa_filled, t)
                a.activation(xg[:, 0:4, :], bank[5][:, :].rearrange("p (c s) -> p c s", c=4), ACT.Copy).then_inc(xa_ready, 1)

            gathered(1)
            act.wait_ge(shared_done, 1)
            act.wait_ge(e_ready, NT)
            for j in range(2):
                act.dma_start(wpg[j], w_ple_gate[0].rearrange("(c q) n -> q c n", q=P)[:, :, WT * j:WT * j + WT]).then_inc(wpg_loaded, 16)
            act.wait_ge(passes_ready, 1)
            np_act = act.value_load(passes[0:1, 1:2], min_val=PAIRS // 2, max_val=PAIRS // 2 * (S // CAP))
            with act.Fori(0, np_act) as k:
                for s in range(2):
                    t = k * 2 + (s + 1)
                    act.wait_ge(pgu_filled, t)
                    a.activation(sil, bank[4][:, 0:DE], ACT.Silu).then_inc(psilu, 1)
                    act.wait_ge(phidT_filled, t)
                    a.activation(hidT, bank[7][:, 0:DE].rearrange("p (c t) -> p c t", c=2), ACT.Copy).then_inc(phidT_ready, 1)
                    gathered(k * 2 + (s + 2))
                    act.wait_ge(y_filled[0], t)
                    a.activation(y[:, 0:WT], bank[4][:, :], ACT.Copy).then_inc(y_ready[0], 1)
            squares(2, h, hn, (6, 8))
            for n in range(NT):
                act.wait_ge(rinv_made, 2 * NT + n + 1)
                for j in range(2):
                    act.wait_ge(pg_filled, NT * n + j + 1)
                    a.activation(gt[:, n, WT * j:WT * j + WT], bank[4 + NT * j + n][:, :], ACT.Sigmoid, scale=rinv_x[2][:, n:n + 1]).then_inc(sg_ready, 1)

        @block.tensor
        def _(pe):
            t = nc.tensor

            def open_bank(name):
                b, turn = place[name]
                if turn > 0:
                    pe.wait_ge(drained[b], turn)
                return bank[b]

            def close(ins, name):
                ins.then_inc(filled[place[name][0]], 1)

            def transposes(name, srcs, rows_in=P):
                o = open_bank(name)
                for i, v in enumerate(srcs):
                    w = v.shape[1]
                    ins = t.transpose(o[0:w, i * P:i * P + rows_in], v, ident[0:rows_in, 0:rows_in])
                close(ins, name)

            def project(name, w, n, lhs=actT):
                o = open_bank(name)
                for c in range(KC):
                    ins = t.matmul(o[:, :], lhs[:, c, n * P:n * P + P], w[:, c, :], start=(c == 0), stop=(c == KC - 1))
                close(ins, name)

            def weights(k):
                pe.wait_ge(w_loaded[k % A_SLOTS], 16 * (k // A_SLOTS + 1))
                return wring[k % A_SLOTS]

            pe.wait_ge(consts, 1)
            for n in range(NT):
                pe.wait_ge(xn_ready, n + 1)
                for j in range(2):
                    transposes(f"xT.{n}.{j}", [xn[:, n, P * c:P * c + P] for c in range(4 * j, 4 * j + 4)])
                if n == 0:
                    pe.wait_ge(rows_loaded, 16 * 9)
                    transposes("cols", [rows[0:R_ALL, :]], R_ALL)
            for n in range(NT):
                for j in range(2):
                    wait_drained(pe, f"xT.{n}.{j}")
            for c2 in range(12):
                if c2 == 0:
                    pe.wait_ge(first_loaded, 16)
                    w = wring[0]
                else:
                    w = weights(W_QKV + c2 // 2)
                o = open_bank(f"qkv.{c2}")
                for i in range(2):
                    col = (2 * c2 + i) % 4 * P
                    for c in range(KC):
                        ins = t.matmul(o[:, i * S:i * S + S], w[:, c, col:col + P], actT[:, c, :], start=(c == 0), stop=(c == KC - 1))
                close(ins, f"qkv.{c2}")
                if c2 == 1:
                    pe.wait_ge(small_loaded, 32)
                    o = open_bank("small")
                    for n in range(NT):
                        for c in range(KC):
                            ins = t.matmul(o[:, 32 * n:32 * n + 32], actT[:, c, n * P:n * P + P], wsm[:, c, :], start=(c == 0), stop=(c == KC - 1))
                    close(ins, "small")
                if c2 == 2:
                    pe.wait_ge(logs_ready, 2)
                    pe.wait_ge(consts, 6)
                    o = open_bank("cum")
                    for k, m in enumerate((tri, ones)):
                        for n in range(NT):
                            lo = 48 * k + 24 * n
                            ins = t.matmul(o[:, lo:lo + 24], m[:, :], la[:, n, :], start=True, stop=True)
                    close(ins, "cum")
                if c2 == 3:
                    pe.wait_ge(gstat, 1)
                    transposes("gbT", [gb[:, 0:16], gb[:, 16:32]])

            def convolved(name):
                n, j = (int(i) for i in name.split(".")[1:])
                pe.wait_ge(conv_done, 2 * j + 2)
                transposes(name, [qkvT[:, c, n * P:n * P + P] for c in range(4 * j, 4 * j + 4)])

            def spread_rows(name):
                kind, j = name.split(".")
                src, s = (gd, gd_made) if kind == "gb" else (bd, bd_made)
                pe.wait_ge(s, 1)
                o = open_bank(name)
                close(t.matmul(o[:, :], ones[0:16, :], src[0:16, 4 * int(j):4 * int(j) + 4, :], start=True, stop=True), name)

            for j in range(5):
                for n in range(NT):
                    convolved(f"tq.{n}.{j}")
            for j in range(6):
                w = weights(W_FOX + j)
                for n in range(NT):
                    project(f"fox.{j}.{n}", w, n)
                    for name in BESIDE_FOX.get((j, n), []):
                        (convolved if name.startswith("tq") else spread_rows)(name)
            o = open_bank("cT")
            for n in range(NT):
                ins = t.transpose(o[0:16, n * P:n * P + P], cf[:, n, :], ident[:, :])
            close(ins, "cT")
            pe.wait_ge(qk_normed, 8)
            for n in range(NT):
                for j in range(4):
                    transposes(f"tk.{n}.{j}", [qk[:, n, P * c:P * c + P] for c in range(4 * j, 4 * j + 4)])

            def problems(name, lhs, rhs, hs=range(4)):
                o = open_bank(name)
                for i, b in enumerate(hs):
                    ins = t.matmul(o[:, i * P:i * P + P], lhs(b), rhs(b), start=True, stop=True)
                close(ins, name)

            def qTb(b):
                return qkvT[:, b % GH, b // GH * P:b // GH * P + P]

            def kTb(b):
                return qkvT[:, GH + b % GH, b // GH * P:b // GH * P + P]

            for n in range(NT):
                for j in range(4):
                    wait_drained(pe, f"tk.{n}.{j}")
            for j in range(4):
                bs = range(4 * j, 4 * j + 4)
                problems(f"kk.{j}", kTb, kTb, bs)
                problems(f"qk.{j}", kTb, qTb, bs)
            z_tile = weights(W_Z)
            project("z.0.0", z_tile, 0)
            for lv in range(LEVELS):
                for j in range(4):
                    bs = range(4 * j, 4 * j + 4)
                    pe.wait_ge(m_ready, 4 * lv + j + 1)
                    if lv > 1:
                        wait_drained(pe, f"X.{lv - 1}.{j}")
                    if lv == 1:
                        wait_drained(pe, f"P.0.{j}")
                    if lv == 0:
                        transposes(f"P.0.{j}", [mT[:, b, :] for b in bs])
                    else:
                        problems(f"P.{lv}.{j}", lambda b: mT[:, b, :], lambda b: xi[:, b, :], bs)
                if lv == 0:
                    project("z.0.1", z_tile, 1)
                    continue
                for q, j in XV_ORDER if lv < LEVELS - 1 else [("V", j) for j in range(4)]:
                    bs = range(4 * j, 4 * j + 4)
                    wait_drained(pe, f"P.{lv}.{j}")
                    if q == "X":
                        if lv > 1:
                            wait_drained(pe, f"V.{lv - 1}.{j}")
                        problems(f"X.{lv}.{j}", lambda b: vi[:, b, :], lambda b: pb[:, b, :], bs)
                    elif lv < LEVELS - 1:
                        wait_drained(pe, f"X.{lv}.{j}")
                        transposes(f"V.{lv}.{j}", [xi[:, b, :] for b in bs])
                    else:
                        wait_drained(pe, f"V.{lv - 1}.{j}")
                        problems(f"V.{lv}.{j}", lambda b: pb[:, b, :], lambda b: vi[:, b, :], bs)
            w = weights(W_Z + 1)
            for n in range(NT):
                project(f"z.1.{n}", w, n)
            for j in range(4):
                wait_drained(pe, f"V.{LEVELS - 1}.{j}")
            pe.wait_ge(scaled, 3)
            for j in range(2):
                hs = range(4 * j, 4 * j + 4)
                transposes(f"tg.{j}", [qk[:, 1, P * c:P * c + P] for c in hs])
                problems(f"wT.{j}", lambda b: kbe[:, b, :], lambda b: vi[:, GH + b, :], hs)
                problems(f"u0.{j}", lambda b: vi[:, b, :], lambda b: vbeta[:, b, :], hs)
            for j in range(2):
                hs = range(4 * j, 4 * j + 4)
                wait_drained(pe, f"u0.{j}")
                problems(f"o0.{j}", lambda b: dT[:, b, :], lambda b: u0[:, b, :], hs)
                problems(f"s1.{j}", lambda b: qk[:, 0, D + P * b:D + P * b + P], lambda b: u0[:, b, :], hs)

            def two(name, terms, hs):
                o = open_bank(name)
                for i, b in enumerate(hs):
                    for k, (lhs, rhs) in enumerate(terms):
                        ins = t.matmul(o[:, i * P:i * P + P], lhs(b), rhs(b), start=(k == 0), stop=(k == 1))
                close(ins, name)

            for j in range(2):
                wait_drained(pe, f"wT.{j}")
                wait_drained(pe, f"s1.{j}")
                two(f"u1.{j}", [(lambda b: vi[:, GH + b, :], lambda b: vbeta[:, GH + b, :]),
                                (lambda b: wTn[:, b, :], lambda b: s1[:, b, :])], range(4 * j, 4 * j + 4))
            for j in range(2):
                wait_drained(pe, f"tg.{j}")
                wait_drained(pe, f"u1.{j}")
                two(f"o1.{j}", [(lambda b: qgT[:, b, :], lambda b: s1[:, b, :]),
                                (lambda b: dT[:, GH + b, :], lambda b: u1[:, b, :])], range(4 * j, 4 * j + 4))

            def key_decays(*js):
                pe.wait_ge(cd_made, 1)
                for j in js:
                    o = open_bank(f"cb.{j}")
                    close(t.matmul(o[:, :], ones[0:16, :], cd[0:16, 2 * j:2 * j + 2, :], start=True, stop=True), f"cb.{j}")

            w = weights(W_MERGE)
            project("merge.0.0", w, 0)
            project("merge.0.1", w, 1)
            key_decays(0)
            w = weights(W_MERGE + 1)
            project("merge.1.0", w, 0)
            key_decays(1, 2)
            project("merge.1.1", w, 1)
            key_decays(3, 4)
            for n in range(NT):
                pe.wait_ge(o_normed, n + 1)
                for j in range(2):
                    transposes(f"oT.{n}.{j}", [oa[:, n, P * c:P * c + P] for c in range(4 * j, 4 * j + 4)])
            for n in range(NT):
                pe.wait_ge(f_normed, n + 1)
                for j in range(4):
                    transposes(f"fT.{n}.{j}", [fox[:, n, P * c:P * c + P] for c in range(4 * j, 4 * j + 4)])
            key_decays(5)
            for n in range(NT):
                for j in range(2):
                    wait_drained(pe, f"oT.{n}.{j}")
            project("merge.2.0", weights(W_MERGE + 2), 0)
            key_decays(6, 7)
            for n in range(NT):
                for j in range(4):
                    wait_drained(pe, f"fT.{n}.{j}")

            def products(g):
                o = [open_bank(f"s.{2 * g + i}") for i in range(2)]
                for i in range(2):
                    hp = slice(FD * i, FD * i + FD)
                    t.matmul(o[i][:, 0:P], foxT[hp, g, 0:P], foxT[hp, 8 + g, 0:P], start=True, stop=True)
                for i in range(2):
                    hp = slice(FD * i, FD * i + FD)
                    close(t.matmul(o[i][:, P:P + S], foxT[hp, g, P:S], foxT[hp, 8 + g, :], start=True, stop=True), f"s.{2 * g + i}")

            products(0)
            products(1)
            for g in range(8):
                if g < 7:
                    kind, j, n = BESIDE_ATTENTION[g].split(".")
                    first, lhs = (W_YA, oT) if kind == "ya" else (W_MERGE, actT)
                    project(BESIDE_ATTENTION[g], weights(first + int(j)), int(n), lhs)
                for f in (2 * g, 2 * g + 1):
                    pe.wait_ge(sdiv, f + 1)
                    transposes(f"pT.{f}", [scores[f % 4][:, k * P:k * P + P] for k in range(3)])
                if g < 6:
                    products(g + 2)
                name = f"pv.{g}"
                o = open_bank(name)
                for f in (2 * g, 2 * g + 1):
                    wait_drained(pe, f"pT.{f}")
                for k, (lo, n) in enumerate(((0, 0), (P, 0), (P, 1))):
                    for i in range(2):
                        c = 2 * D + FD * (2 * g + i)
                        ins = t.matmul(o[FD * i:FD * i + FD, lo:lo + P], fox[:, n, c:c + FD], probsT[i][:, k * P:k * P + P],
                                       start=(k < 2), stop=(k != 1))
                close(ins, name)
            for g in range(8):
                wait_drained(pe, f"pv.{g}")
            for j in range(2):
                w = weights(W_YF + j)
                for n in range(NT):
                    project(f"yf.{j}.{n}", w, n, ofT)
            pe.wait_ge(p_loaded, 32)
            for n in range(NT):
                transposes(f"pT2.{n}", [p_t[:, n, 0:P], p_t[:, n, P:S]])
            for n in range(NT):
                wait_drained(pe, f"pT2.{n}")

            def embedding(n, j):
                o = open_bank(f"e.{n}.{j}")
                for c in range(2):
                    ins = t.matmul(o[:, :], pT[:, c, n * P:n * P + P], wple[:, c, WT * j:WT * j + WT], start=(c == 0), stop=(c == 1))
                close(ins, f"e.{n}.{j}")

            embedding(0, 0)
            for n in range(NT):
                pe.wait_ge(mixed, 2 * NT)
                for j in range(2):
                    transposes(f"mT.{n}.{j}", [mix[:, n, P * c:P * c + P] for c in range(4 * j, 4 * j + 4)])
            for n in range(NT):
                for j in range(2):
                    wait_drained(pe, f"mT.{n}.{j}")
            for j in range(2):
                w = weights(W_WO + j)
                for n in range(NT):
                    project(f"wo.{j}.{n}", w, n, mixT)
            embedding(0, 1)
            embedding(1, 0)
            for n in range(NT):
                pe.wait_ge(xn_ready, NT + n + 1)
                for j in range(2):
                    transposes(f"hT.{n}.{j}", [hn[:, n, P * c:P * c + P] for c in range(4 * j, 4 * j + 4)])
            embedding(1, 1)
            for n in range(NT):
                for j in range(2):
                    wait_drained(pe, f"hT.{n}.{j}")
            pe.wait_ge(router_loaded, 32)
            o = open_bank("router")
            for n in range(NT):
                for c in range(KC):
                    ins = t.matmul(o[:, NE * n:NE * n + NE], actT[:, c, n * P:n * P + P], wrt[:, c, :], start=(c == 0), stop=(c == KC - 1))
            close(ins, "router")
            pe.wait_ge(shared_loaded, 32)
            for n in range(NT):
                o = open_bank(f"sh.{n}")
                for w, part in ((sgw, 0), (suw, DE)):
                    for c in range(KC):
                        ins = t.matmul(o[:, part:part + DE], actT[:, c, n * P:n * P + P], w[:, c, :], start=(c == 0), stop=(c == KC - 1))
                close(ins, f"sh.{n}")
            pe.wait_ge(onehot_ready, 1)
            o = open_bank("rank")
            for n in range(NT):
                lo = n * NE
                ins = t.matmul(o[:, lo:lo + NE], stri[:, :], chosen[:, n, :], start=True, stop=(n == 0))
                if n == 1:
                    ins = t.matmul(o[:, lo:lo + NE], ones[:, :], chosen[:, 0, :], start=False, stop=True)
            for n in range(NT):
                ins = t.matmul(o[:, 2 * NE:3 * NE], ones[:, :], chosen[:, n, :], start=(n == 0), stop=(n == 1))
            close(ins, "rank")
            for b in range(8):
                if b != place["rank"][0]:
                    pe.wait_ge(drained[b], len([1 for q in fills if place[q][0] == b]))
            for n in range(NT):
                for c in range(2):
                    ins = t.transpose(bank[6 + n][:, c * P:c * P + P], shid[n][:, c * P:c * P + P], ident[:, :])
                ins.then_inc(hidT_filled, 1)
            pe.wait_ge(sdw_loaded, 16)
            wait_drained(pe, "rank")
            for n in range(NT):
                pe.wait_ge(hidT_ready, n + 1)
                for j in range(2):
                    for c in range(2):
                        ins = t.matmul(bank[2 * n + j][:, :], shidT[n][:, c, :], sdw[:, c, WT * j:WT * j + WT],
                                       start=(c == 0), stop=False, skip_group_check=True)
            ins.then_inc(shared_done, 1)

            def gather(t_):
                pe.wait_ge(onehot_ready, t_ + 1)
                for half, s in ((0, xa_filled), (1, xb_filled)):
                    for c in range(4):
                        for i, (k, n) in enumerate((k, n) for k in range(3) for n in range(NT)):
                            ins = t.matmul(bank[5 + half][:, c * P:c * P + P], hparts[:, k, n, (4 * half + c) * P:(4 * half + c + 1) * P],
                                           onehot[:, n, :], start=(i == 0), stop=(i == 5))
                    ins.then_inc(s, 1)

            def places(e2):
                b16 = bank[7][:, DE:DE + P].bitcast(BF16)
                for n in range(NT):
                    t.transpose(b16[:, n * P:n * P + P], onehot[:, n, :], identb[:, :])
                for n in range(NT):
                    ins = t.matmul(bank[7][:, 400:406], onehot[:, n, :], gparts[:, n, e2, :], start=(n == 0), stop=(n == 1))
                ins.then_inc(place_filled, 1)

            def add_to_tokens(s):
                for n in range(NT):
                    for j in range(2):
                        ins = t.matmul(bank[2 * n + j][:, :], spread[s][:, n, :], y[:, WT * j:WT * j + WT],
                                       start=False, stop=False, skip_group_check=True)
                ins.then_inc(added, 1)

            pe.wait_ge(parts_ready, 2 * NT)
            gather(1)
            pe.wait_ge(gparts_ready, 1)
            places(slice(0, 2))
            pe.wait_ge(passes_ready, 1)
            np_pe = pe.value_load(passes[0:1, 0:1], min_val=1, max_val=S // CAP)
            with pe.Fori(0, np_pe) as r:
                with pe.Fori(0, PAIRS // 2) as k:
                    for s in range(2):
                        before = r * PAIRS + k * 2 + s
                        turn = r * (PAIRS // 2) + k + 1
                        pe.wait_ge(gu_loaded[s], turn * 32)
                        pe.wait_ge(xa_ready, before + 1)
                        pe.wait_ge(xb_ready, before + 1)
                        pe.wait_ge(y_ready[0], before + 1)
                        for c in range(KC):
                            for e in range(2):
                                w = gu_in[s][:, :, e, c * DE:c * DE + DE]
                                ins = t.matmul(bank[4][e * CAP:e * CAP + CAP, :], xg[:, c, e * CAP:e * CAP + CAP], w, start=(c == 0), stop=(c == KC - 1))
                        ins.then_inc(pgu_filled, 1)
                        pe.wait_ge(y_ready[1], before + 1)
                        pe.wait_ge(place_ready, before + 1)
                        add_to_tokens(1 - s)
                        pe.wait_ge(phid_ready, before + 1)
                        for c in range(2):
                            ins = t.transpose(bank[7][:, c * P:c * P + P], hid[:, c * P:c * P + P], ident[:, :])
                        ins.then_inc(phidT_filled, 1)
                        gather(before + 2)
                        pe.wait_ge(phidT_ready, before + 1)
                        places(bass.ds(k * 4 + (2 * s + 2), 2))
                        pe.wait_ge(d_loaded[s], turn * 16)
                        for j in range(2):
                            if j == 1:
                                pe.wait_ge(xa_ready, before + 2)
                            for c in range(2):
                                for e in range(2):
                                    ins = t.matmul(bank[4 + j][e * CAP:e * CAP + CAP, :], hidT[:, c, e * CAP:e * CAP + CAP],
                                                   d_in[s][:, e, c * D + WT * j:c * D + WT * j + WT], start=(c == 0), stop=(c == 1))
                            ins.then_inc(y_filled[j], 1)
            last = np_pe * PAIRS
            pe.wait_ge(y_ready[0], last + 1)
            pe.wait_ge(y_ready[1], last + 1)
            pe.wait_ge(place_ready, last + 1)
            for n in range(NT):
                for j in range(2):
                    t.matmul(bank[2 * n + j][:, :], spread[1][:, n, :], y[:, WT * j:WT * j + WT],
                             start=False, stop=True, skip_group_check=True).then_inc(added, 1)
            for n in range(NT):
                pe.wait_ge(h_ready, 4 + 2 * n + 2)
                for j in range(2):
                    for c in range(4):
                        ins = t.transpose(bank[2 * n + j][:, c * P:c * P + P], h[:, n, (4 * j + c) * P:(4 * j + c + 1) * P], ident[:, :])
                    ins.then_inc(hidT_filled, 1)
            pe.wait_ge(wpg_loaded, 32)
            for n in range(NT):
                pe.wait_ge(e_ready, NT + 2 * n + 2)
                for j in range(2):
                    for c in range(KC):
                        ins = t.matmul(bank[4 + NT * j + n][:, :], actT[:, c, n * P:n * P + P], wpg[j][:, c, :], start=(c == 0), stop=(c == KC - 1))
                    ins.then_inc(pg_filled, 1)

        @block.vector
        def _(dve):
            v = nc.vector
            steps = [0]

            def step(ins):
                steps[0] += 1
                ins.then_inc(dve_step, 1)
                return steps[0]

            def seq(ins):
                dve.wait_ge(dve_step, step(ins))

            def close(ins, name):
                ins.then_inc(drained[place[name][0]], 1)

            def blocks4(name, n=4):
                return ps(name)[:, 0:n * P].rearrange("p (a b) -> p a b", a=n)

            def norm(k, dst):
                for n in range(NT):
                    if k == 0:
                        dve.wait_ge(x_loaded[n], 16)
                    dve.wait_ge(rinv_made, NT * k + n + 1)
                    v.tensor_scalar(dst[:, n, :], h[:, n, :], rinv_x[k][:, n:n + 1], None, ALU.mult).then_inc(xn_ready, 1)

            norm(0, xn)
            wait_filled(dve, "cols")
            seq(v.tensor_copy(cols[:, 0:R_ALL], ps("cols")[:, 0:R_ALL]))
            close(v.tensor_scalar(cols[:, R_QN:R_QN + 1], cols[:, R_QN:R_QN + 1], FD ** -0.5, None, ALU.mult), "cols")
            wait_drained(dve, "cols")
            for n in range(NT):
                for j in range(2):
                    nm = f"xT.{n}.{j}"
                    wait_filled(dve, nm)
                    close(v.tensor_tensor(actT[:, 4 * j:4 * j + 4, n * P:n * P + P], blocks4(nm), bc(cols[:, R_NMIX + 4 * j:R_NMIX + 4 * j + 4], 2, P), ALU.mult), nm)
            for c2 in range(12):
                nm = f"qkv.{c2}"
                wait_filled(dve, nm)
                for s in range(4):
                    for i in range(2):
                        ct = 2 * c2 + i
                        wcol = cols[:, R_CONV + 24 * (3 - s) + ct:R_CONV + 24 * (3 - s) + ct + 1]
                        src = ps(nm)[:, i * S:i * S + S - s]
                        dst = qkvT[:, ct, s:S]
                        if s == 0:
                            k = step(v.tensor_scalar(dst, src, wcol, None, ALU.mult))
                        else:
                            dve.wait_ge(dve_step, k - 1 + i if s == 1 else k - 1)
                            ins = v.scalar_tensor_tensor(out=dst, in0=src, scalar=wcol, in1=dst, op0=ALU.mult, op1=ALU.add)
                            if s == 3 and i == 1:
                                close(ins, nm)
                            else:
                                k = step(ins)
                if c2 == 1:
                    dve.wait_ge(bias_loaded, 48)
                    dve.wait_ge(consts, 1)
                    wait_filled(dve, "small")
                    close(v.tensor_tensor(u_s, ps("small")[:, 0:64].rearrange("p (n c) -> p n c", n=NT), bc(bias3[:, :], 1, NT), ALU.add), "small")
                    wait_drained(dve, "small")
                    seq(v.tensor_scalar(t_s, u_s, -1.0, None, ALU.mult))
                    v.tensor_tensor(t_s, t_s, u_s, ALU.max).then_inc(logs_ready, 1)
                    dve.wait_ge(soft, 3)
                    seq(v.tensor_scalar(t_s[:, :, 0:8], u_s[:, :, 0:8], 0.0, None, ALU.max))
                    seq(v.tensor_tensor(t_s[:, :, 0:8], t_s[:, :, 0:8], l_s[:, :, 0:8], ALU.add))
                    seq(v.tensor_scalar(nega[:, :], nega[:, :], -1.0, None, ALU.mult))
                    seq(v.tensor_tensor(la[:, :, 0:8], t_s[:, :, 0:8], bc(nega[:, :], 1, NT), ALU.mult))
                    seq(v.tensor_scalar(t_s[:, :, 16:32], u_s[:, :, 16:32], 0.0, None, ALU.min))
                    v.tensor_tensor(la[:, :, 8:24], t_s[:, :, 16:32], l_s[:, :, 16:32], ALU.subtract).then_inc(logs_ready, 1)
                    seq(v.tensor_scalar(beta, beta, 1.0, None, ALU.add))
                    seq(v.reciprocal(beta, beta))
                if c2 == 2:
                    wait_filled(dve, "cum")
                    close(v.tensor_copy(cs, ps("cum")[:, 0:96]), "cum")
                    wait_drained(dve, "cum")
                    run = cs[:, 0:48].rearrange("p (n c) -> p n c", n=NT)
                    tot = cs[:, 48:96].rearrange("p (n c) -> p n c", n=NT)
                    seq(v.tensor_tensor(gtail.rearrange("p (n c) -> p n c", n=NT), tot[:, :, 0:8], run[:, :, 0:8], ALU.subtract))
                    seq(v.tensor_scalar(cf[:, 0, :], run[:, 0, 8:24], -1.0, None, ALU.mult))
                    seq(v.tensor_tensor(cf[:, 1, :], run[:, 1, 8:24], tot[:, 0, 8:24], ALU.add))
                    seq(v.tensor_scalar(cf[:, 1, :], cf[:, 1, :], -1.0, None, ALU.mult))
                    seq(v.tensor_copy(gb[:, 16:32].rearrange("p (n c) -> p n c", n=NT), beta))
                    v.tensor_copy(gb[:, 0:16].rearrange("p (n c) -> p n c", n=NT), run[:, :, 0:8]).then_inc(gstat, 1)
                if c2 == 3:
                    wait_filled(dve, "gbT")
                    close(v.tensor_copy(gbT[0:16, :], ps("gbT")[0:16, 0:256]), "gbT")
            for j in range(4):
                for n in range(NT):
                    nm = f"tq.{n}.{j}"
                    wait_drained(dve, nm)
                    src = qk[:, n, WT * j:WT * j + WT]
                    seq(v.tensor_tensor(sq[:, 0:WT], src, src, ALU.mult))
                    v.tensor_reduce(qk_ss[:, n, 4 * j:4 * j + 4], sq[:, 0:WT].rearrange("p (a b) -> p a b", a=4), AX.X, ALU.add).then_inc(qkss, 1)
                    dve.wait_ge(qkss, NT * j + n + 1)
            for j in range(2):
                for n in range(NT):
                    nm = f"tq.{n}.{4 + j}"
                    wait_filled(dve, nm)
                    close(v.tensor_tensor(vbeta[:, GH * n + 4 * j:GH * n + 4 * j + 4, :], blocks4(nm), bc(beta[:, n, 4 * j:4 * j + 4], 2, P), ALU.mult), nm)
            for j in range(4):
                for n in range(NT):
                    dve.wait_ge(qkrinv, NT * j + n + 1)
                    src = qk[:, n, WT * j:WT * j + WT].rearrange("p (a b) -> p a b", a=4)
                    v.tensor_tensor(src, src, bc(qk_ri[:, n, 4 * j:4 * j + 4], 2, P), ALU.mult).then_inc(qk_normed, 1)
            dve.wait_ge(qk_normed, 8)
            dve.wait_ge(consts, 6)
            for j in range(4):
                nm = f"gb.{j}"
                wait_filled(dve, nm)
                d4 = dT[:, 4 * j:4 * j + 4, :]
                close(v.tensor_tensor(d4, blocks4(nm), bc(gb[:, 4 * j:4 * j + 4], 2, P), ALU.subtract), nm)
                wait_drained(dve, nm)
                v.tensor_scalar(d4, d4, 0.0, None, ALU.min).then_inc(d_ready, 1)
            for j in range(4):
                dve.wait_ge(dexp_ready, j + 1)
                d4 = dT[:, 4 * j:4 * j + 4, :]
                v.tensor_tensor(d4, d4, bc(tri[:, :], 1, 4), ALU.mult).then_inc(d_masked, 1)
            for j in range(4):
                dve.wait_ge(d_masked, j + 1)
                nm = f"bb.{j}"
                l4, d4 = lT[:, 4 * j:4 * j + 4, :], dT[:, 4 * j:4 * j + 4, :]
                seq(v.tensor_tensor(l4, d4, bc(stri[:, :], 1, 4), ALU.mult))
                wait_filled(dve, nm)
                close(v.tensor_tensor(l4, l4, blocks4(nm), ALU.mult), nm)
            wait_filled(dve, "cT")
            dve.wait_ge(bd_made, 1)
            close(v.tensor_copy(cT[0:16, :], ps("cT")[0:16, 0:256]), "cT")
            for j in range(4):
                l4, d4 = lT[:, 4 * j:4 * j + 4, :], dT[:, 4 * j:4 * j + 4, :]
                wait_drained(dve, f"bb.{j}")
                wait_filled(dve, f"kk.{j}")
                close(v.tensor_tensor(l4, l4, blocks4(f"kk.{j}"), ALU.mult), f"kk.{j}")
                wait_filled(dve, f"qk.{j}")
                close(v.tensor_tensor(d4, d4, blocks4(f"qk.{j}"), ALU.mult), f"qk.{j}")

            dve.wait_ge(masks_made, LEVELS)

            def coupling(lv):
                for j in range(4):
                    if lv == 0:
                        wait_drained(dve, f"kk.{j}")
                    else:
                        wait_filled(dve, f"P.{lv - 1}.{j}")
                    v.tensor_tensor(mT[:, 4 * j:4 * j + 4, :], lT[:, 4 * j:4 * j + 4, :], bc(lmask[:, lv, :], 1, 4), ALU.mult).then_inc(m_ready, 1)

            coupling(0)
            for j in range(4):
                dve.wait_ge(m_ready, j + 1)
                wait_filled(dve, f"gb.{j}")
                wait_filled(dve, f"bb.3")
                seq(v.tensor_tensor(vi[:, 4 * j:4 * j + 4, :], bc(ident[:, :], 1, 4), mT[:, 4 * j:4 * j + 4, :], ALU.subtract))
                nm = f"P.0.{j}"
                wait_filled(dve, nm)
                close(v.tensor_tensor(xi[:, 4 * j:4 * j + 4, :], bc(ident[:, :], 1, 4), blocks4(nm), ALU.subtract), nm)
            coupling(1)
            for lv in range(1, LEVELS):
                if lv < LEVELS - 1:
                    coupling(lv + 1)
                for j in range(4):
                    nm, t4 = (f"X.{lv}.{j}", xi[:, 4 * j:4 * j + 4, :]) if lv < LEVELS - 1 else (f"V.{lv}.{j}", vi[:, 4 * j:4 * j + 4, :])
                    wait_filled(dve, nm)
                    if lv == LEVELS - 1:
                        wait_drained(dve, f"V.{lv - 1}.{j}")
                    else:
                        wait_drained(dve, f"X.{lv - 1}.{j}" if lv > 1 else f"P.0.{j}")
                    close(v.tensor_tensor(t4, t4, blocks4(nm), ALU.subtract), nm)
            for j in range(4):
                wait_filled(dve, f"V.{LEVELS - 2}.{j}")
            for n in range(NT):
                for part in range(2):
                    for j in range(2):
                        wait_drained(dve, f"fox.{2 * part + j}.{n}")
                    src = fox[:, n, D * part:D * part + D]
                    seq(v.tensor_tensor(at(TX, 1024), src, src, ALU.mult))
                    ins = v.tensor_reduce(f_ss[:, n, 16 * part:16 * part + 16], at(TX, 1024).rearrange("p (a b) -> p a b", a=16), AX.X, ALU.add)
                    if part:
                        ins.then_inc(fss, 1)
                        dve.wait_ge(fss, n + 1)
                    else:
                        seq(ins)
            dve.wait_ge(geg, 2)
            seq(v.tensor_tensor(be_s, eg_s, gb[:, 16:32], ALU.mult))
            q1 = qk[:, 1, 0:D].rearrange("p (h d) -> p h d", h=GH)
            k0 = qk[:, 0, D:2 * D].rearrange("p (h d) -> p h d", h=GH)
            k1 = qk[:, 1, D:2 * D].rearrange("p (h d) -> p h d", h=GH)
            for n in range(NT):
                for j in range(4):
                    wait_drained(dve, f"tk.{n}.{j}")
            v.tensor_tensor(q1, q1, bc(eg_s[:, 8:16], 2, P), ALU.mult).then_inc(scaled, 1)
            wait_filled(dve, f"P.{LEVELS - 1}.3")
            v.tensor_tensor(kbe, k1, bc(be_s[:, 8:16], 2, P), ALU.mult).then_inc(scaled, 1)
            v.tensor_tensor(k0, k0, bc(et_s[:, 0:8], 2, P), ALU.mult).then_inc(scaled, 1)

            def key_decays(*js):
                for j in js:
                    nm = f"cb.{j}"
                    wait_filled(dve, nm)
                    if j == 5:
                        for n in range(NT):
                            for half in range(2):
                                wait_filled(dve, f"oT.{n}.{half}")
                    src = ps(nm)[:, :].rearrange("p (f k) -> p f k", f=2)
                    dst = cbm[:, 2 * j:2 * j + 2, :]
                    step(v.tensor_tensor(dst[:, :, 0:P], src[:, :, 0:P], bc(negm[:, :], 1, 2), ALU.add))
                    step(v.tensor_copy(dst[:, :, P:2 * P], src[:, :, 0:P]))
                    close(v.tensor_tensor(dst[:, :, 2 * P:3 * P], src[:, :, P:S], bc(negm[:, :], 1, 2), ALU.add), nm)

            for nm in ("o0.0", "o0.1", "o1.0", "o1.1"):
                wait_drained(dve, nm)
            o16 = oa.rearrange("p n (h v) -> p (n h) v", h=GH)
            for n in range(NT):
                seq(v.tensor_tensor(at(TPB, 1024), oa[:, n, :], oa[:, n, :], ALU.mult))
                ins = v.tensor_reduce(o_ss[:, 8 * n:8 * n + 8], at(TPB, 1024).rearrange("p (a b) -> p a b", a=8), AX.X, ALU.add)
                if n:
                    ins.then_inc(oss, 1)
                else:
                    seq(ins)
            for n in range(NT):
                dve.wait_ge(frinv, n + 1)
                src = fox[:, n, 0:2 * D].rearrange("p (a b) -> p a b", a=32)
                v.tensor_tensor(src, src, bc(f_ri[:, n, :], 2, FD), ALU.mult).then_inc(f_normed, 1)
            key_decays(0)
            dve.wait_ge(orinv, 1)
            for j in range(2):
                for n in range(NT):
                    wait_drained(dve, f"z.{j}.{n}")
            for n in range(NT):
                o8 = o16[:, 8 * n:8 * n + 8, :]
                seq(v.tensor_tensor(o8, o8, bc(o_ri[:, 8 * n:8 * n + 8], 2, P), ALU.mult))
                v.tensor_tensor(oa[:, n, :], oa[:, n, :], zs[:, n, :], ALU.mult).then_inc(o_normed, 1)
            key_decays(1, 2, 3, 4)
            key_decays(5, 6, 7)
            for jm in range(2):
                for n in range(NT):
                    wait_drained(dve, f"merge.{jm}.{n}")

            def gated(j, n):
                nm = f"ya.{j}.{n}"
                wait_filled(dve, nm)
                close(v.tensor_tensor(mix[:, n, WT * j:WT * j + WT], ps(nm)[:, :], merge[:, n, WT * j:WT * j + WT], ALU.mult), nm)

            dve.wait_ge(dve_step, steps[0])
            for g in range(8):
                wait_drained(dve, f"cb.{g}")

            def maxima(g):
                for f in (2 * g, 2 * g + 1):
                    nm = f"s.{f}"
                    wait_filled(dve, nm)
                    if g > 1:
                        wait_filled(dve, f"pT.{f - 4}")
                    close(v.tensor_tensor(scores[f % 4], ps(nm)[:, 0:384], cbm[:, f, :], ALU.add), nm)
                for f in (2 * g, 2 * g + 1):
                    sc = scores[f % 4]
                    wait_drained(dve, f"s.{f}")
                    v.tensor_reduce(mx[:, 2 * f:2 * f + 1], sc[:, 0:P], AX.X, ALU.max, negate=True).then_inc(smax, 1)
                    v.tensor_reduce(mx[:, 2 * f + 1:2 * f + 2], sc[:, P:3 * P], AX.X, ALU.max, negate=True).then_inc(smax, 1)

            maxima(0)
            for g in range(8):
                if g < 7:
                    maxima(g + 1)
                f = 2 * g
                dve.wait_ge(sexp, 2 * f + 4)
                seq(v.reciprocal(dri[:, 2 * f:2 * f + 4], den[:, 2 * f:2 * f + 4]))
                for f in (2 * g, 2 * g + 1):
                    sc = scores[f % 4]
                    step(v.tensor_scalar(sc[:, 0:P], sc[:, 0:P], dri[:, 2 * f:2 * f + 1], None, ALU.mult))
                    v.tensor_scalar(sc[:, P:3 * P], sc[:, P:3 * P], dri[:, 2 * f + 1:2 * f + 2], None, ALU.mult).then_inc(sdiv, 1)
                if 3 <= g < 7:
                    gated((g - 3) // NT, (g - 3) % NT)
            for jm in (2, 3):
                for n in range(NT):
                    wait_drained(dve, f"merge.{jm}.{n}")
            for j in range(2):
                for n in range(NT):
                    nm = f"yf.{j}.{n}"
                    wait_filled(dve, nm)
                    close(v.tensor_tensor(mixf[:, n, WT * j:WT * j + WT], ps(nm)[:, :], merge[:, n, D + WT * j:D + WT * j + WT], ALU.mult), nm)
                    wait_drained(dve, nm)
                    wait_drained(dve, f"ya.{j}.{n}")
                    m = mix[:, n, WT * j:WT * j + WT]
                    v.tensor_tensor(m, m, mixf[:, n, WT * j:WT * j + WT], ALU.add).then_inc(mixed, 1)
            for j in range(2):
                for n in range(NT):
                    nm = f"wo.{j}.{n}"
                    wait_filled(dve, nm)
                    hv = h[:, n, WT * j:WT * j + WT]
                    close(v.tensor_tensor(hv, hv, ps(nm)[:, :], ALU.add), nm)
                    wait_drained(dve, nm)
                    v.memset(stat[:, 990 + 2 * j + n:991 + 2 * j + n], 0.0).then_inc(h_ready, 1)

            dve.wait_ge(ngain_loaded, 16)
            for n in range(NT):
                dve.wait_ge(rinv_made, NT + n + 1)
                v.scalar_tensor_tensor(out=hn[:, n, :].rearrange("p (c q) -> p c q", c=KC), in0=h[:, n, :].rearrange("p (q c) -> p c q", c=KC),
                                       scalar=rinv_x[1][:, n:n + 1], in1=ngain.rearrange("p (q c) -> p c q", c=KC),
                                       op0=ALU.mult, op1=ALU.mult).then_inc(xn_ready, 1)
            wait_drained(dve, "router")
            for n in range(NT):
                seq(v.tensor_tensor(sel[:, n, :], sg[:, n, :], rbias[:, :], ALU.add))
                seq(v.max(top[:, n, :], sel[:, n, :]))
                seq(v.match_replace(out=gates[:, n, :], in_to_replace=top[:, n, :], in_values=sel[:, n, :], imm_value=-1e30))
                ins = v.tensor_tensor(chosen[:, n, :], gates[:, n, :], sel[:, n, :], ALU.not_equal)
                if n == 1:
                    ins.then_inc(onehot_ready, 1)
                else:
                    seq(ins)
            dve.wait_ge(onehot_ready, 1)
            for n in range(NT):
                seq(v.tensor_tensor(gates[:, n, :], chosen[:, n, :], sg[:, n, :], ALU.mult))
                seq(v.tensor_reduce(gsum[:, n, 0:1], gates[:, n, :], AX.X, ALU.add))
                seq(v.reciprocal(gsum[:, n, 1:2], gsum[:, n, 0:1]))
                seq(v.tensor_scalar(gates[:, n, :], gates[:, n, :], gsum[:, n, 1:2], ROUTED_SCALE, ALU.mult, ALU.mult))
            for n in range(NT):
                dve.wait_ge(parts_ready, n + 1)
                for j in range(2):
                    wait_filled(dve, f"hT.{n}.{j}")
                seq(v.tensor_tensor(hn[:, n, :], hn[:, n, :], hparts[:, 0, n, :], ALU.subtract))
            for n in range(NT):
                seq(v.tensor_copy(hparts[:, 1, n, :], hn[:, n, :]))
                v.tensor_tensor(hparts[:, 2, n, :], hn[:, n, :], hparts[:, 1, n, :], ALU.subtract).then_inc(parts_ready, 1)
            for n in range(NT):
                dve.wait_ge(gu_silu, n + 1)
                up = ps(f"sh.{n}")[:, DE:2 * DE].rearrange("p (q c) -> p c q", c=2)
                close(v.tensor_tensor(shid[n].rearrange("p (c q) -> p c q", c=2), ssil[n].rearrange("p (q c) -> p c q", c=2), up, ALU.mult), f"sh.{n}")
            wait_filled(dve, "rank")
            px = posx[:, :, 0:NE]
            seq(v.tensor_scalar(px, ps("rank")[:, 0:2 * NE].rearrange("p (n c) -> p n c", n=NT), 1.0, None, ALU.add))
            seq(v.tensor_tensor(px, px, chosen[:, :, :], ALU.mult))
            seq(v.tensor_scalar(px, px, -1.0, None, ALU.add))
            seq(v.tensor_scalar(posx[:, :, NE:NX], posx[:, :, 0:LOOKAHEAD], -float(CAP), None, ALU.add))
            close(v.tensor_reduce(gsum[:, 0, 0:1], ps("rank")[:, 2 * NE:3 * NE], AX.X, ALU.max), "rank")
            wait_drained(dve, "rank")
            m, q = gsum[:, 0, 0:1], gsum[:, 0, 1:2]
            seq(v.tensor_scalar(q, m, float(CAP), 1.0, ALU.is_gt, ALU.add))
            for k in range(2, S // CAP):
                seq(v.scalar_tensor_tensor(out=q, in0=m, scalar=float(CAP * k), in1=q, op0=ALU.is_gt, op1=ALU.add))
            seq(v.tensor_copy(passes[:, 0:1], q))
            v.tensor_scalar(passes[:, 1:2], q, float(PAIRS // 2), None, ALU.mult).then_inc(passes_ready, 1)
            r1 = sel[:, :, :]
            gp = lambda k: gparts[:, :, 0:NE, k]
            seq(v.tensor_copy(gp(0), gates[:, :, :]))
            seq(v.tensor_tensor(r1, gates[:, :, :], gp(0), ALU.subtract))
            seq(v.tensor_copy(gp(1), r1))
            seq(v.tensor_tensor(gp(2), r1, gp(1), ALU.subtract))
            v.tensor_copy(gparts[:, :, NE:NX, :], gparts[:, :, 0:LOOKAHEAD, :]).then_inc(gparts_ready, 1)
            dve.wait_ge(passes_ready, 1)

            def place_tokens(e2):
                for n in range(NT):
                    dst = onehot[:, n, :].rearrange("p (e s) -> p e s", e=2)
                    ins = v.tensor_tensor(dst, bc(iota[:, :], 1, 2), bc(posx[:, n, e2], 2, CAP), ALU.is_equal)
                    if n == 0:
                        seq(ins)
                ins.then_inc(onehot_ready, 1)

            place_tokens(slice(0, 2))
            wait_drained(dve, "e.1.1")
            for j in range(2):
                v.memset(y[:, WT * j:WT * j + WT], 0.0).then_inc(y_ready[j], 1)
            seq(v.memset(spread[1], 0.0))

            def gathered(t, s):
                dve.wait_ge(xb_filled, t)
                v.tensor_copy(xg[:, 4:8, :], bank[6][:, :].rearrange("p (c s) -> p c s", c=4)).then_inc(xb_ready, 1)
                dve.wait_ge(place_filled, t)
                seq(v.tensor_copy(spread[s], bank[7][:, DE:DE + P].bitcast(BF16).rearrange("p (n t) -> p n t", n=NT)))
                for e in range(2):
                    lo = e * CAP
                    ins = v.tensor_reduce(gslot[lo:lo + CAP, :], bank[7][lo:lo + CAP, 400 + 3 * e:403 + 3 * e], AX.X, ALU.add)
                    if e == 0:
                        seq(ins)
                ins.then_inc(place_ready, 1)

            gathered(1, 0)
            place_tokens(slice(2, 4))
            dve.wait_ge(plen_loaded, 16)
            for n in range(NT):
                dve.wait_ge(erinv, n + 1)
                seq(v.tensor_scalar(e_t[:, n, :], e_t[:, n, :], e_ri[:, n:n + 1], None, ALU.mult))
                v.tensor_tensor(e_t[:, n, :], e_t[:, n, :], plen, ALU.mult).then_inc(e_ready, 1)
            np_dve = dve.value_load(passes[0:1, 0:1], min_val=1, max_val=S // CAP)
            with dve.Fori(0, np_dve) as r:
                with dve.Fori(0, PAIRS // 2) as k:
                    for s in range(2):
                        before = r * PAIRS + k * 2 + s
                        dve.wait_ge(psilu, before + 1)
                        dve.wait_ge(place_ready, before + 1)
                        up = bank[4][:, DE:2 * DE].rearrange("p (q c) -> p c q", c=2)
                        v.scalar_tensor_tensor(out=hid.rearrange("p (c q) -> p c q", c=2), in0=sil.rearrange("p (q c) -> p c q", c=2),
                                               scalar=gslot[:, 0:1], in1=up, op0=ALU.mult, op1=ALU.mult).then_inc(phid_ready, 1)
                        dve.wait_ge(xb_filled, before + 2)
                        v.tensor_copy(xg[:, 4:8, :], bank[6][:, :].rearrange("p (c s) -> p c s", c=4)).then_inc(xb_ready, 1)
                        dve.wait_ge(place_filled, before + 2)
                        dve.wait_ge(phid_ready, before + 1)
                        v.tensor_copy(spread[1 - s], bank[7][:, DE:DE + P].bitcast(BF16).rearrange("p (n t) -> p n t", n=NT)).then_inc(spread_made, 1)
                        for e in range(2):
                            lo = e * CAP
                            v.tensor_reduce(gslot[lo:lo + CAP, :], bank[7][lo:lo + CAP, 400 + 3 * e:403 + 3 * e], AX.X, ALU.add).then_inc(place_half if e == 0 else place_ready, 1)
                        ahead = bass.ds(k * 4 + (2 * s + 4), 2)
                        for n in range(NT):
                            dst = onehot[:, n, :].rearrange("p (e s) -> p e s", e=2)
                            v.tensor_tensor(dst, bc(iota[:, :], 1, 2), bc(posx[:, n, ahead], 2, CAP), ALU.is_equal).then_inc(onehot_half if n == 0 else onehot_ready, 1)
                        dve.wait_ge(y_filled[1], before + 1)
                        v.tensor_copy(y[:, WT:D], bank[5][:, :]).then_inc(y_ready[1], 1)
                dve.wait_ge(onehot_ready, r * PAIRS + (PAIRS + 3))
                v.tensor_scalar(iota[:, :], iota[:, :], float(CAP), None, ALU.add).then_inc(iota_moved, 1)
                dve.wait_ge(iota_moved, r + 1)
            for n in range(NT):
                for j in range(2):
                    dve.wait_ge(added, np_dve * PAIRS + (2 * n + j + 1))
                    hv = h[:, n, WT * j:WT * j + WT]
                    v.tensor_tensor(hv, hv, bank[2 * n + j][:, :], ALU.add).then_inc(h_ready, 1)
            for n in range(NT):
                for j in range(2):
                    dve.wait_ge(hidT_filled, NT + 2 * n + j + 1)
                    src = bank[2 * n + j][:, :].rearrange("p (a b) -> p a b", a=4)
                    v.tensor_tensor(actT[:, 4 * j:4 * j + 4, n * P:n * P + P], src, bc(cols[:, R_NPG + 4 * j:R_NPG + 4 * j + 4], 2, P), ALU.mult).then_inc(e_ready, 1)
            for n in range(NT):
                for j in range(2):
                    dve.wait_ge(sg_ready, NT * n + j + 1)
                    o = gt[:, n, WT * j:WT * j + WT]
                    seq(v.tensor_tensor(o, o, e_t[:, n, WT * j:WT * j + WT], ALU.mult))
                    v.tensor_tensor(o, o, h[:, n, WT * j:WT * j + WT], ALU.add).then_inc(out_ready, 1)


_INS = ['x', 'p', 'norm_mix', 'w_in', 'conv_w', 'a_log', 'dt_bias', 'gdn_norm', 'fox_f_bias', 'q_norm', 'k_norm',
        'w_branch_gdn', 'w_branch_fox', 'w_out', 'norm_ffn', 'w_router', 'router_bias', 'we_gate', 'we_up', 'we_down',
        'ws_gate', 'ws_up', 'ws_down', 'w_ple', 'ple_norm', 'ple_gate_norm', 'w_ple_gate']


def kernel(**inputs):
    import numpy as np
    import concourse.bacc as bacc
    from concourse.bass_utils import run_bass_kernel_spmd

    nc = bacc.Bacc("TRN2", target_bir_lowering=False, num_devices=1)
    arrays, args = {}, []
    for name in _INS:
        a = np.ascontiguousarray(inputs[name])
        arrays[f"in_{name}"] = a
        args.append(nc.dram_tensor(f"in_{name}", a.shape, mybir.dt.from_np(a.dtype), kind="ExternalInput").ap())
    res = nc.dram_tensor("out_0", (1, S, D), F32, kind="ExternalOutput").ap()
    program(nc, *args, res)
    r = run_bass_kernel_spmd(nc, [arrays], core_ids=[0])
    return r.results[0]["out_0"]
```
